# Optimizing a Trainium2 kernel written in Bass

```python
import math
import numpy as np
import jax
import jax.numpy as jnp
from jax import lax
import jax, jax.numpy as jnp

D_MODEL = 1024
BATCH = 1
SEQ = 512
DEPTH = 1

HEAD_DIM = 64
ROPE_DIM = HEAD_DIM // 4
ROPE_THETA = 500000.0
DIFF_HEADS = 4
DIFF_V_DIM = 2 * HEAD_DIM
NSA_HEADS = 8
NSA_KV_HEADS = 2
NSA_GROUP = NSA_HEADS // NSA_KV_HEADS
N_BRANCH = 3
CMP_BLOCK = 32
CMP_STRIDE = 16
CMP_HIDDEN = 4 * HEAD_DIM
SEL_BLOCK = 64
SEL_TOP_N = 16
WINDOW = 512
D_FF = 2816
Q_BLOCK = 128
SEL_Q_CHUNK = 64
MIX_WIDTH = DIFF_HEADS * DIFF_V_DIM + NSA_HEADS * HEAD_DIM
IN_SIZES = (DIFF_HEADS * 2 * HEAD_DIM, DIFF_HEADS * 2 * HEAD_DIM, DIFF_HEADS * DIFF_V_DIM,
            NSA_HEADS * HEAD_DIM) + (NSA_KV_HEADS * HEAD_DIM,) * 6 + (NSA_HEADS * N_BRANCH,)
IN_WIDTH = sum(IN_SIZES)
EPS = 1e-6
NEG_INF = -1e30
FORCE_SCORE = 1e9


def rms_norm(x, g):
    xf = x.astype(jnp.float32)
    y = xf * lax.rsqrt(jnp.mean(xf * xf, axis=-1, keepdims=True) + EPS)
    return (y * g.astype(jnp.float32)).astype(x.dtype)

def rope_tables(S):
    pos = jnp.arange(S, dtype=jnp.float32)
    inv = ROPE_THETA ** (-jnp.arange(0, ROPE_DIM, 2, dtype=jnp.float32) / ROPE_DIM)
    ang = pos[:, None] * inv[None, :]
    return jnp.cos(ang), jnp.sin(ang)

def partial_rope(x, cos, sin):
    xr = x[..., :ROPE_DIM].astype(jnp.float32)
    x1, x2 = xr[..., :ROPE_DIM // 2], xr[..., ROPE_DIM // 2:]
    rot = jnp.concatenate([x1 * cos - x2 * sin, x2 * cos + x1 * sin], axis=-1)
    return jnp.concatenate([rot.astype(x.dtype), x[..., ROPE_DIM:]], axis=-1)

def swiglu(h, w_gate, w_up, w_down):
    return (jax.nn.silu(h @ w_gate) * (h @ w_up)) @ w_down

def diff_attention(q, k, v, lam, subln_g, lambda_init):
    B, Hd, _, S, dh = q.shape
    nb = S // Q_BLOCK
    scale = dh ** -0.5
    qb = q.reshape(B, Hd, 2, nb, Q_BLOCK, dh).transpose(3, 0, 1, 2, 4, 5)
    kpos = jnp.arange(S)

    def block(args):
        qi, i = args
        s = jnp.einsum('bhmqd,bhmkd->bhmqk', qi, k).astype(jnp.float32) * scale
        qpos = i * Q_BLOCK + jnp.arange(Q_BLOCK)
        s = jnp.where(kpos[None, :] <= qpos[:, None], s, NEG_INF)
        p = jax.nn.softmax(s, axis=-1)
        a = p[:, :, 0] - lam * p[:, :, 1]
        return jnp.einsum('bhqk,bhkd->bhqd', a.astype(v.dtype), v)

    o = lax.map(block, (qb, jnp.arange(nb)))
    o = o.transpose(1, 2, 0, 3, 4).reshape(B, Hd, S, 2 * dh)
    o = rms_norm(o, subln_g) * (1.0 - lambda_init)
    return o.transpose(0, 2, 1, 3).reshape(B, S, Hd * 2 * dh)

def compress(x, pe, w1, w2):
    B, G, S, dh = x.shape
    r = CMP_BLOCK // CMP_STRIDE
    nc = S // CMP_STRIDE - r + 1
    sub = x.reshape(B, G, S // CMP_STRIDE, CMP_STRIDE, dh)
    blocks = jnp.concatenate([sub[:, :, j:j + nc] for j in range(r)], axis=3)
    blocks = (blocks + pe).reshape(B, G, nc, CMP_BLOCK * dh)
    return jax.nn.gelu(blocks @ w1) @ w2

def sel_overlap(nc, n_sel):
    cs = np.arange(nc)[:, None] * CMP_STRIDE
    ss = np.arange(n_sel)[None, :] * SEL_BLOCK
    ov = np.minimum(cs + CMP_BLOCK, ss + SEL_BLOCK) - np.maximum(cs, ss)
    return jnp.asarray(np.clip(ov, 0, None) / CMP_BLOCK, dtype=jnp.float32)

def nsa_attention(q, k_cmp, v_cmp, k_sel, v_sel, k_win, v_win, gates,
                  pe_k, wk1, wk2, pe_v, wv1, wv2):
    B, H, S, dh = q.shape
    G, Hg = NSA_KV_HEADS, NSA_GROUP
    scale = dh ** -0.5
    qg = q.reshape(B, G, Hg, S, dh)
    t = jnp.arange(S)

    kc = compress(k_cmp, pe_k, wk1, wk2)
    vc = compress(v_cmp, pe_v, wv1, wv2)
    nc = kc.shape[2]
    cend = jnp.arange(nc) * CMP_STRIDE + CMP_BLOCK - 1
    cvalid = cend[None, :] <= t[:, None]
    s = jnp.einsum('bghsd,bgcd->bghsc', qg, kc).astype(jnp.float32) * scale
    p_cmp = jnp.where(cvalid, jax.nn.softmax(jnp.where(cvalid, s, NEG_INF), axis=-1), 0.0)
    o_cmp = jnp.einsum('bghsc,bgcd->bghsd', p_cmp.astype(vc.dtype), vc)

    n_sel = S // SEL_BLOCK
    top_n = min(SEL_TOP_N, n_sel)
    imp = jnp.einsum('bghsc,cj->bgsj', p_cmp, sel_overlap(nc, n_sel))
    blk = jnp.arange(n_sel)[None, :]
    cur = (t // SEL_BLOCK)[:, None]
    causal_blk = blk * SEL_BLOCK <= t[:, None]
    forced = (blk == 0) | ((blk <= cur) & (blk >= cur - 1))
    imp = jnp.where(forced, FORCE_SCORE, jnp.where(causal_blk, imp, -1.0))
    _, idx = lax.top_k(imp, top_n)

    kb = k_sel.reshape(B, G, n_sel, SEL_BLOCK, dh)
    vb = v_sel.reshape(B, G, n_sel, SEL_BLOCK, dh)
    C = SEL_Q_CHUNK
    nq = S // C
    q_c = qg.reshape(B, G, Hg, nq, C, dh).transpose(3, 0, 1, 2, 4, 5)
    idx_c = idx.reshape(B, G, nq, C, top_n).transpose(2, 0, 1, 3, 4)
    bi = jnp.arange(B)[:, None, None, None]
    gi = jnp.arange(G)[None, :, None, None]

    def sel_chunk(args):
        qi, ii, c = args
        ks = kb[bi, gi, ii]
        vs = vb[bi, gi, ii]
        s = jnp.einsum('bghqd,bgqnld->bghqnl', qi, ks).astype(jnp.float32) * scale
        kpos = ii[..., None] * SEL_BLOCK + jnp.arange(SEL_BLOCK)
        qpos = c * C + jnp.arange(C)
        mask = kpos <= qpos[None, None, :, None, None]
        s = jnp.where(mask[:, :, None], s, NEG_INF).reshape(B, G, Hg, C, top_n * SEL_BLOCK)
        p = jax.nn.softmax(s, axis=-1).reshape(B, G, Hg, C, top_n, SEL_BLOCK)
        return jnp.einsum('bghqnl,bgqnld->bghqd', p.astype(vs.dtype), vs)

    o_sel = lax.map(sel_chunk, (q_c, idx_c, jnp.arange(nq)))
    o_sel = o_sel.transpose(1, 2, 3, 0, 4, 5).reshape(B, G, Hg, S, dh)

    nb = S // Q_BLOCK
    span = WINDOW + Q_BLOCK
    kp = jnp.pad(k_win, ((0, 0), (0, 0), (WINDOW, 0), (0, 0)))
    vp = jnp.pad(v_win, ((0, 0), (0, 0), (WINDOW, 0), (0, 0)))
    q_w = qg.reshape(B, G, Hg, nb, Q_BLOCK, dh).transpose(3, 0, 1, 2, 4, 5)

    def win_block(args):
        qi, i = args
        start = i * Q_BLOCK
        ks = lax.dynamic_slice_in_dim(kp, start, span, axis=2)
        vs = lax.dynamic_slice_in_dim(vp, start, span, axis=2)
        s = jnp.einsum('bghqd,bgkd->bghqk', qi, ks).astype(jnp.float32) * scale
        qpos = start + jnp.arange(Q_BLOCK)
        kpos = start - WINDOW + jnp.arange(span)
        d = qpos[:, None] - kpos[None, :]
        mask = (d >= 0) & (d < WINDOW) & (kpos[None, :] >= 0)
        p = jax.nn.softmax(jnp.where(mask, s, NEG_INF), axis=-1)
        return jnp.einsum('bghqk,bgkd->bghqd', p.astype(vs.dtype), vs)

    o_win = lax.map(win_block, (q_w, jnp.arange(nb)))
    o_win = o_win.transpose(1, 2, 3, 0, 4, 5).reshape(B, G, Hg, S, dh)

    o = gates[..., 0:1] * o_cmp + gates[..., 1:2] * o_sel + gates[..., 2:3] * o_win
    return o.transpose(0, 3, 1, 2, 4).reshape(B, S, H * dh)

def hybrid_mixer(h, w_in, lambda_q1, lambda_k1, lambda_q2, lambda_k2, diff_subln,
                 cmp_pe_k, cmp_k_w1, cmp_k_w2, cmp_pe_v, cmp_v_w1, cmp_v_w2, w_out, lambda_init):
    B, S, _ = h.shape
    dh = HEAD_DIM
    cos, sin = rope_tables(S)
    pts = [int(v) for v in np.cumsum(IN_SIZES)[:-1]]
    dq, dk, dv, nq, kc, vc, ks, vs, kw, vw, gl = jnp.split(h @ w_in, pts, axis=-1)

    dq = partial_rope(dq.reshape(B, S, DIFF_HEADS, 2, dh).transpose(0, 2, 3, 1, 4), cos, sin)
    dk = partial_rope(dk.reshape(B, S, DIFF_HEADS, 2, dh).transpose(0, 2, 3, 1, 4), cos, sin)
    dv = dv.reshape(B, S, DIFF_HEADS, DIFF_V_DIM).transpose(0, 2, 1, 3)
    lq1, lk1 = lambda_q1.astype(jnp.float32), lambda_k1.astype(jnp.float32)
    lq2, lk2 = lambda_q2.astype(jnp.float32), lambda_k2.astype(jnp.float32)
    lam = jnp.exp(jnp.sum(lq1 * lk1)) - jnp.exp(jnp.sum(lq2 * lk2)) + lambda_init
    o_diff = diff_attention(dq, dk, dv, lam, diff_subln, lambda_init)

    def kv_heads(a):
        return a.reshape(B, S, NSA_KV_HEADS, dh).transpose(0, 2, 1, 3)
    nq = partial_rope(nq.reshape(B, S, NSA_HEADS, dh).transpose(0, 2, 1, 3), cos, sin)
    gates = jax.nn.sigmoid(gl.reshape(B, S, NSA_HEADS, N_BRANCH)).transpose(0, 2, 1, 3)
    gates = gates.reshape(B, NSA_KV_HEADS, NSA_GROUP, S, N_BRANCH)
    o_nsa = nsa_attention(nq, kv_heads(kc), kv_heads(vc),
                          partial_rope(kv_heads(ks), cos, sin), kv_heads(vs),
                          partial_rope(kv_heads(kw), cos, sin), kv_heads(vw), gates,
                          cmp_pe_k, cmp_k_w1, cmp_k_w2, cmp_pe_v, cmp_v_w1, cmp_v_w2)

    return jnp.concatenate([o_diff, o_nsa], axis=-1) @ w_out

def first_inputs(seed: int = 0) -> dict:
    key = jax.random.key(seed)
    ks = jax.random.split(key, 26)
    f32 = jnp.float32
    L = DEPTH

    def w(k, shape, fan_in):
        return jax.random.normal(k, shape, f32) * fan_in ** -0.5

    def gain(k, n):
        return 1.0 + 0.1 * jax.random.normal(k, (L, n), f32)

    return {
        'x': jax.random.normal(ks[0], (BATCH, SEQ, D_MODEL), f32),
        'ff1_norm_pre': gain(ks[1], D_MODEL),
        'ff1_w_gate': w(ks[2], (L, D_MODEL, D_FF), D_MODEL),
        'ff1_w_up': w(ks[3], (L, D_MODEL, D_FF), D_MODEL),
        'ff1_w_down': w(ks[4], (L, D_FF, D_MODEL), D_FF),
        'ff1_norm_post': gain(ks[5], D_MODEL),
        'mix_norm_pre': gain(ks[6], D_MODEL),
        'w_in': w(ks[7], (L, D_MODEL, IN_WIDTH), D_MODEL),
        'lambda_q1': 0.1 * jax.random.normal(ks[8], (L, HEAD_DIM), f32),
        'lambda_k1': 0.1 * jax.random.normal(ks[9], (L, HEAD_DIM), f32),
        'lambda_q2': 0.1 * jax.random.normal(ks[10], (L, HEAD_DIM), f32),
        'lambda_k2': 0.1 * jax.random.normal(ks[11], (L, HEAD_DIM), f32),
        'diff_subln': gain(ks[12], DIFF_V_DIM),
        'cmp_pe_k': 0.1 * jax.random.normal(ks[13], (L, CMP_BLOCK, HEAD_DIM), f32),
        'cmp_k_w1': w(ks[14], (L, CMP_BLOCK * HEAD_DIM, CMP_HIDDEN), CMP_BLOCK * HEAD_DIM),
        'cmp_k_w2': w(ks[15], (L, CMP_HIDDEN, HEAD_DIM), CMP_HIDDEN),
        'cmp_pe_v': 0.1 * jax.random.normal(ks[16], (L, CMP_BLOCK, HEAD_DIM), f32),
        'cmp_v_w1': w(ks[17], (L, CMP_BLOCK * HEAD_DIM, CMP_HIDDEN), CMP_BLOCK * HEAD_DIM),
        'cmp_v_w2': w(ks[18], (L, CMP_HIDDEN, HEAD_DIM), CMP_HIDDEN),
        'w_out': w(ks[19], (L, MIX_WIDTH, D_MODEL), MIX_WIDTH),
        'mix_norm_post': gain(ks[20], D_MODEL),
        'ff2_norm_pre': gain(ks[21], D_MODEL),
        'ff2_w_gate': w(ks[22], (L, D_MODEL, D_FF), D_MODEL),
        'ff2_w_up': w(ks[23], (L, D_MODEL, D_FF), D_MODEL),
        'ff2_w_down': w(ks[24], (L, D_FF, D_MODEL), D_FF),
        'ff2_norm_post': gain(ks[25], D_MODEL),
    }

def first_block(x, ff1_norm_pre, ff1_w_gate, ff1_w_up, ff1_w_down, ff1_norm_post,
              mix_norm_pre, w_in, lambda_q1, lambda_k1, lambda_q2, lambda_k2, diff_subln,
              cmp_pe_k, cmp_k_w1, cmp_k_w2, cmp_pe_v, cmp_v_w1, cmp_v_w2, w_out, mix_norm_post,
              ff2_norm_pre, ff2_w_gate, ff2_w_up, ff2_w_down, ff2_norm_post):
    for l in range(DEPTH):
        lambda_init = 0.8 - 0.6 * math.exp(-0.3 * l)
        h = swiglu(rms_norm(x, ff1_norm_pre[l]), ff1_w_gate[l], ff1_w_up[l], ff1_w_down[l])
        x = x + 0.5 * rms_norm(h, ff1_norm_post[l])
        h = hybrid_mixer(rms_norm(x, mix_norm_pre[l]), w_in[l], lambda_q1[l], lambda_k1[l],
                         lambda_q2[l], lambda_k2[l], diff_subln[l], cmp_pe_k[l], cmp_k_w1[l],
                         cmp_k_w2[l], cmp_pe_v[l], cmp_v_w1[l], cmp_v_w2[l], w_out[l], lambda_init)
        x = x + rms_norm(h, mix_norm_post[l])
        h = swiglu(rms_norm(x, ff2_norm_pre[l]), ff2_w_gate[l], ff2_w_up[l], ff2_w_down[l])
        x = x + 0.5 * rms_norm(h, ff2_norm_post[l])
    return x


DEPTH_2 = 2

N_MEM = 256
MIX_WIDTH_2 = D_MODEL
MEM_HEADS = 4
MEM_WIDTH = MEM_HEADS * HEAD_DIM
MAIN_WIDTH = MIX_WIDTH_2 - MEM_WIDTH
SB_HEADS = MAIN_WIDTH // HEAD_DIM
CONV_WIDTH = 3
D_FF_2 = -(-8 * D_MODEL // (3 * 256)) * 256
N_A_LAYERS = DEPTH_2 // 2
N_B_LAYERS = DEPTH_2 - N_A_LAYERS
BLOCK_Q = 128


def rmsnorm(x, g):
    xf = x.astype(jnp.float32)
    y = xf * lax.rsqrt(jnp.mean(xf * xf, axis=-1, keepdims=True) + EPS)
    return (y * g.astype(jnp.float32)).astype(x.dtype)

def causal_short_conv(u, w):
    c = u.shape[-1]
    return lax.conv_general_dilated(
        u, w[:, None, :].astype(u.dtype), window_strides=(1,),
        padding=[(CONV_WIDTH - 1, 0)],
        dimension_numbers=("NWC", "WIO", "NWC"),
        feature_group_count=c)

def memory_cross_attention(q, mem_k, mem_v):
    scale = 1.0 / math.sqrt(HEAD_DIM)
    s = jnp.einsum("bshd,bmhd->bhsm", q.astype(jnp.float32), mem_k.astype(jnp.float32)) * scale
    p = jax.nn.softmax(s, axis=-1)
    o = jnp.einsum("bhsm,bmhd->bshd", p, mem_v.astype(jnp.float32))
    return o.astype(q.dtype)

def stick_breaking_attention(q, k, v):
    b, s_len, h, d = q.shape
    scale = 1.0 / math.sqrt(d)
    qh = jnp.transpose(q, (0, 2, 1, 3)).astype(jnp.float32)
    kh = jnp.transpose(k, (0, 2, 1, 3)).astype(jnp.float32)
    vh = jnp.transpose(v, (0, 2, 1, 3)).astype(jnp.float32)
    outs = []
    for blk in range(s_len // BLOCK_Q):
        start = blk * BLOCK_Q
        end = start + BLOCK_Q
        qb = qh[:, :, start:end]
        kb = kh[:, :, :end]
        vb = vh[:, :, :end]
        z = jnp.einsum("bhtd,bhsd->bhts", qb, kb) * scale
        t_idx = start + jnp.arange(BLOCK_Q)[:, None]
        s_idx = jnp.arange(end)[None, :]
        causal = s_idx < t_idx
        log_not = jnp.where(causal, jax.nn.log_sigmoid(-z), 0.0)
        tail = lax.cumsum(log_not, axis=3, reverse=True) - log_not
        log_a = jax.nn.log_sigmoid(z) + tail
        a = jnp.where(causal, jnp.exp(log_a), 0.0)
        outs.append(jnp.einsum("bhts,bhsd->bhtd", a, vb))
    o = jnp.concatenate(outs, axis=2)
    return jnp.transpose(o, (0, 2, 1, 3)).astype(q.dtype)

def swiglu_2(h, w_gate, w_up, w_down):
    return (jax.nn.silu(h @ w_gate) * (h @ w_up)) @ w_down

def second_inputs(seed: int = 0) -> dict:
    key = jax.random.key(seed)
    ks = jax.random.split(key, 16)
    f32 = jnp.float32

    def nrm(k, shape, fan_in):
        return jax.random.normal(k, shape, f32) * (fan_in ** -0.5)

    def gain(k, shape):
        return jnp.ones(shape, f32) + 0.02 * jax.random.normal(k, shape, f32)

    x = jax.random.normal(ks[0], (BATCH, SEQ, D_MODEL), f32)
    mem = jax.random.normal(ks[1], (BATCH, N_MEM, D_MODEL), f32)
    return {
        "x": x,
        "mem": mem,
        "mix_norm": gain(ks[2], (DEPTH_2, D_MODEL)),
        "a_in": nrm(ks[3], (N_A_LAYERS, D_MODEL, 3 * MAIN_WIDTH + MEM_WIDTH), D_MODEL),
        "conv_w": nrm(ks[4], (N_A_LAYERS, CONV_WIDTH, MAIN_WIDTH), CONV_WIDTH),
        "b_in": nrm(ks[5], (N_B_LAYERS, D_MODEL, MAIN_WIDTH + MEM_WIDTH), D_MODEL),
        "kv_norm": gain(ks[6], (D_MODEL,)),
        "w_kv_shared": nrm(ks[7], (D_MODEL, 2 * MAIN_WIDTH), D_MODEL),
        "w_mem_kv": nrm(ks[8], (DEPTH_2, D_MODEL, 2 * MEM_WIDTH), D_MODEL),
        "w_o": nrm(ks[9], (DEPTH_2, MIX_WIDTH_2, D_MODEL), MIX_WIDTH_2),
        "ffn_norm": gain(ks[10], (DEPTH_2, D_MODEL)),
        "w_gate": nrm(ks[11], (DEPTH_2, D_MODEL, D_FF_2), D_MODEL),
        "w_up": nrm(ks[12], (DEPTH_2, D_MODEL, D_FF_2), D_MODEL),
        "w_down": nrm(ks[13], (DEPTH_2, D_FF_2, D_MODEL), D_FF_2),
        "mem_norm": gain(ks[14], (D_MODEL,)),
        "final_norm": gain(ks[15], (D_MODEL,)),
    }

def second_block(x, mem, mix_norm, a_in, conv_w, b_in, kv_norm, w_kv_shared, w_mem_kv,
              w_o, ffn_norm, w_gate, w_up, w_down, mem_norm, final_norm):
    b, s_len, _ = x.shape
    m_len = mem.shape[1]
    mem_n = rmsnorm(mem, mem_norm)
    k_sh = None
    v_sh = None
    for i in range(DEPTH_2):
        h = rmsnorm(x, mix_norm[i])
        mkv = (mem_n @ w_mem_kv[i]).reshape(b, m_len, 2, MEM_HEADS, HEAD_DIM)
        mem_k, mem_v = mkv[:, :, 0], mkv[:, :, 1]
        if i < N_A_LAYERS:
            p = h @ a_in[i]
            b_gate = p[..., :MAIN_WIDTH]
            c_gate = p[..., MAIN_WIDTH:2 * MAIN_WIDTH]
            u = p[..., 2 * MAIN_WIDTH:3 * MAIN_WIDTH]
            q_mem = p[..., 3 * MAIN_WIDTH:]
            y_main = b_gate * causal_short_conv(c_gate * u, conv_w[i])
        else:
            j = i - N_A_LAYERS
            p = h @ b_in[j]
            q_sb = p[..., :MAIN_WIDTH].reshape(b, s_len, SB_HEADS, HEAD_DIM)
            q_mem = p[..., MAIN_WIDTH:]
            y_main = stick_breaking_attention(q_sb, k_sh, v_sh).reshape(b, s_len, MAIN_WIDTH)
        y_mem = memory_cross_attention(
            q_mem.reshape(b, s_len, MEM_HEADS, HEAD_DIM), mem_k, mem_v
        ).reshape(b, s_len, MEM_WIDTH)
        x = x + jnp.concatenate([y_main, y_mem], axis=-1) @ w_o[i]
        x = x + swiglu_2(rmsnorm(x, ffn_norm[i]), w_gate[i], w_up[i], w_down[i])
        if i == N_A_LAYERS - 1:
            kv = (rmsnorm(x, kv_norm) @ w_kv_shared).reshape(b, s_len, 2, SB_HEADS, HEAD_DIM)
            k_sh, v_sh = kv[:, :, 0], kv[:, :, 1]
    return rmsnorm(x, final_norm)


def setup_inputs(seed=0):
    out = dict(first_inputs(seed))
    for name, value in second_inputs(seed + 1).items():
        if name != "x":
            out[name + "_2"] = value
    return out


def reference(
    x, ff1_norm_pre, ff1_w_gate, ff1_w_up, ff1_w_down, ff1_norm_post, mix_norm_pre, w_in,
    lambda_q1, lambda_k1, lambda_q2, lambda_k2, diff_subln, cmp_pe_k, cmp_k_w1, cmp_k_w2,
    cmp_pe_v, cmp_v_w1, cmp_v_w2, w_out, mix_norm_post, ff2_norm_pre, ff2_w_gate, ff2_w_up,
    ff2_w_down, ff2_norm_post, mem_2, mix_norm_2, a_in_2, conv_w_2, b_in_2, kv_norm_2,
    w_kv_shared_2, w_mem_kv_2, w_o_2, ffn_norm_2, w_gate_2, w_up_2, w_down_2, mem_norm_2,
    final_norm_2,
):
    x = first_block(
        x, ff1_norm_pre, ff1_w_gate, ff1_w_up, ff1_w_down, ff1_norm_post, mix_norm_pre, w_in,
        lambda_q1, lambda_k1, lambda_q2, lambda_k2, diff_subln, cmp_pe_k, cmp_k_w1, cmp_k_w2,
        cmp_pe_v, cmp_v_w1, cmp_v_w2, w_out, mix_norm_post, ff2_norm_pre, ff2_w_gate, ff2_w_up,
        ff2_w_down, ff2_norm_post,
    )
    return second_block(
        x, mem_2, mix_norm_2, a_in_2, conv_w_2, b_in_2, kv_norm_2, w_kv_shared_2, w_mem_kv_2,
        w_o_2, ffn_norm_2, w_gate_2, w_up_2, w_down_2, mem_norm_2, final_norm_2,
    )


_drawn_inputs = setup_inputs


def setup_inputs(seed=0):
    import zlib

    import numpy as np

    out = dict(_drawn_inputs(seed))
    spreads = {}
    factors = {'lambda_k1': 8.0,
     'lambda_q2': 8.0,
     'cmp_pe_k': 8.0,
     'mix_norm_2': 3.147,
     'kv_norm_2': 37.273,
     'ffn_norm_2': 4.401,
     'mem_norm_2': 8.0,
     'final_norm_2': 8.23}
    for name, (base, spread) in spreads.items():
        noise = np.random.default_rng([zlib.crc32(name.encode()), seed]).standard_normal(out[name].shape)
        drawn = base * np.exp(spread * noise) if base else spread * noise
        out[name] = jnp.asarray(drawn.astype(out[name].dtype))
    for name, factor in factors.items():
        out[name] = (out[name] * factor).astype(out[name].dtype)
    return out
```

```python
from contextlib import ExitStack

import numpy as np

import concourse.bass as bass
from concourse import mybir

P = 128
S = 512
NT = S // P
D = 1024
KC = D // P
FF = 2816
FC = FF // P
M = 256
DH = 64
EPS = 1e-6
NEG = -1e30
SPW = 40.0
NCMP = 31
NG = 2
LAMBDA_INIT = 0.2
QSCALE = DH ** -0.5

RING = 4
LOADS = RING // 2

PARTS = [("mem0", 4), ("mem1", 4), ("gu0", 2 * FC), ("down0", FC),
         ("proj1", 23), ("w1", 8), ("out1", 8), ("gu1", 2 * FC), ("down1", FC),
         ("projA", 20), ("outA", 8), ("gu2", 2 * FC), ("down2", FC),
         ("kv", 12), ("projB", 8), ("outB", 8), ("gu3", 2 * FC), ("down3", FC)]
U0 = {}
_u = 0
for _name, _n in PARTS:
    U0[_name] = _u
    _u += _n
NUNITS = _u
NLOAD = -(-NUNITS // RING) * RING

GAINS = ["mem", "ff1_pre", "ff1_post", "mix_pre", "mix_post", "ff2_pre", "ff2_post",
         "mixA", "ffnA", "kv", "mixB", "ffnB", "final"]
GCOL = {g: KC * i for i, g in enumerate(GAINS)}
C_SUB = KC * len(GAINS)
C_LAM = C_SUB + 1
C_PE = C_LAM + 4
C_W2 = C_PE + 32
C_CONV = C_W2 + 256
NSMALL = C_CONV + 18

K_ONE, K_NEG, K_TRI, K_ID, K_PERM, K_MASK, K_COS, K_SIN, K_ROW = 0, 128, 256, 384, 512, 640, 768, 1280, 1792
NCONST = K_ROW + 32
B_ID, B_CAUSAL, B_STRICT, B_CMP = 0, 128, 256, 384
NCONSTB = B_CMP + NT * 32

NORMS = [("mem", KC), ("ff1_pre", KC), ("ff1_post", KC), ("mix_pre", KC),
         ("sub0", 1), ("sub1", 1), ("sub2", 1), ("sub3", 1), ("mix_post", KC), ("ff2_pre", KC),
         ("ff2_post", KC), ("mixA", KC), ("ffnA", KC), ("kv", KC), ("ffnB", KC), ("final", KC)]
NIDX, SQ0 = {}, {}
_q = 0
for _i, (_name, _n) in enumerate(NORMS):
    NIDX[_name], SQ0[_name] = _i, _q
    _q += _n

XN = {n: i for i, n in enumerate(
    ["mem", "ff1", "proj1", "out1", "ff2", "projA", "outA", "ffnA", "kv", "projB", "outB", "ffnB"])}
XU = {n: i for i, n in enumerate(["ff1", "mix1", "ff2", "mixA", "ffnA", "mixB", "ffnB"])}


def attention_groups(part):
    out = []
    if part == "mix1":
        for c in range(4):
            for i in range(NT):
                out.append(dict(kind="diff", chunk=c, half=0, tile=i, blocks=i + 1,
                                first=True, last=True, end=i == NT - 1))
        for c in range(4, 8):
            for g in range(NG):
                for i in range(NT):
                    for b, kind in enumerate(("cmp", "sel", "win")):
                        out.append(dict(kind=kind, chunk=c, half=g, tile=i,
                                        blocks=1 if kind == "cmp" else i + 1, first=b == 0, last=b == 2,
                                        gate=3 * (c - 4 + 4 * g) + b,
                                        end=b == 2 and g == 1 and i == NT - 1))
    else:
        for c in range(6, 8):
            for g in range(2):
                for i in range(NT):
                    out.append(dict(kind="mem", chunk=c, half=g, tile=i, blocks=M // P, first=True,
                                    last=True, end=g == 1 and i == NT - 1))
    return out


def number_groups():
    plans, s, g, o = {}, 0, 0, 0
    for part in ("mix1", "mixA", "mixB"):
        plans[part] = attention_groups(part)
        for x in plans[part]:
            x["g"], x["s"], x["o"] = g, s, o
            s += 2 if x["kind"] == "diff" else 1
            g += 1
            if x["end"]:
                o += 1
    return plans, s


ATT, NSTEP = number_groups()
LAG_T, LAG_V = 2, 3


def program(nc, xT, memT, wstream, small, consts, constsb, out):
    F, R, BF = mybir.dt.float32, mybir.dt.float32r, mybir.dt.bfloat16
    ALU, ACT, AX = mybir.AluOpType, mybir.ActivationFunctionType, mybir.AxisListType

    ctx = ExitStack()
    with ctx:
        def sb(name, shape, dt=F):
            return ctx.enter_context(nc.sbuf_tensor(name, shape, dt))

        def sem(name):
            return ctx.enter_context(nc.semaphore(name))

        X = sb("X", [P, KC, S])
        XH = sb("XH", [P, KC, S], R)
        XL = sb("XL", [P, KC, S], R)
        W = sb("WORK", [P, FC, S])
        RAW = sb("RAW", [P, RING, D])
        WH = sb("WH", [P, RING, KC, P], R)
        WL = sb("WL", [P, RING, KC, P], R)
        HH = sb("HH", [P, 2, S], R)
        HL = sb("HL", [P, 2, S], R)
        RSTD = sb("RSTD", [P, S])
        LNV = sb("LNV", [P, S])
        SQ = sb("SQ", [P, 2, S])
        TMP = sb("TMP", [P, 2, S])
        Y7 = sb("Y7", [P, S])
        PB = sb("PB", [P, 4, S])
        PT = sb("PT", [P, 2, S])
        CST = sb("CST", [P, NCONST])
        CSB = sb("CSB", [P, NCONSTB], BF)
        SM = sb("SM", [P, NSMALL])
        MK = sb("MK", [P, 2, 2, M])
        MV = sb("MV", [P, 2, 2, M])
        NMAX = sb("NMAX", [P, NSTEP])
        RSUM = sb("RSUM", [P, NSTEP])
        REC = sb("REC", [P, NSTEP])
        GATE = sb("GATE", [P, NT, 24])
        LAM = sb("LAM", [P, 8])
        HID = sb("HID", [P, 2, 2, 2 * NCMP])
        KCT = sb("KCT", [P, 32])
        VC = sb("VC", [32, P])
        EPSB = sb("EPSB", [P, 1])
        PS = ctx.enter_context(nc.psum_tensor("PS", [P, 8, S], F))

        Q = W
        V_DIFF = W[:, 14:18, :]
        V_SEL = W[:, 18, :].rearrange("p (t c) -> p t c", t=NT)
        V_WIN = W[:, 19, :].rearrange("p (t c) -> p t c", t=NT)
        V_SB = W[:, 14:20, :].rearrange("p a b -> p (a b)").rearrange("p (t c) -> p t c", t=NT)
        Z = W[:, 16:20, :].rearrange("p a b -> p (a b)").rearrange("p (t c) -> p t c", t=2)[:, :, 0:S + 2]
        BH = HH[:, :, :].rearrange("p a b -> p (a b)")[:, 0:16 * 2 * NCMP].rearrange("p (l n) -> p l n", l=16)
        BL = HL[:, :, :].rearrange("p a b -> p (a b)")[:, 0:16 * 2 * NCMP].rearrange("p (l n) -> p l n", l=16)
        BT = TMP[:, :, :].rearrange("p a b -> p (a b)")[:, 0:16 * 2 * NCMP]
        ONES, NEGS, TRI = CST[:, K_ONE:K_ONE + P], CST[:, K_NEG:K_NEG + P], CST[:, K_TRI:K_TRI + P]
        IDF, PERM = CST[:, K_ID:K_ID + P], CST[:, K_PERM:K_PERM + P]
        COS, SIN = CST[:, K_COS:K_COS + S], CST[:, K_SIN:K_SIN + S]
        CSB_IN = W[:, 8:10, :].rearrange("p a b -> p (a b)")[:, 0:NCONSTB]
        IDB = CSB[:, B_ID:B_ID + P]

        def gain(name, k):
            return SM[:, GCOL[name] + k:GCOL[name] + k + 1]

        consts_in = sem("consts_in")
        masks_ready = sem("masks_ready")
        x_in = sem("x_in")
        mem_in = sem("mem_in")
        loaded = [sem(f"loaded{i}") for i in range(LOADS)]
        hi_done = sem("hi_done")
        split_ready = sem("split_ready")
        unit_done = sem("unit_done")
        sq_ready = sem("sq_ready")
        sq_used = sem("sq_used")
        ln_done = sem("ln_done")
        rstd_ready = sem("rstd_ready")
        t_ready = sem("t_ready")
        xh_ready = sem("xh_ready")
        xn_ready = sem("xn_ready")
        x_ready = sem("x_ready")
        silu_done = sem("silu_done")
        gu_free = sem("gu_free")
        hk_hi = sem("hk_hi")
        hk_ready = sem("hk_ready")
        y7_done = sem("y7_done")
        taken = sem("taken")
        raw_q = sem("raw_q")
        swapped = sem("swapped")
        roped = sem("roped")
        qk_done = sem("qk_done")
        nmax_ready = sem("nmax_ready")
        exp_done = sem("exp_done")
        p_ready = sem("p_ready")
        tr_done = sem("tr_done")
        pt_ready = sem("pt_ready")
        pv_done = sem("pv_done")
        o_taken = sem("o_taken")
        dve_chain = sem("dve_chain")
        lam_prod, lam_sum, lam_exp = sem("lam_prod"), sem("lam_sum"), sem("lam_exp")
        eps_set = sem("eps_set")
        stack_raw = sem("stack_raw")
        stacked = sem("stacked")
        b_tmp, b_hi, b_ready = sem("b_tmp"), sem("b_hi"), sem("b_ready")
        hid_ready = sem("hid_ready")
        cmp_done = sem("cmp_done")
        cmp_taken = sem("cmp_taken")
        gates_raw, gates_ready = sem("gates_raw"), sem("gates_ready")
        cg_ready = sem("cg_ready")
        z_ready = sem("z_ready")
        zsc_done, zcl_done = sem("zsc_done"), sem("zcl_done")
        sb_qk, sb_clip, sb_exp, sb_ln = sem("sb_qk"), sem("sb_clip"), sem("sb_exp"), sem("sb_ln")
        sb_l, sb_r, sb_tri, sb_a, sb_pv, sb_o = (sem("sb_l"), sem("sb_r"), sem("sb_tri"), sem("sb_a"),
                                                 sem("sb_pv"), sem("sb_o"))
        out_ready, stored = sem("out_ready"), sem("stored")

        SBSTEPS = [(h, j) for h in range(12) for j in range(NT - 1, -1, -1)]

        P1_ROPE, P1_CMP, P1_V, P1_GATE = range(0, 14), range(14, 16), range(16, 22), 22

        block = ctx.enter_context(nc.Block())

        @block.sync
        def _(sp):
            sp.dma_start(CST[:, :], consts).then_inc(consts_in, 16)
            sp.dma_start(SM[:, :], small).then_inc(consts_in, 16)
            sp.dma_start(CSB_IN, constsb).then_inc(consts_in, 16)
            sp.dma_start(W[:, 0:4, :].rearrange("p a b -> p (a b)"), memT).then_inc(mem_in, 16)
            for s in range(LOADS):
                sp.dma_start(RAW[:, 2 * s:2 * s + 2, :].rearrange("p a b -> p (a b)"),
                             wstream[s]).then_inc(loaded[s], 16)
            sp.dma_start(X[:, :, :].rearrange("p a b -> p (a b)"), xT).then_inc(x_in, 16)
            with sp.Fori(1, NLOAD // RING) as i:
                for s in range(LOADS):
                    sp.wait_ge(split_ready, i * RING + (2 * s + 2 - RING))
                    sp.dma_start(RAW[:, 2 * s:2 * s + 2, :].rearrange("p a b -> p (a b)"),
                                 wstream[bass.ds(i * LOADS + s, 1)].rearrange("o p n -> (o p) n")
                                 ).then_inc(loaded[s], 16)
            for k in range(KC):
                sp.wait_ge(out_ready, k + 1)
                sp.dma_start(out[:, k, :], W[:, k, :]).then_inc(stored, 16)
            sp.wait_ge(stored, 16 * KC)

        @block.gpsimd
        def _(pool):
            with pool.Fori(0, NLOAD // RING) as i:
                for s in range(RING):
                    pool.wait_ge(hi_done, i * RING + (s + 1))
                    pool.tensor_tensor(WL[:, s, :, :].rearrange("p a b -> p (a b)"), RAW[:, s, :],
                                       WH[:, s, :, :].rearrange("p a b -> p (a b)").bitcast(F),
                                       ALU.subtract).then_inc(split_ready, 1)

        @block.scalar
        def _(act):
            def round_unit(v, i=None):
                if v >= NLOAD:
                    return
                n = 16 * (v // RING + 1)
                act.wait_ge(loaded[(v // 2) % LOADS], n if i is None else i * 16 + n)
                act.activation(WH[:, v % RING, :, :].rearrange("p a b -> p (a b)"), RAW[:, v % RING, :],
                               ACT.Copy).then_inc(hi_done, 1)

            def unit(u, i=None):
                act.wait_ge(unit_done, u + 1 if i is None else i * RING + (u + 1))

            def norm(name, src, n, ready, cols=S, wait_each=True):
                for k in range(n):
                    ready(k)
                    q = SQ0[name] + k
                    if q >= 2:
                        act.wait_ge(sq_used, q - 1)
                    act.activation(SQ[:, q % 2, 0:cols], src(k), ACT.Square).then_inc(sq_ready, 1)
                act.wait_ge(sq_used, SQ0[name] + n)
                if NIDX[name]:
                    act.wait_ge(rstd_ready, NIDX[name])
                act.activation(LNV[:, 0:cols], PS[:, 7, 0:cols], ACT.Ln, bias=EPSB[:, 0:1],
                               scale=1.0 / (n * P)).then_inc(ln_done, 1)
                act.wait_ge(ln_done, NIDX[name] + 1)
                act.activation(RSTD[:, 0:cols], LNV[:, 0:cols], ACT.Exp, scale=-0.5).then_inc(rstd_ready, 1)

            def round_x(stage, cols=S):
                for k in range(KC):
                    act.wait_ge(t_ready, T0[stage] + k + 1)
                    act.activation(XH[:, k, 0:cols], TMP[:, k % 2, 0:cols], ACT.Copy).then_inc(xh_ready, 1)

            def round_o(stage, ready):
                for k in range(KC):
                    ready(k)
                    act.activation(XH[:, k, :], W[:, k, :], ACT.Copy).then_inc(xh_ready, 1)

            def x_updated(stage):
                return lambda k: act.wait_ge(x_ready, KC * XU[stage] + k + 1)

            def gate_up(l):
                u0 = U0[f"gu{l}"]

                def step(f, slot, i=None):
                    u = u0 + 2 * f
                    unit(u, i)
                    if f >= 2:
                        n = FC * l + f - 1
                        act.wait_ge(gu_free, n if i is None else i * 2 + n)
                    act.activation(SQ[:, slot, :], PS[:, 2 * slot, :], ACT.Silu).then_inc(silu_done, 1)
                    round_unit(u + RING, i)
                    unit(u + 1, i)
                    round_unit(u + 1 + RING, i)

                step(0, 0)
                step(1, 1)
                with act.Fori(0, FC // 2 - 1) as i:
                    step(2, 0, i)
                    step(3, 1, i)

            def down(l):
                u0 = U0[f"down{l}"]
                for k in range(2):
                    act.wait_ge(gu_free, FC * l + k + 1)
                    act.activation(HH[:, k, :], W[:, k, :], ACT.Copy).then_inc(hk_hi, 1)
                act.wait_ge(gu_free, FC * (l + 1))
                turns = (FC - 2) // RING - 1
                with act.Fori(0, turns) as i:
                    for s in range(RING):
                        unit(u0 + s, i)
                        round_unit(u0 + s + RING, i)
                        act.activation(HH[:, s % 2, :],
                                       W[:, bass.ds(i * RING + (s + 2), 1), :].rearrange("p a b -> p (a b)"),
                                       ACT.Copy).then_inc(hk_hi, 1)
                for k in range(turns * RING, FC):
                    unit(u0 + k)
                    round_unit(u0 + k + RING)
                    if k + 2 < FC:
                        act.activation(HH[:, k % 2, :], W[:, k + 2, :], ACT.Copy).then_inc(hk_hi, 1)

            def refill(part, n, off=0):
                for u in range(U0[part] + off, U0[part] + off + n):
                    unit(u)
                    round_unit(u + RING)

            def attention(part):
                gs = ATT[part]
                for t in range(len(gs) + LAG_T):
                    if t < len(gs):
                        x = gs[t]
                        for m in range(2 if x["kind"] == "diff" else 1):
                            s = x["s"] + m
                            n = NCMP if x["kind"] == "cmp" else x["blocks"] * P
                            act.wait_ge(nmax_ready, s + 1)
                            if s >= 4:
                                act.wait_ge(tr_done, GROUP_OF[s - 4] + 1)
                            act.activation(PB[:, s % 4, 0:n], PS[:, s % 4, 0:n], ACT.Exp,
                                           bias=NMAX[:, s:s + 1],
                                           accum_out=RSUM[:, s:s + 1]).then_inc(exp_done, 1)
                    if t >= LAG_T:
                        x = gs[t - LAG_T]
                        g = x["g"]
                        act.wait_ge(tr_done, g + 1)
                        if g >= 2:
                            act.wait_ge(pv_done, g - 1)
                        kp = NCMP if x["kind"] == "cmp" else P
                        act.activation(PT[0:kp, g % 2, 0:x["blocks"] * P],
                                       PS[0:kp, 4 + g % 2, 0:x["blocks"] * P], ACT.Copy).then_inc(pt_ready, 1)

            def mem_project(layer):
                u0 = U0[f"mem{layer}"]
                for j in range(4):
                    unit(u0 + j)
                    if j < 2:
                        act.activation(MK[:, layer, j, :], PS[:, j, 0:M], ACT.Copy).then_inc(taken, 1)
                    else:
                        act.activation(MV[:, layer, :, (j - 2) * P:(j - 1) * P],
                                       PS[:, j, 0:2 * P].rearrange("p (t c) -> p t c", t=2),
                                       ACT.Copy).then_inc(taken, 1)
                    round_unit(u0 + j + RING)

            act.wait_ge(eps_set, 1)
            for v in range(RING):
                round_unit(v)
            act.wait_ge(lam_sum, 1)
            act.activation(LAM[:, 2:4], PS[:, 6, 0:2], ACT.Exp).then_inc(lam_exp, 1)
            norm("mem", lambda k: W[:, k // 2, (k % 2) * M:(k % 2 + 1) * M], KC,
                 lambda k: act.wait_ge(mem_in, 16), cols=M)
            round_x("mem", M)
            mem_project(0)
            mem_project(1)
            norm("ff1_pre", lambda k: X[:, k, :], KC, lambda k: act.wait_ge(x_in, 16))
            round_x("ff1")
            gate_up(0)
            down(0)

            def y_bank(name, part, last):
                def ready(k):
                    if k == KC - 1:
                        act.wait_ge(y7_done, last)
                return norm(name, lambda k: PS[:, k, :] if k < KC - 1 else Y7[:, :], KC, ready)

            y_bank("ff1_post", "down0", 1)
            norm("mix_pre", lambda k: X[:, k, :], KC, x_updated("ff1"))
            round_x("proj1")
            u0 = U0["proj1"]
            for j in P1_ROPE:
                unit(u0 + j)
                if j >= 2:
                    act.wait_ge(roped, j - 1)
                act.activation(SQ[:, j % 2, :], PS[:, j % 4, :], ACT.Copy,
                               scale=QSCALE if j < 8 else 1.0).then_inc(raw_q, 1)
                round_unit(u0 + j + RING)
            for j in P1_CMP:
                unit(u0 + j)
                act.activation(W[:, 20 + j - 14, :], PS[:, j % 4, :], ACT.Copy).then_inc(stack_raw, 1)
                round_unit(u0 + j + RING)
            for j in P1_CMP:
                act.wait_ge(stack_raw, 2)
                for g in range(NG):
                    for par in range(2):
                        act.dma_start(PB[par * DH:(par + 1) * DH, 2 * (j - 14) + g, 0:S - 1],
                                      W[g * DH:(g + 1) * DH, 20 + j - 14, par:par + S - 1]
                                      ).then_inc(stacked, 16)
            for j in P1_V:
                unit(u0 + j)
                round_unit(u0 + j + RING)
            unit(u0 + P1_GATE)
            act.activation(GATE[:, :, :], PS[:, P1_GATE % 4, :].rearrange("p (t c) -> p t c", t=NT)[:, :, 0:24],
                           ACT.Sigmoid).then_inc(gates_raw, 1)
            round_unit(u0 + P1_GATE + RING)
            for kv in range(2):
                act.wait_ge(b_tmp, 16 * (kv + 1))
                if kv:
                    refill("w1", 4)
                act.activation(HH[:, :, :].rearrange("p a b -> p (a b)")[:, 0:32 * NCMP], BT,
                               ACT.Copy).then_inc(b_hi, 1)
            refill("w1", 4, 4)
            for kv in range(2):
                for hc in range(2):
                    act.activation(HID[:, kv, hc, :], PS[:, 2 * kv + hc, 0:2 * NCMP],
                                   ACT.Gelu_apprx_tanh).then_inc(hid_ready, 1)
            act.wait_ge(cmp_done, 1)
            act.activation(KCT[:, 0:NCMP], PS[:, 4, 0:NCMP], ACT.Copy).then_inc(cmp_taken, 1)
            act.activation(VC[0:NCMP, :], PS[0:NCMP, 5, 0:P], ACT.Copy).then_inc(cmp_taken, 1)
            attention("mix1")
            for h in range(4):
                norm(f"sub{h}", lambda k: W[:, h, :], 1, lambda k: act.wait_ge(o_taken, h + 1))
                act.wait_ge(t_ready, T0["sub"] + h + 1)
                act.activation(XH[:, h, :], W[:, h, :], ACT.Copy).then_inc(xh_ready, 1)
            for k in range(4, KC):
                act.wait_ge(o_taken, k + 1)
                act.activation(XH[:, k, :], W[:, k, :], ACT.Copy).then_inc(xh_ready, 1)
            refill("out1", 8)
            y_bank("mix_post", "out1", 2)
            norm("ff2_pre", lambda k: X[:, k, :], KC, x_updated("mix1"))
            round_x("ff2")
            gate_up(1)
            down(1)
            y_bank("ff2_post", "down1", 3)
            norm("mixA", lambda k: X[:, k, :], KC, x_updated("ff2"))
            round_x("projA")
            u0 = U0["projA"]
            for c in range(6):
                for j in range(3):
                    u = 3 * c + j
                    unit(u0 + u)
                    if j == 0:
                        if c >= 2:
                            act.wait_ge(z_ready, c - 1)
                        act.activation(W[:, 12 + c % 2, :], PS[:, u % 4, :], ACT.Copy).then_inc(cg_ready, 1)
                    round_unit(u0 + u + RING)
            refill("projA", 2, 18)
            attention("mixA")
            round_o("outA", lambda k: act.wait_ge(taken, T_CONV + k + 1) if k < 6 else
                    act.wait_ge(o_taken, 8 + k - 5))
            refill("outA", 8)
            norm("ffnA", lambda k: X[:, k, :], KC, x_updated("mixA"))
            round_x("ffnA")
            gate_up(2)
            down(2)
            norm("kv", lambda k: X[:, k, :], KC, x_updated("ffnA"))
            round_x("kv")
            refill("kv", 12)
            round_x("projB")
            refill("projB", 8)
            n = len(SBSTEPS)
            for t in range(n + 2):
                if t < n:
                    w = S - SBSTEPS[t][1] * P
                    act.wait_ge(sb_clip, t + 1)
                    act.activation(PT[:, t % 2, 0:w], PT[:, t % 2, 0:w], ACT.Exp).then_inc(sb_exp, 1)
                    act.wait_ge(sb_exp, t + 1)
                    act.activation(PT[:, t % 2, 0:w], PT[:, t % 2, 0:w], ACT.Ln, bias=1.0).then_inc(sb_ln, 1)
                if t >= 2:
                    a = t - 2
                    w = S - SBSTEPS[a][1] * P
                    act.wait_ge(sb_tri, a + 1)
                    if a >= 2:
                        act.wait_ge(sb_pv, a - 1)
                    act.activation(PB[:, 2 + a % 2, 0:w], PS[:, a % 4, 0:w], ACT.Exp).then_inc(sb_a, 1)
            attention("mixB")
            round_o("outB", lambda k: act.wait_ge(sb_o, k + 1) if k < 6 else
                    act.wait_ge(o_taken, 10 + k - 5))
            refill("outB", 8)
            norm("ffnB", lambda k: X[:, k, :], KC, x_updated("mixB"))
            round_x("ffnB")
            gate_up(3)
            down(3)
            norm("final", lambda k: X[:, k, :], KC, x_updated("ffnB"))

        @block.tensor
        def _(pe):
            def three(o, wh, wl, xh, xl, start, stop):
                pe.matmul(o, wh, xh, start=start, stop=False)
                pe.matmul(o, wh, xl, start=False, stop=False)
                return pe.matmul(o, wl, xh, start=False, stop=stop)

            def have(u, i=None):
                pe.wait_ge(split_ready, u + 1 if i is None else i * RING + (u + 1))

            def features(u, bank, stage, cols=S, first=False, i=None):
                have(u, i)
                for k in range(KC):
                    if first:
                        pe.wait_ge(xn_ready, KC * XN[stage] + k + 1)
                    mm = three(PS[:, bank, 0:cols], WH[:, u % RING, k, :], WL[:, u % RING, k, :],
                               XH[:, k, 0:cols], XL[:, k, 0:cols], k == 0, k == KC - 1)
                mm.then_inc(unit_done, 1)

            def tokens(u, bank, tiles=NT):
                have(u)
                for t in range(tiles):
                    for k in range(KC):
                        xh, xl = XH[:, k, t * P:(t + 1) * P], XL[:, k, t * P:(t + 1) * P]
                        wh, wl = WH[:, u % RING, k, :], WL[:, u % RING, k, :]
                        o = PS[:, bank, t * P:(t + 1) * P]
                        pe.matmul(o, xh, wh, start=k == 0, stop=False)
                        pe.matmul(o, xh, wl, start=False, stop=False)
                        mm = pe.matmul(o, xl, wh, start=False, stop=k == KC - 1)
                mm.then_inc(unit_done, 1)

            def norm(name, n, cols=S):
                for k in range(n):
                    q = SQ0[name] + k
                    pe.wait_ge(sq_ready, q + 1)
                    pe.matmul(PS[:, 7, 0:cols], ONES, SQ[:, q % 2, 0:cols], start=k == 0,
                              stop=k == n - 1).then_inc(sq_used, 1)

            def gate_up(l, stage):
                u0 = U0[f"gu{l}"]
                for f in range(2):
                    for j in range(2):
                        features(u0 + 2 * f + j, 2 * f + j, stage, first=f + j == 0)
                with pe.Fori(0, FC // 2 - 1) as i:
                    for f in range(2):
                        pe.wait_ge(gu_free, i * 2 + (FC * l + f + 1))
                        for j in range(2):
                            features(u0 + 4 + 2 * f + j, 2 * f + j, stage, i=i)

            def down(l):
                u0 = U0[f"down{l}"]

                def step(k, order=range(KC), i=None):
                    u = u0 + k
                    have(u, i)
                    n = FC * l + k + 1
                    pe.wait_ge(hk_ready, n if i is None else i * RING + n)
                    for c in order:
                        if k == 0 and c == 0:
                            pe.wait_ge(gu_free, FC * (l + 1))
                        mm = three(PS[:, c, :], WH[:, u % RING, c, :], WL[:, u % RING, c, :],
                                   HH[:, k % 2, :], HL[:, k % 2, :], k == 0, k == FC - 1)
                    mm.then_inc(unit_done, 1)

                step(0, (4, 5, 6, 7, 0, 1, 2, 3))
                step(1)
                with pe.Fori(0, (FC - 2) // RING - 1) as i:
                    for s in range(RING):
                        step(2 + s, i=i)
                for k in range(FC - RING, FC):
                    step(k)

            def projection(part, n, stage, free, tok=(), first_bank=0, banks=4):
                for j in range(n):
                    if j >= banks:
                        free(j - banks)
                    if j in tok:
                        tokens(U0[part] + j, j % banks)
                    else:
                        features(U0[part] + j, j % banks, stage, first=j == 0)

            def scores(part, x):
                c, h, i = x["chunk"], x["half"], x["tile"]
                for m in range(2 if x["kind"] == "diff" else 1):
                    s = x["s"] + m
                    if s >= 4:
                        pe.wait_ge(exp_done, s - 3)
                    r = slice(DH * (m if x["kind"] == "diff" else h), DH * (m if x["kind"] == "diff" else h) + DH)
                    q = Q[r, c, i * P:(i + 1) * P]
                    n = x["blocks"] * P
                    if x["kind"] == "diff":
                        k = W[r, 8 + c, 0:n]
                    elif x["kind"] == "sel":
                        k = W[r, 12, 0:n]
                    elif x["kind"] == "win":
                        k = W[r, 13, 0:n]
                    elif x["kind"] == "cmp":
                        n = NCMP
                        k = KCT[r, 0:n]
                    else:
                        k = MK[r, 0 if part == "mixA" else 1, c - 6, :]
                    masked = x["kind"] != "mem"
                    mm = pe.matmul(PS[:, s % 4, 0:n], q, k, start=True, stop=not masked)
                    if x["kind"] == "cmp":
                        mm = pe.matmul(PS[:, s % 4, 0:n], IDB, CSB[:, B_CMP + 32 * i:B_CMP + 32 * i + n],
                                       start=False, stop=True)
                    elif masked:
                        mm = pe.matmul(PS[:, s % 4, n - P:n], IDB, CSB[:, B_CAUSAL:B_CAUSAL + P],
                                       start=False, stop=True)
                    mm.then_inc(qk_done, 1)

            def transposes(x):
                g = x["g"]
                pe.wait_ge(p_ready, g + 1)
                if g >= 2:
                    pe.wait_ge(pt_ready, g - 1)
                for b in range(x["blocks"]):
                    n = NCMP if x["kind"] == "cmp" else P
                    mm = pe.transpose(PS[0:n, 4 + g % 2, b * P:(b + 1) * P],
                                      PB[:, x["s"] % 4, b * P:b * P + n], IDF)
                mm.then_inc(tr_done, 1)

            def values(part, x):
                g, c, h, i = x["g"], x["chunk"], x["half"], x["tile"]
                pe.wait_ge(pt_ready, g + 1)
                if x["first"] and h == 0 and i == 0 and x["o"] >= 2:
                    pe.wait_ge(o_taken, x["o"] - 1)
                bank = 6 + x["o"] % 2
                for b in range(x["blocks"]):
                    if x["kind"] == "diff":
                        v, o = V_DIFF[:, b, c * P:(c + 1) * P], PS[:, bank, i * P:(i + 1) * P]
                    else:
                        o = PS[h * DH:(h + 1) * DH, bank, i * P:(i + 1) * P]
                        f = slice(h * DH, (h + 1) * DH)
                        if x["kind"] == "cmp":
                            v = VC[0:NCMP, f]
                        elif x["kind"] == "sel":
                            v = V_SEL[:, b, f]
                        elif x["kind"] == "win":
                            v = V_WIN[:, b, f]
                        else:
                            f = slice((c - 6) * P + h * DH, (c - 6) * P + (h + 1) * DH)
                            v = MV[:, 0 if part == "mixA" else 1, b, f]
                    kp = NCMP if x["kind"] == "cmp" else P
                    mm = pe.matmul(o, v, PT[0:kp, g % 2, b * P:(b + 1) * P],
                                   start=x["first"] and b == 0, stop=x["last"] and b == x["blocks"] - 1)
                mm.then_inc(pv_done, 1)

            def attention(part):
                gs = ATT[part]
                for t in range(len(gs) + LAG_V):
                    if t < len(gs):
                        scores(part, gs[t])
                    if 0 <= t - LAG_T < len(gs):
                        transposes(gs[t - LAG_T])
                    if t >= LAG_V:
                        values(part, gs[t - LAG_V])

            def output(part, stage):
                for j in range(KC):
                    features(U0[part] + j, j, stage, first=j == 0)

            pe.wait_ge(consts_in, 48)
            pe.wait_ge(lam_prod, 1)
            pe.matmul(PS[:, 6, 0:2], ONES, LAM[:, 0:2], start=True, stop=True).then_inc(lam_sum, 1)
            norm("mem", KC, M)
            for layer in range(2):
                for j in range(4):
                    if layer:
                        pe.wait_ge(taken, j + 1)
                    u = U0[f"mem{layer}"] + j
                    if j < 2:
                        features(u, j, "mem", cols=M, first=layer + j == 0)
                    else:
                        tokens(u, j, tiles=2)
            pe.wait_ge(taken, 8)
            norm("ff1_pre", KC)
            gate_up(0, "ff1")
            down(0)
            pe.wait_ge(y7_done, 1)
            norm("ff1_post", KC)
            norm("mix_pre", KC)
            u0 = U0["proj1"]

            def swap(j):
                pe.wait_ge(raw_q, j + 1)
                if j >= 2:
                    pe.wait_ge(roped, j - 1)
                pe.matmul(PS[:, 4 + j % 2, :], PERM, SQ[:, j % 2, :], start=True, stop=True).then_inc(swapped, 1)

            for j in range(23):
                if 4 <= j < 18:
                    pe.wait_ge(raw_q, j - 3)
                elif 18 <= j < 20:
                    pe.wait_ge(stack_raw, j - 17)
                elif j >= 20:
                    pe.wait_ge(taken, 8 + j - 19)
                if j in P1_ROPE or j in P1_CMP:
                    features(u0 + j, j % 4, "proj1", first=j == 0)
                else:
                    tokens(u0 + j, j % 4)
                if 1 <= j < 15:
                    swap(j - 1)
            pe.wait_ge(taken, 8 + 6)
            pe.wait_ge(gates_ready, 1)
            for kv in range(2):
                pe.wait_ge(b_ready, kv + 1)
                for t in range(4):
                    u = U0["w1"] + 4 * kv + t
                    have(u)
                    for j in range(8):
                        l, hc = 4 * t + j // 2, j % 2
                        mm = three(PS[:, 2 * kv + hc, 0:2 * NCMP], WH[:, u % RING, j, :], WL[:, u % RING, j, :],
                                   BH[:, l, :], BL[:, l, :], l == 0, l == 15)
                    mm.then_inc(unit_done, 1)
            w2 = SM[:, C_W2:C_W2 + 256].rearrange("p (v h d) -> p v h d", v=2, h=2)
            pe.wait_ge(hid_ready, 4)
            for g in range(NG):
                n = slice(g * NCMP, (g + 1) * NCMP)
                for hc in range(2):
                    pe.matmul(PS[g * DH:(g + 1) * DH, 4, 0:NCMP], w2[:, 0, hc, :], HID[:, 0, hc, n],
                              start=hc == 0, stop=hc == 1)
            for g in range(NG):
                n = slice(g * NCMP, (g + 1) * NCMP)
                for hc in range(2):
                    mm = pe.matmul(PS[0:NCMP, 5, g * DH:(g + 1) * DH], HID[:, 1, hc, n], w2[:, 1, hc, :],
                                   start=hc == 0, stop=hc == 1)
            mm.then_inc(cmp_done, 1)
            pe.wait_ge(cmp_taken, 2)
            pe.wait_ge(roped, 14)
            pe.wait_ge(masks_ready, 1)
            attention("mix1")
            for h in range(4):
                if h == 0:
                    pe.wait_ge(o_taken, 8)
                else:
                    pe.wait_ge(ln_done, NIDX["sub0"] + h)
                norm(f"sub{h}", 1)
            pe.wait_ge(ln_done, NIDX["sub3"] + 1)
            output("out1", "out1")
            pe.wait_ge(y7_done, 2)
            norm("mix_post", KC)
            pe.wait_ge(ln_done, NIDX["mix_post"] + 1)
            norm("ff2_pre", KC)
            gate_up(1, "ff2")
            down(1)
            pe.wait_ge(y7_done, 3)
            norm("ff2_post", KC)
            pe.wait_ge(ln_done, NIDX["ff2_post"] + 1)
            norm("mixA", KC)
            for j in range(20):
                if j >= 4:
                    c, m = (j - 4) // 3, (j - 4) % 3
                    if m == 0:
                        pe.wait_ge(cg_ready, c + 1)
                    elif m == 1:
                        pe.wait_ge(z_ready, c + 1)
                    else:
                        pe.wait_ge(taken, T_CONV + c + 1)
                features(U0["projA"] + j, j % 4, "projA", first=j == 0)
            pe.wait_ge(taken, T_CONV + 8)
            attention("mixA")
            pe.wait_ge(o_taken, 10)
            output("outA", "outA")
            pe.wait_ge(x_ready, KC * (XU["mixA"] + 1))
            norm("ffnA", KC)
            gate_up(2, "ffnA")
            down(2)
            pe.wait_ge(x_ready, KC * (XU["ffnA"] + 1))
            norm("kv", KC)
            for j in range(12):
                if j >= 4:
                    pe.wait_ge(taken, T_KV + j - 3)
                if j < 6:
                    features(U0["kv"] + j, j % 4, "kv", first=j == 0)
                else:
                    tokens(U0["kv"] + j, j % 4)
            for j in range(8):
                pe.wait_ge(taken, T_KV + 12 + j - 3)
                features(U0["projB"] + j, j % 4, "projB", first=j == 0)
            pe.wait_ge(taken, T_KV + 20)
            n = len(SBSTEPS)

            def sb_scores(t):
                h, j = SBSTEPS[t]
                if t >= 4:
                    pe.wait_ge(sb_a, t - 3)
                r = slice(DH * (h % 2), DH * (h % 2) + DH)
                pe.matmul(PS[:, t % 4, 0:S - j * P], W[r, 8 + h // 2, j * P:(j + 1) * P],
                          Q[r, h // 2, j * P:S], start=True, stop=True).then_inc(sb_qk, 1)

            def sb_tail(t):
                h, j = SBSTEPS[t]
                w = S - j * P
                pe.wait_ge(sb_l, t + 1)
                pe.matmul(PS[:, t % 4, 0:w], TRI, PB[:, t % 2, 0:w], start=False, stop=False,
                          skip_group_check=True)
                if j < NT - 1:
                    pe.wait_ge(sb_r, t)
                    pe.matmul(PS[:, t % 4, P:w], NEGS, W[:, 20 + (t - 1) % 2, 0:w - P], start=False,
                              stop=False, skip_group_check=True)
                pe.matmul(PS[:, t % 4, 0:P], IDB, CSB[:, B_STRICT:B_STRICT + P], start=False, stop=True,
                          skip_group_check=True).then_inc(sb_tri, 1)

            def sb_values(t):
                h, j = SBSTEPS[t]
                c = h // 2
                w = S - j * P
                pe.wait_ge(sb_a, t + 1)
                if h % 2 == 0 and j == NT - 1 and c >= 2:
                    pe.wait_ge(sb_o, c - 1)
                r = slice(DH * (h % 2), DH * (h % 2) + DH)
                pe.matmul(PS[r, 6 + c % 2, j * P:S], V_SB[:, j, h * DH:(h + 1) * DH], PB[:, 2 + t % 2, 0:w],
                          start=j == NT - 1, stop=j == 0, skip_group_check=True).then_inc(sb_pv, 1)

            for t in range(n + LAG_V):
                if t < n:
                    sb_scores(t)
                if 0 <= t - LAG_T < n:
                    sb_tail(t - LAG_T)
                if t >= LAG_V:
                    sb_values(t - LAG_V)
            pe.wait_ge(sb_o, 6)
            attention("mixB")
            pe.wait_ge(o_taken, 12)
            output("outB", "outB")
            pe.wait_ge(x_ready, KC * (XU["mixB"] + 1))
            norm("ffnB", KC)
            gate_up(3, "ffnB")
            down(3)
            pe.wait_ge(x_ready, KC * (XU["ffnB"] + 1))
            norm("final", KC)

        @block.vector
        def _(dve):
            chained = [0]

            def chain(ins):
                chained[0] += 1
                ins.then_inc(dve_chain, 1)
                dve.wait_ge(dve_chain, chained[0])

            def normed(stage, name, src, cols=S, rstd=None):
                xb = KC * XN[stage]
                dve.wait_ge(rstd_ready, NIDX[rstd or name] + 1)

                def low(k):
                    dve.wait_ge(xh_ready, xb + k + 1)
                    dve.tensor_tensor(XL[:, k, 0:cols], TMP[:, k % 2, 0:cols],
                                      XH[:, k, 0:cols].bitcast(F), ALU.subtract).then_inc(xn_ready, 1)

                for k in range(KC):
                    if k >= 2:
                        low(k - 2)
                        dve.wait_ge(xn_ready, xb + k - 1)
                    dve.scalar_tensor_tensor(TMP[:, k % 2, 0:cols], src(k), gain(name, k), RSTD[:, 0:cols],
                                             ALU.mult, ALU.mult).then_inc(t_ready, 1)
                low(KC - 2)
                low(KC - 1)
                dve.wait_ge(xn_ready, xb + KC)

            def low_o(stage):
                xb = KC * XN[stage]
                for k in range(KC):
                    dve.wait_ge(xh_ready, xb + k + 1)
                    dve.tensor_tensor(XL[:, k, :], W[:, k, :], XH[:, k, :].bitcast(F),
                                      ALU.subtract).then_inc(xn_ready, 1)

            def gate_up(l):
                u0 = U0[f"gu{l}"]
                with dve.Fori(0, FC // 2) as i:
                    for f in range(2):
                        dve.wait_ge(silu_done, i * 2 + (FC * l + f + 1))
                        dve.wait_ge(unit_done, i * RING + (u0 + 2 * f + 2))
                        dve.tensor_tensor(W[:, bass.ds(i * 2 + f, 1), :].rearrange("p a b -> p (a b)"),
                                          SQ[:, f, :], PS[:, 2 * f + 1, :], ALU.mult).then_inc(gu_free, 1)

            def down(l):
                with dve.Fori(0, FC // 2) as i:
                    for s in range(2):
                        dve.wait_ge(hk_hi, i * 2 + (FC * l + s + 1))
                        dve.tensor_tensor(HL[:, s, :], W[:, bass.ds(i * 2 + s, 1), :].rearrange("p a b -> p (a b)"),
                                          HH[:, s, :].bitcast(F), ALU.subtract).then_inc(hk_ready, 1)

            def copy_y7(part):
                n = dict(PARTS)[part]
                dve.wait_ge(unit_done, U0[part] + n)
                dve.tensor_copy(Y7[:, :], PS[:, KC - 1, :]).then_inc(y7_done, 1)

            def post(name, weight):
                dve.wait_ge(rstd_ready, NIDX[name] + 1)
                for k in range(KC):
                    y = PS[:, k, :] if k < KC - 1 else Y7[:, :]
                    chain(dve.scalar_tensor_tensor(TMP[:, k % 2, :], y, gain(name, k), RSTD[:, :],
                                                   ALU.mult, ALU.mult))
                    dve.scalar_tensor_tensor(X[:, k, :], TMP[:, k % 2, :], weight, X[:, k, :],
                                             ALU.mult, ALU.add).then_inc(x_ready, 1)

            def add_y(part, each):
                n = dict(PARTS)[part]
                for k in range(KC):
                    dve.wait_ge(unit_done, U0[part] + (k + 1 if each else n))
                    dve.tensor_tensor(X[:, k, :], X[:, k, :], PS[:, k, :], ALU.add).then_inc(x_ready, 1)

            def attention(part):
                gs = ATT[part]

                def take(x):
                    dve.wait_ge(pv_done, x["g"] + 1)
                    dve.tensor_copy(W[:, x["chunk"], :], PS[:, 6 + x["o"] % 2, :]).then_inc(o_taken, 1)

                def scale(x):
                    s, i = x["s"], x["tile"]
                    n = NCMP if x["kind"] == "cmp" else x["blocks"] * P
                    p = PB[:, s % 4, 0:n]
                    if x["kind"] == "diff":
                        dve.wait_ge(exp_done, s + 2)
                        chain(dve.reciprocal(REC[:, s:s + 2], RSUM[:, s:s + 2]))
                        chain(dve.tensor_scalar(REC[:, s + 1:s + 2], REC[:, s + 1:s + 2], LAM[:, 6:7], None,
                                                ALU.mult))
                        p1 = PB[:, (s + 1) % 4, 0:n]
                        chain(dve.tensor_scalar(p1, p1, REC[:, s + 1:s + 2], None, ALU.mult))
                        dve.scalar_tensor_tensor(p, p, REC[:, s:s + 1], p1, ALU.mult,
                                                 ALU.add).then_inc(p_ready, 1)
                        return
                    dve.wait_ge(exp_done, s + 1)
                    chain(dve.reciprocal(REC[:, s:s + 1], RSUM[:, s:s + 1]))
                    if x["kind"] == "mem":
                        dve.tensor_scalar(p, p, REC[:, s:s + 1], None, ALU.mult).then_inc(p_ready, 1)
                    else:
                        dve.tensor_scalar(p, p, REC[:, s:s + 1], GATE[:, i, x["gate"]:x["gate"] + 1],
                                          ALU.mult, ALU.mult).then_inc(p_ready, 1)

                for t in range(len(gs) + LAG_V + 2):
                    if t < len(gs):
                        x = gs[t]
                        for m in range(2 if x["kind"] == "diff" else 1):
                            s = x["s"] + m
                            n = NCMP if x["kind"] == "cmp" else x["blocks"] * P
                            dve.wait_ge(qk_done, s + 1)
                            dve.tensor_reduce(NMAX[:, s:s + 1], PS[:, s % 4, 0:n], AX.X, ALU.max,
                                              negate=True).then_inc(nmax_ready, 1)
                    if 1 <= t <= len(gs):
                        scale(gs[t - 1])
                    if 0 <= t - LAG_V - 1 < len(gs) and gs[t - LAG_V - 1]["end"]:
                        take(gs[t - LAG_V - 1])

            dve.memset(EPSB[:, :], EPS).then_inc(eps_set, 1)
            dve.wait_ge(consts_in, 48)
            dve.tensor_copy(CSB[:, :], CSB_IN).then_inc(masks_ready, 1)
            dve.wait_ge(masks_ready, 1)
            dve.tensor_tensor(LAM[:, 0:2], SM[:, C_LAM:C_LAM + 2], SM[:, C_LAM + 2:C_LAM + 4],
                              ALU.mult).then_inc(lam_prod, 1)
            dve.wait_ge(lam_exp, 1)
            chain(dve.tensor_tensor(LAM[:, 4:5], LAM[:, 3:4], LAM[:, 2:3], ALU.subtract))
            chain(dve.tensor_scalar(LAM[:, 6:7], LAM[:, 4:5], LAMBDA_INIT, None, ALU.subtract))
            normed("mem", "mem", lambda k: W[:, k // 2, (k % 2) * M:(k % 2 + 1) * M], cols=M)
            dve.wait_ge(unit_done, 8)
            normed("ff1", "ff1_pre", lambda k: X[:, k, :])
            gate_up(0)
            down(0)
            copy_y7("down0")
            post("ff1_post", 0.5)
            normed("proj1", "mix_pre", lambda k: X[:, k, :])
            u0 = U0["proj1"]
            for j in P1_ROPE:
                dst = W[:, j, :]
                t0, t1 = TMP[:, 0, :], TMP[:, 1, :]
                dve.wait_ge(raw_q, j + 1)
                chain(dve.tensor_tensor(t0, SQ[:, j % 2, :], COS, ALU.mult))
                dve.wait_ge(swapped, j + 1)
                chain(dve.tensor_tensor(t1, SIN, PS[:, 4 + j % 2, :], ALU.mult))
                dve.tensor_tensor(dst, t0, t1, ALU.add).then_inc(roped, 1)
                dve.wait_ge(roped, j + 1)
            for j in P1_V:
                dve.wait_ge(unit_done, u0 + j + 1)
                v = j - 16
                src = PS[:, j % 4, :].rearrange("p (t c) -> p t c", t=NT)
                dst = V_DIFF[:, :, v * P:(v + 1) * P] if v < 4 else (V_SEL if v == 4 else V_WIN)
                dve.tensor_copy(dst, src).then_inc(taken, 1)
            dve.wait_ge(gates_raw, 1)
            g0 = GATE[:, :, :].rearrange("p t (h b) -> p t h b", b=3)[:, :, :, 0]
            dve.tensor_tensor(g0, g0, CST[:, K_ROW:K_ROW + 32].rearrange("p (t h) -> p t h", t=NT),
                              ALU.mult).then_inc(gates_ready, 1)
            dve.wait_ge(stacked, 16 * 8)
            for kv in range(2):
                if kv:
                    dve.wait_ge(b_ready, 1)
                for l in range(16):
                    src = PB[:, 2 * kv:2 * kv + 2, 2 * l:2 * l + 16 * (NCMP - 1) + 1:16]
                    dve.tensor_scalar(TMP[:, :, :].rearrange("p a b -> p (a b)")[
                        :, 2 * NCMP * l:2 * NCMP * (l + 1)].rearrange("p (g c) -> p g c", g=NG), src,
                        SM[:, C_PE + 16 * kv + l:C_PE + 16 * kv + l + 1], None, ALU.add).then_inc(b_tmp, 1)
                dve.wait_ge(b_hi, kv + 1)
                dve.tensor_tensor(HL[:, :, :].rearrange("p a b -> p (a b)")[:, 0:32 * NCMP], BT,
                                  HH[:, :, :].rearrange("p a b -> p (a b)")[:, 0:32 * NCMP].bitcast(F),
                                  ALU.subtract).then_inc(b_ready, 1)
            attention("mix1")
            for h in range(4):
                dve.wait_ge(rstd_ready, NIDX[f"sub{h}"] + 1)
                chain(dve.scalar_tensor_tensor(W[:, h, :], W[:, h, :], SM[:, C_SUB:C_SUB + 1], RSTD[:, :],
                                               ALU.mult, ALU.mult))
                dve.tensor_scalar(W[:, h, :], W[:, h, :], 1.0 - LAMBDA_INIT, None,
                                  ALU.mult).then_inc(t_ready, 1)
            low_o("out1")
            copy_y7("out1")
            post("mix_post", 1.0)
            normed("ff2", "ff2_pre", lambda k: X[:, k, :])
            gate_up(1)
            down(1)
            copy_y7("down1")
            post("ff2_post", 0.5)
            normed("projA", "mixA", lambda k: X[:, k, :])
            for s in range(2):
                chain(dve.memset(Z[:, s, 0:2], 0.0))
            u0 = U0["projA"]
            for c in range(6):
                dve.wait_ge(cg_ready, c + 1)
                dve.wait_ge(unit_done, u0 + 3 * c + 2)
                z = Z[:, c % 2, :]
                dve.tensor_tensor(z[:, 2:S + 2], W[:, 12 + c % 2, :], PS[:, (3 * c + 1) % 4, :],
                                  ALU.mult).then_inc(z_ready, 1)
                dve.wait_ge(z_ready, c + 1)
                w = [SM[:, C_CONV + 3 * c + n:C_CONV + 3 * c + n + 1] for n in range(3)]
                chain(dve.tensor_scalar(TMP[:, 0, :], z[:, 0:S], w[0], None, ALU.mult))
                chain(dve.scalar_tensor_tensor(TMP[:, 1, :], z[:, 1:S + 1], w[1], TMP[:, 0, :], ALU.mult, ALU.add))
                chain(dve.scalar_tensor_tensor(TMP[:, 0, :], z[:, 2:S + 2], w[2], TMP[:, 1, :], ALU.mult, ALU.add))
                dve.wait_ge(unit_done, u0 + 3 * c + 3)
                dve.tensor_tensor(W[:, c, :], TMP[:, 0, :], PS[:, (3 * c + 2) % 4, :], ALU.mult).then_inc(taken, 1)
                dve.wait_ge(taken, T_CONV + c + 1)
            for j in (18, 19):
                dve.wait_ge(unit_done, u0 + j + 1)
                dve.tensor_scalar(W[:, j - 12, :], PS[:, j % 4, :], QSCALE, None, ALU.mult).then_inc(taken, 1)
            attention("mixA")
            low_o("outA")
            add_y("outA", True)
            normed("ffnA", "ffnA", lambda k: X[:, k, :])
            gate_up(2)
            down(2)
            add_y("down2", False)
            normed("kv", "kv", lambda k: X[:, k, :])
            u0 = U0["kv"]
            for j in range(12):
                dve.wait_ge(unit_done, u0 + j + 1)
                if j < 6:
                    dve.tensor_copy(W[:, 8 + j, :], PS[:, j % 4, :]).then_inc(taken, 1)
                else:
                    dve.tensor_copy(V_SB[:, :, (j - 6) * P:(j - 5) * P],
                                    PS[:, j % 4, :].rearrange("p (t c) -> p t c", t=NT)).then_inc(taken, 1)
            normed("projB", "mixB", lambda k: X[:, k, :], rstd="kv")
            u0 = U0["projB"]
            for j in range(8):
                dve.wait_ge(unit_done, u0 + j + 1)
                dve.tensor_scalar(W[:, j, :], PS[:, j % 4, :], QSCALE, None, ALU.mult).then_inc(taken, 1)
            n = len(SBSTEPS)

            def sb_take(c):
                dve.wait_ge(sb_pv, 8 * (c + 1))
                dve.tensor_copy(W[:, c, :], PS[:, 6 + c % 2, :]).then_inc(sb_o, 1)

            def sb_clip_(t):
                w = S - SBSTEPS[t][1] * P
                dve.wait_ge(sb_qk, t + 1)
                if t >= 2:
                    dve.wait_ge(sb_l, t - 1)
                dve.tensor_scalar(PT[:, t % 2, 0:w], PS[:, t % 4, 0:w], SPW, None, ALU.min).then_inc(sb_clip, 1)

            def sb_soft(t):
                j = SBSTEPS[t][1]
                w = S - j * P
                dve.wait_ge(sb_ln, t + 1)
                if t >= 2:
                    dve.wait_ge(sb_tri, t - 1)
                    dve.wait_ge(sb_r, t - 1)
                lt, pt, ps = PB[:, t % 2, :], PT[:, t % 2, :], PS[:, t % 4, :]
                chain(dve.tensor_tensor(lt[:, 0:w], pt[:, 0:w], ps[:, 0:w], ALU.max))
                dve.tensor_tensor(lt[:, 0:P], lt[:, 0:P], CST[:, K_MASK:K_MASK + P], ALU.mult).then_inc(sb_l, 1)
                dve.wait_ge(sb_l, t + 1)
                if t >= 2:
                    dve.wait_ge(sb_tri, t)
                r, old = W[:, 20 + t % 2, :], W[:, 20 + (t - 1) % 2, :]
                if w > P:
                    dve.wait_ge(sb_r, t)
                    chain(dve.tensor_tensor(r[:, P:w], lt[:, P:w], old[:, 0:w - P], ALU.add))
                dve.tensor_copy(r[:, 0:P], lt[:, 0:P]).then_inc(sb_r, 1)

            for t in range(n + 6):
                if t < n:
                    sb_clip_(t)
                if 1 <= t <= n:
                    sb_soft(t - 1)
                d = t - 4
                if 0 <= d < n and d % 8 == 7:
                    sb_take(d // 8)
            attention("mixB")
            low_o("outB")
            add_y("outB", True)
            normed("ffnB", "ffnB", lambda k: X[:, k, :])
            gate_up(3)
            down(3)
            add_y("down3", False)
            dve.wait_ge(rstd_ready, NIDX["final"] + 1)
            for k in range(KC):
                dve.scalar_tensor_tensor(W[:, k, :], X[:, k, :], gain("final", k), RSTD[:, :],
                                         ALU.mult, ALU.mult).then_inc(out_ready, 1)


T0 = {"mem": 0, "ff1": 8, "proj1": 16, "sub": 24, "ff2": 28, "projA": 36, "ffnA": 44, "kv": 52,
      "projB": 60, "ffnB": 68}
T_CONV = 8 + 6
T_KV = T_CONV + 8
GROUP_OF = {}
for _part in ("mix1", "mixA", "mixB"):
    for _x in ATT[_part]:
        for _m in range(2 if _x["kind"] == "diff" else 1):
            GROUP_OF[_x["s"] + _m] = _x["g"]


def column_units(w):
    n = w.shape[1] // P
    return w.reshape(KC, P, n, P).transpose(2, 1, 0, 3)


def row_units(w):
    return w.reshape(w.shape[0] // P, P, KC, P)


def gate_up_units(g, u):
    return np.stack([column_units(g), column_units(u)], axis=1).reshape(2 * FC, P, KC, P)


def compress_units(w):
    return w.reshape(4, 4, P, 2, P).transpose(0, 2, 1, 3, 4).reshape(4, P, 8, P)


def per_feature(g):
    return g.reshape(-1, P).T


def make_constants():
    c = np.zeros((P, NCONST), np.float32)
    r = np.arange(P)
    c[:, K_ONE:K_ONE + P] = 1.0
    c[:, K_NEG:K_NEG + P] = -1.0
    c[:, K_TRI:K_TRI + P] = -(r[:, None] >= r[None, :]).astype(np.float32)
    c[:, K_ID:K_ID + P] = np.eye(P, dtype=np.float32)
    for b in (0, DH):
        for n in range(8):
            c[b + n + 8, K_PERM + b + n] = -1.0
            c[b + n, K_PERM + b + n + 8] = 1.0
    c[:, K_MASK:K_MASK + P] = (r[:, None] < r[None, :])
    pos = np.arange(S, dtype=np.float32)
    inv = np.float32(500000.0) ** (-np.arange(0, 16, 2, dtype=np.float32) / np.float32(16))
    ang = (pos[None, :] * inv[:, None]).astype(np.float32)
    c[:, K_COS:K_COS + S] = 1.0
    for b in (0, 8, DH, DH + 8):
        c[b:b + 8, K_COS:K_COS + S] = np.cos(ang)
        c[b:b + 8, K_SIN:K_SIN + S] = np.sin(ang)
    tok = r[:, None] + P * np.arange(NT)[None, :]
    c[:, K_ROW:K_ROW + 32] = np.repeat((tok >= 31), 8, axis=1)
    b = np.zeros((P, NCONSTB), np.float32)
    b[:, B_ID:B_ID + P] = np.eye(P)
    b[:, B_CAUSAL:B_CAUSAL + P] = np.where(r[None, :] <= r[:, None], 0.0, NEG)
    b[:, B_STRICT:B_STRICT + P] = np.where(r[:, None] < r[None, :], 0.0, NEG)
    end = 16 * np.arange(32) + 31
    for t in range(NT):
        b[:, B_CMP + 32 * t:B_CMP + 32 * t + 32] = np.where(end[None, :] <= (P * t + r)[:, None], 0.0, NEG)
    return c, b


def kernel(**inputs):
    import concourse.bacc as bacc
    from concourse.bass_utils import run_bass_kernel_spmd

    a = {k: np.asarray(v) for k, v in inputs.items()}
    w_in = a["w_in"][0]
    pair = np.concatenate([np.r_[DH * c:DH * (c + 1), DH * (c + 4):DH * (c + 5)] for c in range(4)])
    dq, dk, dv, nq = w_in[:, 0:512], w_in[:, 512:1024], w_in[:, 1024:1536], w_in[:, 1536:2048][:, pair]
    kc, vc, ks, vs, kw, vw = (w_in[:, 2048 + P * i:2048 + P * (i + 1)] for i in range(6))
    gl = np.concatenate([w_in[:, 2816:2840], np.zeros((D, P - 24), np.float32)], axis=1)
    proj1 = np.concatenate([dq, nq, dk, ks, kw, kc, vc, dv, vs, vw, gl], axis=1)
    w_out = a["w_out"][0]
    w_out = np.concatenate([w_out[0:512], w_out[512:1024][pair]], axis=0)
    ain = a["a_in_2"][0]
    gate_b, gate_c, conv_u, qm = (ain[:, 0:768], ain[:, 768:1536], ain[:, 1536:2304], ain[:, 2304:2560])
    proj_a = np.stack([gate_c.reshape(D, 6, P), conv_u.reshape(D, 6, P), gate_b.reshape(D, 6, P)],
                      axis=2).reshape(D, 18 * P)
    proj_a = np.concatenate([proj_a, qm], axis=1)
    parts = [column_units(a["w_mem_kv_2"][0]), column_units(a["w_mem_kv_2"][1]),
             gate_up_units(a["ff1_w_gate"][0], a["ff1_w_up"][0]), row_units(a["ff1_w_down"][0]),
             column_units(proj1), compress_units(a["cmp_k_w1"][0]), compress_units(a["cmp_v_w1"][0]),
             column_units(w_out),
             gate_up_units(a["ff2_w_gate"][0], a["ff2_w_up"][0]), row_units(a["ff2_w_down"][0]),
             column_units(proj_a), column_units(a["w_o_2"][0]),
             gate_up_units(a["w_gate_2"][0], a["w_up_2"][0]), row_units(a["w_down_2"][0]),
             column_units(a["w_kv_shared_2"]), column_units(a["b_in_2"][0]), column_units(a["w_o_2"][1]),
             gate_up_units(a["w_gate_2"][1], a["w_up_2"][1]), row_units(a["w_down_2"][1]),
             np.zeros((NLOAD - NUNITS, P, KC, P), np.float32)]
    stream = np.concatenate([p.reshape(-1, P, D) for p in parts], axis=0)
    stream = stream.reshape(NLOAD // 2, 2, P, D).transpose(0, 2, 1, 3).reshape(NLOAD // 2, P, 2 * D)

    def col(v):
        return np.concatenate([v, np.zeros(P - v.shape[0], np.float32)])[:, None]

    gains = {"mem": a["mem_norm_2"], "ff1_pre": a["ff1_norm_pre"][0], "ff1_post": a["ff1_norm_post"][0],
             "mix_pre": a["mix_norm_pre"][0], "mix_post": a["mix_norm_post"][0],
             "ff2_pre": a["ff2_norm_pre"][0], "ff2_post": a["ff2_norm_post"][0],
             "mixA": a["mix_norm_2"][0], "ffnA": a["ffn_norm_2"][0], "kv": a["kv_norm_2"],
             "mixB": a["mix_norm_2"][1], "ffnB": a["ffn_norm_2"][1], "final": a["final_norm_2"]}
    small = [per_feature(gains[g]) for g in GAINS] + [a["diff_subln"][0][:, None]]
    small += [col(a[n][0]) for n in ("lambda_q1", "lambda_q2", "lambda_k1", "lambda_k2")]
    small += [a[n][0].reshape(16, P).T for n in ("cmp_pe_k", "cmp_pe_v")]
    small += [a[n][0].reshape(2, P, DH).transpose(1, 0, 2).reshape(P, P) for n in ("cmp_k_w2", "cmp_v_w2")]
    small += [a["conv_w_2"][0].reshape(3, 6, P).transpose(2, 1, 0).reshape(P, 18)]
    small = np.concatenate(small, axis=1)
    consts, constsb = make_constants()
    arrays = {
        "xT": a["x"][0].T.reshape(KC, P, S).transpose(1, 0, 2).reshape(P, KC * S),
        "memT": a["mem_2"][0].T.reshape(KC, P, M).transpose(1, 0, 2).reshape(P, KC * M),
        "wstream": stream, "small": small, "consts": consts, "constsb": constsb,
    }
    arrays = {k: np.ascontiguousarray(v) for k, v in arrays.items()}
    nc = bacc.Bacc("TRN2", target_bir_lowering=False, num_devices=1)
    args = [nc.dram_tensor(k, v.shape, mybir.dt.from_np(v.dtype), kind="ExternalInput").ap()
            for k, v in arrays.items()]
    args.append(nc.dram_tensor("outT", (P, KC, S), mybir.dt.float32, kind="ExternalOutput").ap())
    program(nc, *args)
    r = run_bass_kernel_spmd(nc, [arrays], core_ids=[0])
    y = np.asarray(r.results[0]["outT"])
    return np.ascontiguousarray(y.transpose(2, 1, 0).reshape(1, S, D))
```

```python
from contextlib import ExitStack

import numpy as np

import concourse.bass as bass
from concourse import mybir

P = 128
S = 512
NT = S // P
D = 1024
KC = D // P
FF = 2816
FC = FF // P
M = 256
DH = 64
EPS = 1e-6
NEG = -1e30
SPW = 40.0
NCMP = 31
NG = 2
LAMBDA_INIT = 0.2
QSCALE = DH ** -0.5

RING = 4
LOADS = RING // 2

PARTS = [("mem", 8), ("gu0", 2 * FC), ("down0", FC),
         ("proj1", 31), ("out1", 8), ("gu1", 2 * FC), ("down1", FC),
         ("projA", 20), ("outA", 8), ("gu2", 2 * FC), ("down2", FC),
         ("kv", 12), ("projB", 8), ("outB", 8), ("gu3", 2 * FC), ("down3", FC)]
U0 = {}
_u = 0
for _name, _n in PARTS:
    U0[_name] = _u
    _u += _n
NUNITS = _u
NLOAD = -(-NUNITS // RING) * RING

GAINS = ["mem", "ff1_pre", "ff1_post", "mix_pre", "mix_post", "ff2_pre", "ff2_post",
         "mixA", "ffnA", "kv", "mixB", "ffnB", "final"]
GCOL = {g: KC * i for i, g in enumerate(GAINS)}
C_SUB = KC * len(GAINS)
C_LAM = C_SUB + 1
C_PE = C_LAM + 4
C_W2 = C_PE + 32
C_CONV = C_W2 + 256
NSMALL = C_CONV + 18

K_ONE, K_NEG, K_TRI, K_ID, K_PERM, K_MASK, K_COS, K_SIN, K_ROW = 0, 128, 256, 384, 512, 640, 768, 1280, 1792
NCONST = K_ROW + 32
B_ID, B_CAUSAL, B_STRICT, B_CMP = 0, 128, 256, 384
NCONSTB = B_CMP + NT * 32

NORMS = [("mem", KC), ("ff1_pre", KC), ("ff1_post", KC), ("mix_pre", KC),
         ("sub0", 1), ("sub1", 1), ("sub2", 1), ("sub3", 1), ("mix_post", KC), ("ff2_pre", KC),
         ("ff2_post", KC), ("mixA", KC), ("ffnA", KC), ("kv", KC), ("ffnB", KC), ("final", KC)]
NIDX, SQ0, ADD0 = {}, {}, {}
_q = _a = 0
for _i, (_name, _n) in enumerate(NORMS):
    NIDX[_name], SQ0[_name], ADD0[_name] = _i, _q, _a
    _q += _n
    _a += _n - 1

PROJ = {
    "mem": [(k, 2 * l + j) for l in range(2) for k in ("mk", "mv") for j in range(2)],
    "proj1": ([("kc", 0), ("vc", 0)] + [("dv", j) for j in range(4)] + [("vs", 0), ("vw", 0), ("gl", 0)]
              + [x for j in range(4) for x in (("dk", j), ("w1k", j))] + [("ks", 0), ("kw", 0), ("dq", 0), ("dq", 1), ("w1v", 0), ("dq", 2), ("w1v", 1), ("dq", 3), ("w1v", 2),
                 ("nq", 0), ("w1v", 3), ("nq", 1), ("nq", 2), ("nq", 3)]),
    "projA": [x for c in range(6) for x in (("cg", c), ("cu", c), ("cb", c))] + [("qa", 0), ("qa", 1)],
    "kv": [("sk", j) for j in range(6)] + [("sv", j) for j in range(6)],
    "projB": [("qb", j) for j in range(8)],
}
TURNED = ("mv", "dv", "vs", "vw", "gl", "sv")
ROTARY = ("dk", "ks", "kw", "dq", "nq")
JOBS = {}
_t = _f = _tf = _rf = 0
for _part, _units in PROJ.items():
    JOBS[_part] = []
    _n = 0
    for _u, (_kind, _j) in enumerate(_units):
        _x = dict(kind=_kind, j=_j, u=U0[_part] + _u)
        if not _kind.startswith("w1"):
            _x.update(n=_n, t=_t)
            _n += 1
            _t += 1
        if _kind in TURNED:
            _tf += 1
            _x.update(f=_f, c=_tf)
            _f += 1
        elif _kind in ROTARY:
            _rf += 1
            _x.update(f=_f, c=_rf)
            _f += 1
        JOBS[_part].append(_x)
TAKEN = {p: max(x["t"] for x in v if "t" in x) + 1 for p, v in JOBS.items()}
FLIPS = {x["f"]: x for v in JOBS.values() for x in v if "f" in x}

XN = {n: i for i, n in enumerate(
    ["mem", "ff1", "proj1", "out1", "ff2", "projA", "outA", "ffnA", "kv", "projB", "outB", "ffnB"])}
XU = {n: i for i, n in enumerate(["ff1", "mix1", "ff2", "mixA", "ffnA", "mixB", "ffnB"])}


def attention_groups(part):
    out = []
    if part == "mix1":
        for c in range(4):
            for i in range(NT):
                out.append(dict(kind="diff", chunk=c, half=0, tile=i, blocks=i + 1,
                                first=True, last=True, end=i == NT - 1))
        for c in range(4, 8):
            for g in range(NG):
                for i in range(NT):
                    for b, kind in enumerate(("cmp", "sel", "win")):
                        out.append(dict(kind=kind, chunk=c, half=g, tile=i,
                                        blocks=1 if kind == "cmp" else i + 1, first=b == 0, last=b == 2,
                                        gate=3 * (c - 4 + 4 * g) + b,
                                        end=b == 2 and g == 1 and i == NT - 1))
    else:
        for c in range(6, 8):
            for g in range(2):
                for i in range(NT):
                    out.append(dict(kind="mem", chunk=c, half=g, tile=i, blocks=M // P, first=True,
                                    last=True, end=g == 1 and i == NT - 1))
    return out


def number_groups():
    plans, s, g, o = {}, 0, 0, 0
    for part in ("mix1", "mixA", "mixB"):
        plans[part] = attention_groups(part)
        for x in plans[part]:
            x["g"], x["s"], x["o"] = g, s, o
            s += 2 if x["kind"] == "diff" else 1
            g += 1
            if x["end"]:
                o += 1
    return plans, s


ATT, NSTEP = number_groups()
NPB = 4
SUB_AT, SUB_EVERY = 22, 5
CHUNK_AT = {46: 4, 70: 5, 94: 6}
LAG_T, LAG_V = 2, 3


def program(nc, xT, memT, wstream, small, consts, constsb, out):
    F, R, BF = mybir.dt.float32, mybir.dt.float32r, mybir.dt.bfloat16
    ALU, ACT, AX = mybir.AluOpType, mybir.ActivationFunctionType, mybir.AxisListType

    ctx = ExitStack()
    with ctx:
        def sb(name, shape, dt=F):
            return ctx.enter_context(nc.sbuf_tensor(name, shape, dt))

        def sem(name):
            return ctx.enter_context(nc.semaphore(name))

        X = sb("X", [P, KC, S])
        XH = sb("XH", [P, KC, S], R)
        XL = sb("XL", [P, KC, S], R)
        W = sb("WORK", [P, FC, S])
        RAW = sb("RAW", [P, RING, D])
        WH = sb("WH", [P, RING, KC, P], R)
        WL = sb("WL", [P, RING, KC, P], R)
        HH = sb("HH", [P, 2, S], R)
        HL = sb("HL", [P, 2, S], R)
        RSTD = sb("RSTD", [P, S])
        LNV = sb("LNV", [P, S])
        SQ = sb("SQ", [P, 2, S])
        TMP = sb("TMP", [P, 2, S])
        Y0 = sb("Y0", [P, S])
        ACC = sb("ACC", [P, S])
        PB = sb("PB", [P, NPB, S])
        PT = sb("PT", [P, 2, S])
        CST = sb("CST", [P, NCONST])
        CSB = sb("CSB", [P, NCONSTB], BF)
        SM = sb("SM", [P, NSMALL])
        MK = sb("MK", [P, 2, 2, M])
        MV = sb("MV", [P, 2, 2, M])
        NMAX = sb("NMAX", [P, NSTEP])
        RSUM = sb("RSUM", [P, NSTEP])
        REC = sb("REC", [P, NSTEP])
        GATE = sb("GATE", [P, NT, 24])
        LAM = sb("LAM", [P, 8])
        HID = sb("HID", [P, 2, 2, 2 * NCMP])
        KCT = sb("KCT", [P, 32])
        VC = sb("VC", [32, P])
        EPSB = sb("EPSB", [P, 1])
        PS = ctx.enter_context(nc.psum_tensor("PS", [P, 8, S], F))

        Q = W
        V_DIFF = W[:, 14:18, :]
        V_SEL = W[:, 18, :].rearrange("p (t c) -> p t c", t=NT)
        V_WIN = W[:, 19, :].rearrange("p (t c) -> p t c", t=NT)
        V_SB = W[:, 14:20, :].rearrange("p a b -> p (a b)").rearrange("p (t c) -> p t c", t=NT)
        RUN = [W[:, 20, :], W[:, 21, :], Y0[:, :], ACC[:, :]]
        Z = W[:, 16:20, :].rearrange("p a b -> p (a b)").rearrange("p (t c) -> p t c", t=2)[:, :, 0:S + 2]
        BH = HH[:, :, :].rearrange("p a b -> p (a b)")[:, 0:16 * 2 * NCMP].rearrange("p (l n) -> p l n", l=16)
        BL = HL[:, :, :].rearrange("p a b -> p (a b)")[:, 0:16 * 2 * NCMP].rearrange("p (l n) -> p l n", l=16)
        BT = PT[:, :, :].rearrange("p a b -> p (a b)")[:, 0:16 * 2 * NCMP]
        ONES, NEGS, TRI = CST[:, K_ONE:K_ONE + P], CST[:, K_NEG:K_NEG + P], CST[:, K_TRI:K_TRI + P]
        IDF, PERM = CST[:, K_ID:K_ID + P], CST[:, K_PERM:K_PERM + P]
        COS, SIN = CST[:, K_COS:K_COS + S], CST[:, K_SIN:K_SIN + S]
        CSB_IN = W[:, 8:10, :].rearrange("p a b -> p (a b)")[:, 0:NCONSTB]
        IDB = CSB[:, B_ID:B_ID + P]

        def gain(name, k):
            return SM[:, GCOL[name] + k:GCOL[name] + k + 1]

        consts_in, small_in = sem("consts_in"), sem("small_in")
        masks_ready = sem("masks_ready")
        x_in = sem("x_in")
        mem_in = sem("mem_in")
        loaded = [sem(f"loaded{i}") for i in range(LOADS)]
        hi_done = sem("hi_done")
        split_ready = sem("split_ready")
        unit_done = sem("unit_done")
        sq_ready = sem("sq_ready")
        sq_added = sem("sq_added")
        ssq_done = sem("ssq_done")
        ln_done = sem("ln_done")
        rstd_ready = sem("rstd_ready")
        sub_ready = sem("sub_ready")
        xh_ready = sem("xh_ready")
        xn_ready = sem("xn_ready")
        x_ready = sem("x_ready")
        g_scaled = sem("g_scaled")
        silu_done = sem("silu_done")
        gu_free = sem("gu_free")
        h_ready = sem("h_ready")
        hk_hi = sem("hk_hi")
        hk_ready = sem("hk_ready")
        y_done = sem("y_done")
        y0_done = sem("y0_done")
        y_scaled = sem("y_scaled")
        taken = sem("taken")
        flipped = sem("flipped")
        turned = sem("turned")
        roped = sem("roped")
        qk_done = sem("qk_done")
        nmax_ready = sem("nmax_ready")
        exp_done = sem("exp_done")
        p_ready = sem("p_ready")
        tr_done = sem("tr_done")
        pt_ready = sem("pt_ready")
        pv_done = sem("pv_done")
        o_taken = sem("o_taken")
        dve_chain = sem("dve_chain")
        lam_prod, lam_sum, lam_exp = sem("lam_prod"), sem("lam_sum"), sem("lam_exp")
        eps_set = sem("eps_set")
        stacked = sem("stacked")
        b_tmp, b_hi, b_ready = sem("b_tmp"), sem("b_hi"), sem("b_ready")
        hid_ready = sem("hid_ready")
        cmp_done = sem("cmp_done")
        cmp_taken = sem("cmp_taken")
        conv_done = sem("conv_done")
        sb_qk, sb_clip, sb_exp, sb_ln = sem("sb_qk"), sem("sb_clip"), sem("sb_exp"), sem("sb_ln")
        sb_l, sb_r, sb_tri, sb_a, sb_pv, sb_o = (sem("sb_l"), sem("sb_r"), sem("sb_tri"), sem("sb_a"),
                                                 sem("sb_pv"), sem("sb_o"))
        out_ready, stored = sem("out_ready"), sem("stored")

        SBSTEPS = [(h, j) for h in range(12) for j in range(NT - 1, -1, -1)]

        def y_wait(eng, part, k):
            if part.startswith("out"):
                eng.wait_ge(unit_done, U0[part] + k + 1)
            elif k < KC - 1:
                eng.wait_ge(y_done, (KC - 1) * int(part[-1]) + k + 1)
            else:
                eng.wait_ge(unit_done, U0[part] + FC)

        def flip_wait(eng, f):
            eng.wait_ge(turned if FLIPS[f]["kind"] in TURNED else roped, FLIPS[f]["c"])

        block = ctx.enter_context(nc.Block())

        @block.sync
        def _(sp):
            sp.dma_start(SM[:, :], small).then_inc(small_in, 16)
            sp.dma_start(W[:, 0:4, :].rearrange("p a b -> p (a b)"), memT).then_inc(mem_in, 16)
            for s in range(LOADS):
                sp.dma_start(RAW[:, 2 * s:2 * s + 2, :].rearrange("p a b -> p (a b)"),
                             wstream[s]).then_inc(loaded[s], 16)
            sp.dma_start(CST[:, :], consts).then_inc(consts_in, 16)
            sp.dma_start(CSB_IN, constsb).then_inc(consts_in, 16)
            sp.dma_start(X[:, :, :].rearrange("p a b -> p (a b)"), xT).then_inc(x_in, 16)
            with sp.Fori(1, NLOAD // RING) as i:
                for s in range(LOADS):
                    sp.wait_ge(split_ready, i * RING + (2 * s + 2 - RING))
                    sp.dma_start(RAW[:, 2 * s:2 * s + 2, :].rearrange("p a b -> p (a b)"),
                                 wstream[bass.ds(i * LOADS + s, 1)].rearrange("o p n -> (o p) n")
                                 ).then_inc(loaded[s], 16)
            for k in range(KC):
                sp.wait_ge(out_ready, k + 1)
                sp.dma_start(out[:, k, :], W[:, k, :]).then_inc(stored, 16)
            sp.wait_ge(stored, 16 * KC)

        @block.gpsimd
        def _(pool):
            with pool.Fori(0, NLOAD // RING) as i:
                for s in range(RING):
                    pool.wait_ge(hi_done, i * RING + (s + 1))
                    pool.tensor_tensor(WL[:, s, :, :].rearrange("p a b -> p (a b)"), RAW[:, s, :],
                                       WH[:, s, :, :].rearrange("p a b -> p (a b)").bitcast(F),
                                       ALU.subtract).then_inc(split_ready, 1)

        @block.scalar
        def _(act):
            def round_unit(v, i=None):
                if v >= NLOAD:
                    return
                n = 16 * (v // RING + 1)
                act.wait_ge(loaded[(v // 2) % LOADS], n if i is None else i * 16 + n)
                act.activation(WH[:, v % RING, :, :].rearrange("p a b -> p (a b)"), RAW[:, v % RING, :],
                               ACT.Copy).then_inc(hi_done, 1)

            def unit(u, i=None):
                act.wait_ge(unit_done, u + 1 if i is None else i * RING + (u + 1))

            def tables():
                act.preload_act_table_set("natural_log_exp_and_others")

            def round_x(src, gain_name, ready, cols=S):
                for k in range(KC):
                    ready(k)
                    act.activation(XH[:, k, 0:cols], src(k), ACT.Copy, scale=gain(gain_name, k)
                                   ).then_inc(xh_ready, 1)

            def squares(name, src, n, ready=None, cols=S):
                for k in range(n):
                    if ready:
                        ready(k)
                    if k >= 2:
                        act.wait_ge(sq_added, ADD0[name] + max(k - 2, 1))
                    act.activation(SQ[:, k % 2, 0:cols], src(k), ACT.Square).then_inc(sq_ready, 1)

            def rstd(name, n, bank, cols=S):
                act.wait_ge(ssq_done, NIDX[name] + 1)
                act.activation(LNV[:, 0:cols], PS[:, bank, 0:cols], ACT.Ln, bias=EPSB[:, 0:1],
                               scale=1.0 / (n * P)).then_inc(ln_done, 1)
                act.wait_ge(ln_done, NIDX[name] + 1)
                act.activation(RSTD[:, 0:cols], LNV[:, 0:cols], ACT.Exp, scale=-0.5).then_inc(rstd_ready, 1)

            def pre_norm(name, ready, cols=S):
                def x(k):
                    return X[:, k, :]

                round_x(x, name, ready)
                squares(name, x, KC)
                rstd(name, KC, 7)

            def post_norm(name, part):
                def ready(k):
                    act.wait_ge(y0_done, POSTS.index(part) + 1) if k == 0 else y_wait(act, part, k)

                squares(name, lambda k: PS[:, k, :] if k else Y0[:, :], KC, ready)
                rstd(name, KC, 0)

            def round_o(chunks, ready):
                for k in chunks:
                    ready(k)
                    act.activation(XH[:, k, :], W[:, k, :], ACT.Copy).then_inc(xh_ready, 1)

            def x_updated(stage):
                return lambda k: act.wait_ge(x_ready, KC * XU[stage] + k + 1)

            def gate_up(l):
                u0 = U0[f"gu{l}"]

                def step(f, slot, i=None):
                    u = u0 + 2 * f
                    unit(u, i)
                    round_unit(u + RING, i)
                    n = FC * l + f + 1
                    act.wait_ge(g_scaled, n if i is None else i * 2 + n)
                    if f >= 2:
                        act.wait_ge(h_ready, n - 2 if i is None else i * 2 + (n - 2))
                    act.activation(SQ[:, slot, :], TMP[:, slot, :], ACT.Silu).then_inc(silu_done, 1)
                    unit(u + 1, i)
                    round_unit(u + 1 + RING, i)

                step(0, 0)
                step(1, 1)
                with act.Fori(0, FC // 2 - 2) as i:
                    step(2, 0, i)
                    step(3, 1, i)
                for k in range(2):
                    act.wait_ge(h_ready, FC * l + k + 1)
                    act.activation(HH[:, k, :], W[:, k, :], ACT.Copy).then_inc(hk_hi, 1)
                step(FC - 2, 0)
                step(FC - 1, 1)

            def down(l):
                u0 = U0[f"down{l}"]
                act.wait_ge(h_ready, FC * (l + 1))
                turns = (FC - 2) // RING - 1
                with act.Fori(0, turns) as i:
                    for s in range(RING):
                        unit(u0 + s, i)
                        round_unit(u0 + s + RING, i)
                        act.activation(HH[:, s % 2, :],
                                       W[:, bass.ds(i * RING + (s + 2), 1), :].rearrange("p a b -> p (a b)"),
                                       ACT.Copy).then_inc(hk_hi, 1)
                for k in range(turns * RING, FC):
                    unit(u0 + k)
                    round_unit(u0 + k + RING)
                    if k + 2 < FC:
                        act.activation(HH[:, k % 2, :], W[:, k + 2, :], ACT.Copy).then_inc(hk_hi, 1)

            def refill(part, n, off=0):
                for u in range(U0[part] + off, U0[part] + off + n):
                    unit(u)
                    round_unit(u + RING)

            def attention(part):
                gs = ATT[part]
                for t in range(len(gs) + LAG_T + 1):
                    if t >= LAG_T + 1:
                        x = gs[t - LAG_T - 1]
                        g = x["g"]
                        act.wait_ge(tr_done, g + 1)
                        if g >= 2:
                            act.wait_ge(pv_done, g - 1)
                        kp = NCMP if x["kind"] == "cmp" else P
                        act.activation(PT[0:kp, g % 2, 0:x["blocks"] * P],
                                       PS[0:kp, 4 + g % 2, 0:x["blocks"] * P], ACT.Copy).then_inc(pt_ready, 1)
                    if t < len(gs):
                        x = gs[t]
                        for m in range(2 if x["kind"] == "diff" else 1):
                            s = x["s"] + m
                            n = NCMP if x["kind"] == "cmp" else x["blocks"] * P
                            act.wait_ge(nmax_ready, s + 1)
                            if s >= NPB:
                                act.wait_ge(tr_done, GROUP_OF[s - NPB] + 1)
                            act.activation(PB[:, s % NPB, 0:n], PS[:, s % 4, 0:n], ACT.Exp,
                                           bias=NMAX[:, s:s + 1],
                                           accum_out=RSUM[:, s:s + 1]).then_inc(exp_done, 1)
                    if part == "mix1":
                        finish_heads(t)

            def finish_heads(t):
                h, phase = divmod(t - SUB_AT, SUB_EVERY)
                if 0 <= h < 4:
                    if phase == 0:
                        act.wait_ge(o_taken, h + 1)
                        squares(f"sub{h}", lambda k: W[:, h, :], 1)
                    elif phase == 2:
                        rstd(f"sub{h}", 1, 7)
                    elif phase == 4:
                        act.wait_ge(sub_ready, h + 1)
                        act.activation(XH[:, h, :], W[:, h, :], ACT.Copy).then_inc(xh_ready, 1)
                if t in CHUNK_AT:
                    k = CHUNK_AT[t]
                    act.wait_ge(o_taken, k + 1)
                    act.activation(XH[:, k, :], W[:, k, :], ACT.Copy).then_inc(xh_ready, 1)

            def turn(x):
                act.wait_ge(flipped, x["f"] + 1)
                src = PS[:, 4 + x["f"] % 2, :].rearrange("p (t c) -> p t c", t=NT)
                j = x["j"]
                func = ACT.Copy
                if x["kind"] == "mv":
                    dst, src = MV[:, j // 2, :, (j % 2) * P:(j % 2 + 1) * P], src[:, 0:2, :]
                elif x["kind"] == "dv":
                    dst = V_DIFF[:, :, j * P:(j + 1) * P]
                elif x["kind"] == "vs":
                    dst = V_SEL
                elif x["kind"] == "vw":
                    dst = V_WIN
                elif x["kind"] == "sv":
                    dst = V_SB[:, :, j * P:(j + 1) * P]
                else:
                    dst, src, func = GATE[:, :, :], src[:, :, 0:24], ACT.Sigmoid
                act.activation(dst, src, func).then_inc(turned, 1)

            def round_b(kv):
                act.wait_ge(b_tmp, 16 * (kv + 1))
                act.activation(HH[:, :, :].rearrange("p a b -> p (a b)")[:, 0:32 * NCMP], BT,
                               ACT.Copy).then_inc(b_hi, 1)

            def gelu(kv):
                for hc in range(2):
                    act.activation(HID[:, kv, hc, :], PS[:, 6 + hc, 0:2 * NCMP],
                                   ACT.Gelu_apprx_tanh).then_inc(hid_ready, 1)

            def project(part):
                jobs = JOBS[part]
                for n, x in enumerate(jobs):
                    unit(x["u"])
                    round_unit(x["u"] + RING)
                    if n >= 2 and jobs[n - 2]["kind"] in TURNED:
                        turn(jobs[n - 2])
                    if x["kind"] == "vc":
                        act.wait_ge(taken, x["t"] + 1)
                        for kv in range(2):
                            for g in range(NG):
                                for par in range(2):
                                    act.dma_start(PB[par * DH:(par + 1) * DH, 2 * kv + g, 0:S - 1],
                                                  W[g * DH:(g + 1) * DH, 20 + kv, par:par + S - 1]
                                                  ).then_inc(stacked, 16)
                    if x["kind"] == "vs":
                        round_b(0)
                    if x["kind"] == "kw":
                        gelu(0)
                        round_b(1)
                    if x["kind"] == "w1v" and x["j"] == 3:
                        gelu(1)
                for x in jobs[-2:]:
                    if x["kind"] in TURNED:
                        turn(x)

            act.wait_ge(eps_set, 1)
            tables()

            def mem(k):
                return W[:, k // 2, (k % 2) * M:(k % 2 + 1) * M]

            act.wait_ge(small_in, 16)
            act.wait_ge(mem_in, 16)
            round_x(mem, "mem", lambda k: None, M)
            for v in range(RING):
                round_unit(v)
            squares("mem", mem, KC, cols=M)
            rstd("mem", KC, 7, M)
            act.wait_ge(lam_sum, 1)
            act.activation(LAM[:, 2:4], PS[:, 6, 0:2], ACT.Exp).then_inc(lam_exp, 1)
            project("mem")
            pre_norm("ff1_pre", lambda k: act.wait_ge(x_in, 16))
            gate_up(0)
            down(0)
            tables()
            post_norm("ff1_post", "down0")
            pre_norm("mix_pre", x_updated("ff1"))
            project("proj1")
            tables()
            act.wait_ge(cmp_done, 1)
            act.activation(KCT[:, 0:NCMP], PS[:, 6, 0:NCMP], ACT.Copy).then_inc(cmp_taken, 1)
            act.activation(VC[0:NCMP, :], PS[0:NCMP, 7, 0:P], ACT.Copy).then_inc(cmp_taken, 1)
            attention("mix1")
            act.wait_ge(o_taken, KC)
            act.activation(XH[:, KC - 1, :], W[:, KC - 1, :], ACT.Copy).then_inc(xh_ready, 1)
            refill("out1", 8)
            post_norm("mix_post", "out1")
            pre_norm("ff2_pre", x_updated("mix1"))
            gate_up(1)
            down(1)
            tables()
            post_norm("ff2_post", "down1")
            pre_norm("mixA", x_updated("ff2"))
            project("projA")
            round_o(range(6), lambda k: act.wait_ge(conv_done, k + 1))
            attention("mixA")
            round_o((6, 7), lambda k: act.wait_ge(o_taken, 8 + k - 5))
            refill("outA", 8)
            pre_norm("ffnA", x_updated("mixA"))
            gate_up(2)
            down(2)
            tables()
            pre_norm("kv", x_updated("ffnA"))
            project("kv")
            round_x(lambda k: X[:, k, :], "mixB", lambda k: None)
            project("projB")
            n = len(SBSTEPS)
            for t in range(n + 2):
                if t < n:
                    w = S - SBSTEPS[t][1] * P
                    act.wait_ge(sb_clip, t + 1)
                    act.activation(PT[:, t % 2, 0:w], PT[:, t % 2, 0:w], ACT.Exp).then_inc(sb_exp, 1)
                    act.wait_ge(sb_exp, t + 1)
                    act.activation(PT[:, t % 2, 0:w], PT[:, t % 2, 0:w], ACT.Ln, bias=1.0).then_inc(sb_ln, 1)
                if t >= 2:
                    a = t - 2
                    w = S - SBSTEPS[a][1] * P
                    act.wait_ge(sb_tri, a + 1)
                    if a >= 2:
                        act.wait_ge(sb_pv, a - 1)
                    act.activation(PB[:, 2 + a % 2, 0:w], PS[:, a % 4, 0:w], ACT.Exp).then_inc(sb_a, 1)
            round_o(range(5), lambda k: act.wait_ge(sb_o, k + 1))
            attention("mixB")
            round_o((5, 6, 7), lambda k: act.wait_ge(sb_o, k + 1) if k < 6 else
                    act.wait_ge(o_taken, 10 + k - 5))
            refill("outB", 8)
            pre_norm("ffnB", x_updated("mixB"))
            gate_up(3)
            down(3)
            tables()
            squares("final", lambda k: X[:, k, :], KC, x_updated("ffnB"))
            rstd("final", KC, 0)

        @block.tensor
        def _(pe):
            def three(o, wh, wl, xh, xl, start, stop):
                pe.matmul(o, wh, xh, start=start, stop=False)
                pe.matmul(o, wh, xl, start=False, stop=False)
                return pe.matmul(o, wl, xh, start=False, stop=stop)

            def have(u, i=None):
                pe.wait_ge(split_ready, u + 1 if i is None else i * RING + (u + 1))

            def features(u, bank, stage, cols=S, first=False, i=None):
                have(u, i)
                for k in range(KC):
                    if first:
                        pe.wait_ge(xn_ready, KC * XN[stage] + k + 1)
                    mm = three(PS[:, bank, 0:cols], WH[:, u % RING, k, :], WL[:, u % RING, k, :],
                               XH[:, k, 0:cols], XL[:, k, 0:cols], k == 0, k == KC - 1)
                mm.then_inc(unit_done, 1)

            def ssq(name, bank, cols=S):
                if name.startswith("sub"):
                    pe.wait_ge(sq_ready, SQ0[name] + 1)
                    src = SQ[:, 0, 0:cols]
                else:
                    pe.wait_ge(sq_added, ADD0[name] + KC - 1)
                    src = ACC[:, 0:cols]
                pe.matmul(PS[:, bank, 0:cols], ONES, src, start=True, stop=True).then_inc(ssq_done, 1)

            def gate_up(l, stage):
                u0 = U0[f"gu{l}"]
                features(u0, 0, stage, first=True)
                ssq(PRE[l], 7)
                for j in range(1, 4):
                    features(u0 + j, j, stage)
                with pe.Fori(0, FC // 2 - 1) as i:
                    for f in range(2):
                        pe.wait_ge(gu_free, i * 2 + (FC * l + f + 1))
                        for j in range(2):
                            features(u0 + 4 + 2 * f + j, 2 * f + j, stage, i=i)

            def down(l):
                u0 = U0[f"down{l}"]

                def step(k, order=range(KC), i=None):
                    u = u0 + k
                    have(u, i)
                    n = FC * l + k + 1
                    pe.wait_ge(hk_ready, n if i is None else i * RING + n)
                    for c in order:
                        if k == 0 and c == 0:
                            pe.wait_ge(gu_free, FC * (l + 1))
                        mm = three(PS[:, c, :], WH[:, u % RING, c, :], WL[:, u % RING, c, :],
                                   HH[:, k % 2, :], HL[:, k % 2, :], k == 0, k == FC - 1)
                        if k == FC - 1 and c < KC - 1:
                            mm.then_inc(y_done, 1)
                    mm.then_inc(unit_done, 1)

                step(0, (4, 5, 6, 7, 0, 1, 2, 3))
                step(1)
                with pe.Fori(0, (FC - 2) // RING - 1) as i:
                    for s in range(RING):
                        step(2 + s, i=i)
                for k in range(FC - RING, FC):
                    step(k)

            def flip(x):
                f = x["f"]
                pe.wait_ge(taken, x["t"] + 1)
                if f >= 2:
                    flip_wait(pe, f - 2)
                if x["kind"] in ROTARY:
                    mm = pe.matmul(PS[:, 4 + f % 2, :], PERM, SQ[:, f % 2, :], start=True, stop=True)
                else:
                    for t in range(2 if x["kind"] == "mv" else NT):
                        mm = pe.transpose(PS[:, 4 + f % 2, t * P:(t + 1) * P], SQ[:, f % 2, t * P:(t + 1) * P], IDF)
                mm.then_inc(flipped, 1)

            def compress(x):
                kv, t, u = int(x["kind"] == "w1v"), x["j"], x["u"]
                have(u)
                if t == 0:
                    pe.wait_ge(b_ready, kv + 1)
                    if kv:
                        pe.wait_ge(hid_ready, 2)
                    else:
                        pe.wait_ge(rstd_ready, NIDX["mix_pre"] + 1)
                for j in range(8):
                    l, hc = 4 * t + j // 2, j % 2
                    mm = three(PS[:, 6 + hc, 0:2 * NCMP], WH[:, u % RING, j, :], WL[:, u % RING, j, :],
                               BH[:, l, :], BL[:, l, :], l == 0, l == 15)
                mm.then_inc(unit_done, 1)

            def project(part, stage, norm=None, cols=S):
                jobs = JOBS[part]
                for i, x in enumerate(jobs):
                    if "n" not in x:
                        compress(x)
                    else:
                        if x["n"] >= 4:
                            pe.wait_ge(taken, x["t"] - 3)
                        elif part == "projB":
                            pe.wait_ge(taken, x["t"] - 3)
                        features(x["u"], x["t"] % 4 if part == "projB" else x["n"] % 4, stage, cols=cols,
                                 first=x["n"] == 0)
                    if i == 0 and norm:
                        if part == "mem":
                            pe.wait_ge(consts_in, 32)
                        ssq(norm, 7, cols)
                        if part == "mem":
                            pe.wait_ge(lam_prod, 1)
                            pe.matmul(PS[:, 6, 0:2], ONES, LAM[:, 0:2], start=True, stop=True).then_inc(lam_sum, 1)
                    if i >= 1 and "f" in jobs[i - 1]:
                        flip(jobs[i - 1])
                if "f" in jobs[-1]:
                    flip(jobs[-1])

            def scores(part, x):
                c, h, i = x["chunk"], x["half"], x["tile"]
                if part == "mix1" and x["s"] == 0:
                    pe.wait_ge(roped, 10)
                if part == "mix1" and c == 4:
                    pe.wait_ge(roped, 14)
                    pe.wait_ge(cmp_taken, 2)
                for m in range(2 if x["kind"] == "diff" else 1):
                    s = x["s"] + m
                    if s >= 4:
                        pe.wait_ge(exp_done, s - 3)
                    r = slice(DH * (m if x["kind"] == "diff" else h), DH * (m if x["kind"] == "diff" else h) + DH)
                    q = Q[r, c, i * P:(i + 1) * P]
                    n = x["blocks"] * P
                    if x["kind"] == "diff":
                        k = W[r, 8 + c, 0:n]
                    elif x["kind"] == "sel":
                        k = W[r, 12, 0:n]
                    elif x["kind"] == "win":
                        k = W[r, 13, 0:n]
                    elif x["kind"] == "cmp":
                        n = NCMP
                        k = KCT[r, 0:n]
                    else:
                        k = MK[r, 0 if part == "mixA" else 1, c - 6, :]
                    masked = x["kind"] != "mem"
                    mm = pe.matmul(PS[:, s % 4, 0:n], q, k, start=True, stop=not masked)
                    if x["kind"] == "cmp":
                        mm = pe.matmul(PS[:, s % 4, 0:n], IDB, CSB[:, B_CMP + 32 * i:B_CMP + 32 * i + n],
                                       start=False, stop=True)
                    elif masked:
                        mm = pe.matmul(PS[:, s % 4, n - P:n], IDB, CSB[:, B_CAUSAL:B_CAUSAL + P],
                                       start=False, stop=True)
                    mm.then_inc(qk_done, 1)

            def transposes(x):
                g = x["g"]
                pe.wait_ge(p_ready, g + 1)
                if g >= 2:
                    pe.wait_ge(pt_ready, g - 1)
                for b in range(x["blocks"]):
                    n = NCMP if x["kind"] == "cmp" else P
                    mm = pe.transpose(PS[0:n, 4 + g % 2, b * P:(b + 1) * P],
                                      PB[:, x["s"] % NPB, b * P:b * P + n], IDF)
                mm.then_inc(tr_done, 1)

            def values(part, x):
                g, c, h, i = x["g"], x["chunk"], x["half"], x["tile"]
                pe.wait_ge(pt_ready, g + 1)
                if x["first"] and h == 0 and i == 0 and x["o"] >= 2:
                    pe.wait_ge(o_taken, x["o"] - 1)
                if x["o"] == 5:
                    pe.wait_ge(ln_done, NIDX["sub3"] + 1)
                if x["o"] == 0:
                    pe.wait_ge(cmp_taken, 2)
                bank = 6 + x["o"] % 2
                for b in range(x["blocks"]):
                    if x["kind"] == "diff":
                        v, o = V_DIFF[:, b, c * P:(c + 1) * P], PS[:, bank, i * P:(i + 1) * P]
                    else:
                        o = PS[h * DH:(h + 1) * DH, bank, i * P:(i + 1) * P]
                        f = slice(h * DH, (h + 1) * DH)
                        if x["kind"] == "cmp":
                            v = VC[0:NCMP, f]
                        elif x["kind"] == "sel":
                            v = V_SEL[:, b, f]
                        elif x["kind"] == "win":
                            v = V_WIN[:, b, f]
                        else:
                            f = slice((c - 6) * P + h * DH, (c - 6) * P + (h + 1) * DH)
                            v = MV[:, 0 if part == "mixA" else 1, b, f]
                    kp = NCMP if x["kind"] == "cmp" else P
                    mm = pe.matmul(o, v, PT[0:kp, g % 2, b * P:(b + 1) * P],
                                   start=x["first"] and b == 0, stop=x["last"] and b == x["blocks"] - 1)
                mm.then_inc(pv_done, 1)

            def attention(part):
                gs = ATT[part]
                for t in range(len(gs) + LAG_V):
                    if t < len(gs):
                        scores(part, gs[t])
                    if 0 <= t - LAG_T < len(gs):
                        transposes(gs[t - LAG_T])
                    if t >= LAG_V:
                        values(part, gs[t - LAG_V])
                    if part == "mix1":
                        h, phase = divmod(t - SUB_AT, SUB_EVERY)
                        if 0 <= h < 4 and phase == 1:
                            pe.wait_ge(o_taken, 4)
                            if h:
                                pe.wait_ge(ln_done, NIDX["sub0"] + h)
                            ssq(f"sub{h}", 7)

            def output(part, stage, order=range(KC)):
                for j in range(KC):
                    u = U0[part] + j
                    have(u)
                    for n, k in enumerate(order):
                        if j == 0:
                            pe.wait_ge(xn_ready, KC * XN[stage] + n + 1)
                        mm = three(PS[:, j, :], WH[:, u % RING, k, :], WL[:, u % RING, k, :],
                                   XH[:, k, :], XL[:, k, :], n == 0, n == KC - 1)
                    mm.then_inc(unit_done, 1)

            project("mem", "mem", "mem", M)
            pe.wait_ge(taken, TAKEN["mem"])
            gate_up(0, "ff1")
            down(0)
            ssq("ff1_post", 0)
            project("proj1", "proj1", "mix_pre")
            w2 = SM[:, C_W2:C_W2 + 256].rearrange("p (v h d) -> p v h d", v=2, h=2)
            pe.wait_ge(hid_ready, 4)
            for g in range(NG):
                n = slice(g * NCMP, (g + 1) * NCMP)
                for hc in range(2):
                    pe.matmul(PS[g * DH:(g + 1) * DH, 6, 0:NCMP], w2[:, 0, hc, :], HID[:, 0, hc, n],
                              start=hc == 0, stop=hc == 1)
            for g in range(NG):
                n = slice(g * NCMP, (g + 1) * NCMP)
                for hc in range(2):
                    mm = pe.matmul(PS[0:NCMP, 7, g * DH:(g + 1) * DH], HID[:, 1, hc, n], w2[:, 1, hc, :],
                                   start=hc == 0, stop=hc == 1)
            mm.then_inc(cmp_done, 1)
            pe.wait_ge(turned, FLIPS[JOBS["proj1"][8]["f"]]["c"])
            pe.wait_ge(masks_ready, 1)
            attention("mix1")
            output("out1", "out1")
            ssq("mix_post", 0)
            gate_up(1, "ff2")
            down(1)
            ssq("ff2_post", 0)
            project("projA", "projA", "mixA")
            pe.wait_ge(taken, TAKEN["projA"])
            attention("mixA")
            output("outA", "outA")
            gate_up(2, "ffnA")
            down(2)
            project("kv", "kv", "kv")
            project("projB", "projB")
            pe.wait_ge(taken, TAKEN["projB"])
            pe.wait_ge(turned, FLIPS[max(FLIPS)]["c"])
            n = len(SBSTEPS)

            def sb_scores(t):
                h, j = SBSTEPS[t]
                if t >= 4:
                    pe.wait_ge(sb_a, t - 3)
                r = slice(DH * (h % 2), DH * (h % 2) + DH)
                pe.matmul(PS[:, t % 4, 0:S - j * P], W[r, 8 + h // 2, j * P:(j + 1) * P],
                          Q[r, h // 2, j * P:S], start=True, stop=True).then_inc(sb_qk, 1)

            def sb_tail(t):
                h, j = SBSTEPS[t]
                w = S - j * P
                pe.wait_ge(sb_l, t + 1)
                pe.matmul(PS[:, t % 4, 0:w], TRI, PB[:, t % 2, 0:w], start=False, stop=False,
                          skip_group_check=True)
                if j < NT - 1:
                    pe.wait_ge(sb_r, t)
                    pe.matmul(PS[:, t % 4, P:w], NEGS, RUN[(t - 1) % 4][:, 0:w - P], start=False,
                              stop=False, skip_group_check=True)
                pe.matmul(PS[:, t % 4, 0:P], IDB, CSB[:, B_STRICT:B_STRICT + P], start=False, stop=True,
                          skip_group_check=True).then_inc(sb_tri, 1)

            def sb_values(t):
                h, j = SBSTEPS[t]
                c = h // 2
                w = S - j * P
                pe.wait_ge(sb_a, t + 1)
                if h % 2 == 0 and j == NT - 1 and c >= 2:
                    pe.wait_ge(sb_o, c - 1)
                r = slice(DH * (h % 2), DH * (h % 2) + DH)
                pe.matmul(PS[r, 6 + c % 2, j * P:S], V_SB[:, j, h * DH:(h + 1) * DH], PB[:, 2 + t % 2, 0:w],
                          start=j == NT - 1, stop=j == 0, skip_group_check=True).then_inc(sb_pv, 1)

            for t in range(n + LAG_V):
                if t < n:
                    sb_scores(t)
                if 0 <= t - LAG_T < n:
                    sb_tail(t - LAG_T)
                if t >= LAG_V:
                    sb_values(t - LAG_V)
            pe.wait_ge(sb_o, 6)
            attention("mixB")
            output("outB", "outB")
            gate_up(3, "ffnB")
            down(3)
            ssq("final", 0)

        @block.vector
        def _(dve):
            chained = [0]

            def chain(ins):
                chained[0] += 1
                ins.then_inc(dve_chain, 1)
                dve.wait_ge(dve_chain, chained[0])

            def low(stage, name, k, src, cols=S):
                dve.wait_ge(xh_ready, KC * XN[stage] + k + 1)
                dve.scalar_tensor_tensor(XL[:, k, 0:cols], src, gain(name, k), XH[:, k, 0:cols].bitcast(F),
                                         ALU.mult, ALU.subtract).then_inc(xn_ready, 1)

            def add_squares(name, cols=S):
                for k in range(1, KC):
                    dve.wait_ge(sq_ready, SQ0[name] + k + 1)
                    if k >= 2:
                        dve.wait_ge(sq_added, ADD0[name] + k - 1)
                    dve.tensor_tensor(ACC[:, 0:cols], SQ[:, 0, 0:cols] if k == 1 else ACC[:, 0:cols],
                                      SQ[:, k % 2, 0:cols], ALU.add).then_inc(sq_added, 1)

            def low_o(stage, chunks):
                for k in chunks:
                    dve.wait_ge(xh_ready, KC * XN[stage] + k + 1)
                    dve.tensor_tensor(XL[:, k, :], W[:, k, :], XH[:, k, :].bitcast(F),
                                      ALU.subtract).then_inc(xn_ready, 1)

            def gate_up(l):
                u0 = U0[f"gu{l}"]
                dve.wait_ge(rstd_ready, NIDX[PRE[l]] + 1)

                def step(f, i=None):
                    n, u = FC * l + f + 1, u0 + 2 * f + 1
                    n, u = (n, u) if i is None else (i * 2 + n, i * RING + u)
                    s = f % 2
                    h = W[:, f, :] if i is None else W[:, bass.ds(i * 2 + f, 1), :].rearrange("p a b -> p (a b)")
                    dve.wait_ge(unit_done, u)
                    dve.tensor_tensor(TMP[:, s, :], RSTD[:, :], PS[:, 2 * s, :], ALU.mult).then_inc(g_scaled, 1)
                    dve.wait_ge(unit_done, u + 1)
                    dve.tensor_tensor(Y0[:, :], RSTD[:, :], PS[:, 2 * s + 1, :], ALU.mult).then_inc(gu_free, 1)
                    dve.wait_ge(gu_free, n)
                    dve.wait_ge(silu_done, n)
                    dve.tensor_tensor(h, SQ[:, s, :], Y0[:, :], ALU.mult).then_inc(h_ready, 1)
                    dve.wait_ge(h_ready, n)

                with dve.Fori(0, FC // 2 - 1) as i:
                    step(0, i)
                    step(1, i)
                for k in range(2):
                    dve.wait_ge(hk_hi, FC * l + k + 1)
                    dve.tensor_tensor(HL[:, k, :], W[:, k, :], HH[:, k, :].bitcast(F),
                                      ALU.subtract).then_inc(hk_ready, 1)
                step(FC - 2)
                step(FC - 1)

            def down(l):
                with dve.Fori(0, FC // 2 - 1) as i:
                    for s in range(2):
                        dve.wait_ge(hk_hi, i * 2 + (FC * l + s + 3))
                        dve.tensor_tensor(HL[:, s, :],
                                          W[:, bass.ds(i * 2 + (s + 2), 1), :].rearrange("p a b -> p (a b)"),
                                          HH[:, s, :].bitcast(F), ALU.subtract).then_inc(hk_ready, 1)

            def post(name, part, weight, update, stage, nxt):
                y_wait(dve, part, 0)
                dve.tensor_copy(Y0[:, :], PS[:, 0, :]).then_inc(y0_done, 1)
                add_squares(name)
                dve.wait_ge(rstd_ready, NIDX[name] + 1)
                y0 = KC * POSTS.index(part)
                x0 = KC * XU[update]

                def scaled(k):
                    if k >= 2:
                        dve.wait_ge(x_ready, x0 + k - 1)
                    dve.scalar_tensor_tensor(TMP[:, k % 2, :], PS[:, k, :] if k else Y0[:, :], gain(name, k),
                                             RSTD[:, :], ALU.mult, ALU.mult).then_inc(y_scaled, 1)

                scaled(0)
                for k in range(KC + 1):
                    if k + 1 < KC:
                        scaled(k + 1)
                    if k < KC:
                        dve.wait_ge(y_scaled, y0 + k + 1)
                        dve.scalar_tensor_tensor(X[:, k, :], TMP[:, k % 2, :], weight, X[:, k, :],
                                                 ALU.mult, ALU.add).then_inc(x_ready, 1)
                    if k >= 1:
                        low(stage, nxt, k - 1, X[:, k - 1, :])
                add_squares(nxt)

            def add_y(part, stage, nxt):
                for k in range(KC + 1):
                    if k < KC:
                        y_wait(dve, part, k)
                        dve.tensor_tensor(X[:, k, :], X[:, k, :], PS[:, k, :], ALU.add).then_inc(x_ready, 1)
                    if k >= 1 and stage:
                        low(stage, nxt, k - 1, X[:, k - 1, :])
                add_squares(nxt)

            def rope(x):
                f = x["f"]
                dst = W[:, {"dq": 0, "nq": 4, "dk": 8, "ks": 12, "kw": 13}[x["kind"]] + x["j"], :]
                if x["c"] >= 2:
                    dve.wait_ge(roped, x["c"] - 1)
                dve.tensor_tensor(TMP[:, 0, :], SQ[:, f % 2, :], COS, ALU.mult).then_inc(dve_chain, 1)
                chained[0] += 1
                dve.wait_ge(flipped, f + 1)
                chain(dve.tensor_tensor(TMP[:, 1, :], SIN, PS[:, 4 + f % 2, :], ALU.mult))
                dve.tensor_tensor(dst, TMP[:, 0, :], TMP[:, 1, :], ALU.add).then_inc(roped, 1)

            def build_b(kv):
                dve.wait_ge(stacked, 16 * 8)
                if kv:
                    dve.wait_ge(b_ready, 1)
                for l in range(16):
                    src = PB[:, 2 * kv:2 * kv + 2, 2 * l:2 * l + 16 * (NCMP - 1) + 1:16]
                    dve.tensor_scalar(BT[:, 2 * NCMP * l:2 * NCMP * (l + 1)].rearrange("p (g c) -> p g c", g=NG), src,
                                      SM[:, C_PE + 16 * kv + l:C_PE + 16 * kv + l + 1], None,
                                      ALU.add).then_inc(b_tmp, 1)

            def low_b(kv):
                dve.wait_ge(b_hi, kv + 1)
                dve.tensor_tensor(HL[:, :, :].rearrange("p a b -> p (a b)")[:, 0:32 * NCMP], BT,
                                  HH[:, :, :].rearrange("p a b -> p (a b)")[:, 0:32 * NCMP].bitcast(F),
                                  ALU.subtract).then_inc(b_ready, 1)

            def conv(x, bank):
                c, rs = x["j"], RSTD[:, :]
                z = Z[:, c % 2, :]
                w = [SM[:, C_CONV + 3 * c + n:C_CONV + 3 * c + n + 1] for n in range(3)]
                if x["kind"] == "cg":
                    dve.tensor_tensor(W[:, 12 + c % 2, :], rs, bank, ALU.mult).then_inc(taken, 1)
                elif x["kind"] == "cu":
                    dve.tensor_tensor(TMP[:, 0, :], rs, bank, ALU.mult).then_inc(taken, 1)
                    dve.wait_ge(taken, x["t"] + 1)
                    chain(dve.tensor_tensor(z[:, 2:S + 2], W[:, 12 + c % 2, :], TMP[:, 0, :], ALU.mult))
                    chain(dve.tensor_scalar(TMP[:, 0, :], z[:, 0:S], w[0], None, ALU.mult))
                    chain(dve.scalar_tensor_tensor(TMP[:, 1, :], z[:, 1:S + 1], w[1], TMP[:, 0, :],
                                                   ALU.mult, ALU.add))
                    chain(dve.scalar_tensor_tensor(TMP[:, 0, :], z[:, 2:S + 2], w[2], TMP[:, 1, :],
                                                   ALU.mult, ALU.add))
                else:
                    dve.tensor_tensor(TMP[:, 1, :], rs, bank, ALU.mult).then_inc(taken, 1)
                    dve.wait_ge(taken, x["t"] + 1)
                    dve.tensor_tensor(W[:, c, :], TMP[:, 0, :], TMP[:, 1, :], ALU.mult).then_inc(conv_done, 1)
                    dve.wait_ge(conv_done, c + 1)

            def project(part, norm, cols=S):
                dve.wait_ge(rstd_ready, NIDX[norm] + 1)
                jobs = JOBS[part]
                rs = RSTD[:, 0:cols]
                for i, x in enumerate(jobs + [dict(kind="end")]):
                    kind, j = x["kind"], x.get("j")
                    if "t" in x:
                        dve.wait_ge(unit_done, x["u"] + 1)
                        bank = PS[:, x["t"] % 4 if part == "projB" else x["n"] % 4, 0:cols]
                        if "f" in x and x["f"] >= 2:
                            if FLIPS[x["f"] - 2]["kind"] in ROTARY:
                                dve.wait_ge(roped, FLIPS[x["f"] - 2]["c"])
                            dve.wait_ge(flipped, x["f"] - 1)
                        if kind in ("cg", "cu", "cb"):
                            conv(x, bank)
                        elif kind in ("dq", "nq"):
                            dve.scalar_tensor_tensor(SQ[:, x["f"] % 2, :], bank, QSCALE, rs,
                                                     ALU.mult, ALU.mult).then_inc(taken, 1)
                        elif "f" in x:
                            dve.tensor_tensor(SQ[:, x["f"] % 2, 0:cols], rs, bank, ALU.mult).then_inc(taken, 1)
                        elif kind in ("qa", "qb"):
                            dve.scalar_tensor_tensor(W[:, j + (6 if kind == "qa" else 0), :], bank, QSCALE, rs,
                                                     ALU.mult, ALU.mult).then_inc(taken, 1)
                        else:
                            dst = {"mk": lambda: MK[:, j // 2, j % 2, :], "kc": lambda: W[:, 20, :],
                                   "vc": lambda: W[:, 21, :], "sk": lambda: W[:, 8 + j, :]}[kind]()
                            dve.tensor_tensor(dst, rs, bank, ALU.mult).then_inc(taken, 1)
                    prev = jobs[i - 1] if i else x
                    if prev["kind"] in ROTARY:
                        dve.wait_ge(taken, prev["t"] + 1)
                        rope(prev)
                    if kind == "dv" and j == 3:
                        build_b(0)
                    if kind == "vw":
                        low_b(0)
                    if kind == "kw":
                        dve.wait_ge(hid_ready, 2)
                        build_b(1)
                    if kind == "dq" and j == 0:
                        low_b(1)

            def attention(part):
                gs = ATT[part]

                def take(x):
                    dve.wait_ge(pv_done, x["g"] + 1)
                    dve.tensor_copy(W[:, x["chunk"], :], PS[:, 6 + x["o"] % 2, :]).then_inc(o_taken, 1)

                def scale(x):
                    s, i = x["s"], x["tile"]
                    n = NCMP if x["kind"] == "cmp" else x["blocks"] * P
                    p = PB[:, s % NPB, 0:n]
                    if x["kind"] == "diff":
                        dve.wait_ge(exp_done, s + 2)
                        chain(dve.reciprocal(REC[:, s:s + 2], RSUM[:, s:s + 2]))
                        chain(dve.tensor_scalar(REC[:, s + 1:s + 2], REC[:, s + 1:s + 2], LAM[:, 6:7], None,
                                                ALU.mult))
                        p1 = PB[:, (s + 1) % NPB, 0:n]
                        chain(dve.tensor_scalar(p1, p1, REC[:, s + 1:s + 2], None, ALU.mult))
                        dve.scalar_tensor_tensor(p, p, REC[:, s:s + 1], p1, ALU.mult,
                                                 ALU.add).then_inc(p_ready, 1)
                        return
                    dve.wait_ge(exp_done, s + 1)
                    chain(dve.reciprocal(REC[:, s:s + 1], RSUM[:, s:s + 1]))
                    if x["kind"] == "mem":
                        dve.tensor_scalar(p, p, REC[:, s:s + 1], None, ALU.mult).then_inc(p_ready, 1)
                    else:
                        dve.tensor_scalar(p, p, REC[:, s:s + 1], GATE[:, i, x["gate"]:x["gate"] + 1],
                                          ALU.mult, ALU.mult).then_inc(p_ready, 1)

                for t in range(len(gs) + LAG_V + 2):
                    if t < len(gs):
                        x = gs[t]
                        for m in range(2 if x["kind"] == "diff" else 1):
                            s = x["s"] + m
                            n = NCMP if x["kind"] == "cmp" else x["blocks"] * P
                            dve.wait_ge(qk_done, s + 1)
                            dve.tensor_reduce(NMAX[:, s:s + 1], PS[:, s % 4, 0:n], AX.X, ALU.max,
                                              negate=True).then_inc(nmax_ready, 1)
                    if 1 <= t <= len(gs):
                        scale(gs[t - 1])
                    if 0 <= t - LAG_V - 1 < len(gs) and gs[t - LAG_V - 1]["end"]:
                        take(gs[t - LAG_V - 1])
                    if part == "mix1":
                        finish_heads(t)

            def finish_heads(t):
                h, phase = divmod(t - SUB_AT, SUB_EVERY)
                if 0 <= h < 4 and phase == 3:
                    dve.wait_ge(rstd_ready, NIDX[f"sub{h}"] + 1)
                    chain(dve.scalar_tensor_tensor(W[:, h, :], W[:, h, :], SM[:, C_SUB:C_SUB + 1], RSTD[:, :],
                                                   ALU.mult, ALU.mult))
                    dve.tensor_scalar(W[:, h, :], W[:, h, :], 1.0 - LAMBDA_INIT, None,
                                      ALU.mult).then_inc(sub_ready, 1)
                if 1 <= h <= 4 and phase == 0:
                    low_o("out1", (h - 1,))
                if t - 1 in CHUNK_AT:
                    low_o("out1", (CHUNK_AT[t - 1],))

            dve.memset(EPSB[:, :], EPS).then_inc(eps_set, 1)
            dve.wait_ge(small_in, 16)
            dve.tensor_tensor(LAM[:, 0:2], SM[:, C_LAM:C_LAM + 2], SM[:, C_LAM + 2:C_LAM + 4],
                              ALU.mult).then_inc(lam_prod, 1)
            def mem(k):
                return W[:, k // 2, (k % 2) * M:(k % 2 + 1) * M]

            for k in range(KC):
                low("mem", "mem", k, mem(k), M)
            add_squares("mem", M)
            dve.wait_ge(consts_in, 32)
            dve.tensor_copy(CSB[:, :], CSB_IN).then_inc(masks_ready, 1)
            dve.wait_ge(masks_ready, 1)
            dve.wait_ge(lam_exp, 1)
            chain(dve.tensor_tensor(LAM[:, 4:5], LAM[:, 3:4], LAM[:, 2:3], ALU.subtract))
            chain(dve.tensor_scalar(LAM[:, 6:7], LAM[:, 4:5], LAMBDA_INIT, None, ALU.subtract))
            project("mem", "mem", M)
            for k in range(KC):
                low("ff1", "ff1_pre", k, X[:, k, :])
            add_squares("ff1_pre")
            gate_up(0)
            down(0)
            post("ff1_post", "down0", 0.5, "ff1", "proj1", "mix_pre")
            project("proj1", "mix_pre")
            dve.wait_ge(turned, FLIPS[JOBS["proj1"][8]["f"]]["c"])
            g0 = GATE[:, :, :].rearrange("p t (h b) -> p t h b", b=3)[:, :, :, 0]
            chain(dve.tensor_tensor(g0, g0, CST[:, K_ROW:K_ROW + 32].rearrange("p (t h) -> p t h", t=NT),
                                    ALU.mult))
            attention("mix1")
            low_o("out1", (KC - 1,))
            post("mix_post", "out1", 1.0, "mix1", "ff2", "ff2_pre")
            gate_up(1)
            down(1)
            post("ff2_post", "down1", 0.5, "ff2", "projA", "mixA")
            for s in range(2):
                chain(dve.memset(Z[:, s, 0:2], 0.0))
            project("projA", "mixA")
            low_o("outA", range(6))
            attention("mixA")
            low_o("outA", (6, 7))
            add_y("outA", "ffnA", "ffnA")
            gate_up(2)
            down(2)
            add_y("down2", "kv", "kv")
            project("kv", "kv")
            for k in range(KC):
                low("projB", "mixB", k, X[:, k, :])
            project("projB", "kv")
            n = len(SBSTEPS)

            def sb_take(c):
                dve.wait_ge(sb_pv, 8 * (c + 1))
                dve.tensor_copy(W[:, c, :], PS[:, 6 + c % 2, :]).then_inc(sb_o, 1)

            def sb_clip_(t):
                w = S - SBSTEPS[t][1] * P
                dve.wait_ge(sb_qk, t + 1)
                if t >= 2:
                    dve.wait_ge(sb_l, t - 1)
                dve.tensor_scalar(PT[:, t % 2, 0:w], PS[:, t % 4, 0:w], SPW, None, ALU.min).then_inc(sb_clip, 1)

            def sb_soft(t):
                j = SBSTEPS[t][1]
                w = S - j * P
                dve.wait_ge(sb_ln, t + 1)
                if t >= 2:
                    dve.wait_ge(sb_tri, t - 1)
                    dve.wait_ge(sb_r, t - 1)
                lt, pt, ps = PB[:, t % 2, :], PT[:, t % 2, :], PS[:, t % 4, :]
                chain(dve.tensor_tensor(lt[:, 0:w], pt[:, 0:w], ps[:, 0:w], ALU.max))
                dve.tensor_tensor(lt[:, 0:P], lt[:, 0:P], CST[:, K_MASK:K_MASK + P], ALU.mult).then_inc(sb_l, 1)
                dve.wait_ge(sb_l, t + 1)
                if t >= 4:
                    dve.wait_ge(sb_tri, t - 2)
                r, old = RUN[t % 4], RUN[(t - 1) % 4]
                if w > P:
                    dve.wait_ge(sb_r, t)
                    chain(dve.tensor_tensor(r[:, P:w], lt[:, P:w], old[:, 0:w - P], ALU.add))
                dve.tensor_copy(r[:, 0:P], lt[:, 0:P]).then_inc(sb_r, 1)

            for t in range(n + 6):
                if t < n:
                    sb_clip_(t)
                if 1 <= t <= n:
                    sb_soft(t - 1)
                d = t - 4
                if 0 <= d < n and d % 8 == 7:
                    sb_take(d // 8)
            low_o("outB", range(5))
            attention("mixB")
            low_o("outB", (5, 6, 7))
            add_y("outB", "ffnB", "ffnB")
            gate_up(3)
            down(3)
            add_y("down3", None, "final")
            dve.wait_ge(rstd_ready, NIDX["final"] + 1)
            for k in range(KC):
                dve.scalar_tensor_tensor(W[:, k, :], X[:, k, :], gain("final", k), RSTD[:, :],
                                         ALU.mult, ALU.mult).then_inc(out_ready, 1)


PRE = ["ff1_pre", "ff2_pre", "ffnA", "ffnB"]
POSTS = ["down0", "out1", "down1"]
GROUP_OF = {}
for _part in ("mix1", "mixA", "mixB"):
    for _x in ATT[_part]:
        for _m in range(2 if _x["kind"] == "diff" else 1):
            GROUP_OF[_x["s"] + _m] = _x["g"]


def column_units(w):
    n = w.shape[1] // P
    return w.reshape(KC, P, n, P).transpose(2, 1, 0, 3)


def row_units(w):
    return w.reshape(w.shape[0] // P, P, KC, P)


def gate_up_units(g, u):
    return np.stack([column_units(g), column_units(u)], axis=1).reshape(2 * FC, P, KC, P)


def compress_units(w):
    return w.reshape(4, 4, P, 2, P).transpose(0, 2, 1, 3, 4).reshape(4, P, 8, P)


def per_feature(g):
    return g.reshape(-1, P).T


def make_constants():
    c = np.zeros((P, NCONST), np.float32)
    r = np.arange(P)
    c[:, K_ONE:K_ONE + P] = 1.0
    c[:, K_NEG:K_NEG + P] = -1.0
    c[:, K_TRI:K_TRI + P] = -(r[:, None] >= r[None, :]).astype(np.float32)
    c[:, K_ID:K_ID + P] = np.eye(P, dtype=np.float32)
    for b in (0, DH):
        for n in range(8):
            c[b + n + 8, K_PERM + b + n] = -1.0
            c[b + n, K_PERM + b + n + 8] = 1.0
    c[:, K_MASK:K_MASK + P] = (r[:, None] < r[None, :])
    pos = np.arange(S, dtype=np.float32)
    inv = np.float32(500000.0) ** (-np.arange(0, 16, 2, dtype=np.float32) / np.float32(16))
    ang = (pos[None, :] * inv[:, None]).astype(np.float32)
    c[:, K_COS:K_COS + S] = 1.0
    for b in (0, 8, DH, DH + 8):
        c[b:b + 8, K_COS:K_COS + S] = np.cos(ang)
        c[b:b + 8, K_SIN:K_SIN + S] = np.sin(ang)
    tok = r[:, None] + P * np.arange(NT)[None, :]
    c[:, K_ROW:K_ROW + 32] = np.repeat((tok >= 31), 8, axis=1)
    b = np.zeros((P, NCONSTB), np.float32)
    b[:, B_ID:B_ID + P] = np.eye(P)
    b[:, B_CAUSAL:B_CAUSAL + P] = np.where(r[None, :] <= r[:, None], 0.0, NEG)
    b[:, B_STRICT:B_STRICT + P] = np.where(r[:, None] < r[None, :], 0.0, NEG)
    end = 16 * np.arange(32) + 31
    for t in range(NT):
        b[:, B_CMP + 32 * t:B_CMP + 32 * t + 32] = np.where(end[None, :] <= (P * t + r)[:, None], 0.0, NEG)
    return c, b


def kernel(**inputs):
    import concourse.bacc as bacc
    from concourse.bass_utils import run_bass_kernel_spmd

    a = {k: np.asarray(v) for k, v in inputs.items()}
    w_in = a["w_in"][0]
    pair = np.concatenate([np.r_[DH * c:DH * (c + 1), DH * (c + 4):DH * (c + 5)] for c in range(4)])
    dq, dk, dv, nq = w_in[:, 0:512], w_in[:, 512:1024], w_in[:, 1024:1536], w_in[:, 1536:2048][:, pair]
    kc, vc, ks, vs, kw, vw = (w_in[:, 2048 + P * i:2048 + P * (i + 1)] for i in range(6))
    gl = np.concatenate([w_in[:, 2816:2840], np.zeros((D, P - 24), np.float32)], axis=1)
    blocks = {"kc": kc, "vc": vc, "dv": dv, "vs": vs, "vw": vw, "gl": gl, "dk": dk, "ks": ks, "kw": kw,
              "dq": dq, "nq": nq}
    blocks = {k: column_units(v) for k, v in blocks.items()}
    blocks["w1k"], blocks["w1v"] = compress_units(a["cmp_k_w1"][0]), compress_units(a["cmp_v_w1"][0])
    proj1 = np.stack([blocks[k][j] for k, j in PROJ["proj1"]])
    w_out = a["w_out"][0]
    w_out = np.concatenate([w_out[0:512], w_out[512:1024][pair]], axis=0)
    ain = a["a_in_2"][0]
    gate_b, gate_c, conv_u, qm = (ain[:, 0:768], ain[:, 768:1536], ain[:, 1536:2304], ain[:, 2304:2560])
    proj_a = np.stack([gate_c.reshape(D, 6, P), conv_u.reshape(D, 6, P), gate_b.reshape(D, 6, P)],
                      axis=2).reshape(D, 18 * P)
    proj_a = np.concatenate([proj_a, qm], axis=1)
    parts = [column_units(a["w_mem_kv_2"][0]), column_units(a["w_mem_kv_2"][1]),
             gate_up_units(a["ff1_w_gate"][0], a["ff1_w_up"][0]), row_units(a["ff1_w_down"][0]),
             proj1, column_units(w_out),
             gate_up_units(a["ff2_w_gate"][0], a["ff2_w_up"][0]), row_units(a["ff2_w_down"][0]),
             column_units(proj_a), column_units(a["w_o_2"][0]),
             gate_up_units(a["w_gate_2"][0], a["w_up_2"][0]), row_units(a["w_down_2"][0]),
             column_units(a["w_kv_shared_2"]), column_units(a["b_in_2"][0]), column_units(a["w_o_2"][1]),
             gate_up_units(a["w_gate_2"][1], a["w_up_2"][1]), row_units(a["w_down_2"][1]),
             np.zeros((NLOAD - NUNITS, P, KC, P), np.float32)]
    stream = np.concatenate([p.reshape(-1, P, D) for p in parts], axis=0)
    stream = stream.reshape(NLOAD // 2, 2, P, D).transpose(0, 2, 1, 3).reshape(NLOAD // 2, P, 2 * D)

    def col(v):
        return np.concatenate([v, np.zeros(P - v.shape[0], np.float32)])[:, None]

    gains = {"mem": a["mem_norm_2"], "ff1_pre": a["ff1_norm_pre"][0], "ff1_post": a["ff1_norm_post"][0],
             "mix_pre": a["mix_norm_pre"][0], "mix_post": a["mix_norm_post"][0],
             "ff2_pre": a["ff2_norm_pre"][0], "ff2_post": a["ff2_norm_post"][0],
             "mixA": a["mix_norm_2"][0], "ffnA": a["ffn_norm_2"][0], "kv": a["kv_norm_2"],
             "mixB": a["mix_norm_2"][1], "ffnB": a["ffn_norm_2"][1], "final": a["final_norm_2"]}
    small = [per_feature(gains[g]) for g in GAINS] + [a["diff_subln"][0][:, None]]
    small += [col(a[n][0]) for n in ("lambda_q1", "lambda_q2", "lambda_k1", "lambda_k2")]
    small += [a[n][0].reshape(16, P).T for n in ("cmp_pe_k", "cmp_pe_v")]
    small += [a[n][0].reshape(2, P, DH).transpose(1, 0, 2).reshape(P, P) for n in ("cmp_k_w2", "cmp_v_w2")]
    small += [a["conv_w_2"][0].reshape(3, 6, P).transpose(2, 1, 0).reshape(P, 18)]
    small = np.concatenate(small, axis=1)
    consts, constsb = make_constants()
    arrays = {
        "xT": a["x"][0].T.reshape(KC, P, S).transpose(1, 0, 2).reshape(P, KC * S),
        "memT": a["mem_2"][0].T.reshape(KC, P, M).transpose(1, 0, 2).reshape(P, KC * M),
        "wstream": stream, "small": small, "consts": consts, "constsb": constsb,
    }
    arrays = {k: np.ascontiguousarray(v) for k, v in arrays.items()}
    nc = bacc.Bacc("TRN2", target_bir_lowering=False, num_devices=1)
    args = [nc.dram_tensor(k, v.shape, mybir.dt.from_np(v.dtype), kind="ExternalInput").ap()
            for k, v in arrays.items()]
    args.append(nc.dram_tensor("outT", (P, KC, S), mybir.dt.float32, kind="ExternalOutput").ap())
    program(nc, *args)
    r = run_bass_kernel_spmd(nc, [arrays], core_ids=[0])
    y = np.asarray(r.results[0]["outT"])
    return np.ascontiguousarray(y.transpose(2, 1, 0).reshape(1, S, D))
```

```python
from contextlib import ExitStack

import numpy as np

import concourse.bass as bass
from concourse import mybir

P = 128
S = 512
NT = S // P
D = 1024
KC = D // P
FF = 2816
FC = FF // P
M = 256
DH = 64
EPS = 1e-6
NEG = -1e30
SPW = 40.0
NCMP = 31
NG = 2
LAMBDA_INIT = 0.2
QSCALE = DH ** -0.5

RING = 4
LOADS = RING // 2

PARTS = [("mem", 8), ("gu0", 2 * FC), ("down0", FC),
         ("proj1", 31), ("out1", 8), ("gu1", 2 * FC), ("down1", FC),
         ("projA", 20), ("outA", 8), ("gu2", 2 * FC), ("down2", FC),
         ("kv", 12), ("projB", 8), ("outB", 8), ("gu3", 2 * FC), ("down3", FC)]
U0 = {}
_u = 0
for _name, _n in PARTS:
    U0[_name] = _u
    _u += _n
NUNITS = _u
NLOAD = -(-NUNITS // RING) * RING

GAINS = ["mem", "ff1_pre", "ff1_post", "mix_pre", "mix_post", "ff2_pre", "ff2_post",
         "mixA", "ffnA", "kv", "mixB", "ffnB", "final"]
GCOL = {g: KC * i for i, g in enumerate(GAINS)}
C_SUB = KC * len(GAINS)
C_LAM = C_SUB + 1
C_PE = C_LAM + 4
C_W2 = C_PE + 32
C_CONV = C_W2 + 256
NSMALL = C_CONV + 18

K_ONE, K_NEG, K_TRI, K_ID, K_PERM, K_MASK, K_COS, K_SIN, K_ROW = 0, 128, 256, 384, 512, 640, 768, 1280, 1792
NCONST = K_ROW + 32
B_ID, B_CAUSAL, B_STRICT, B_CMP = 0, 128, 256, 384
NCONSTB = B_CMP + NT * 32

NORMS = [("mem", KC), ("ff1_pre", KC), ("ff1_post", KC), ("mix_pre", KC),
         ("sub0", 1), ("sub1", 1), ("sub2", 1), ("sub3", 1), ("mix_post", KC), ("ff2_pre", KC),
         ("ff2_post", KC), ("mixA", KC), ("ffnA", KC), ("kv", KC), ("ffnB", KC), ("final", KC)]
NIDX, SQ0, ADD0 = {}, {}, {}
_q = _a = 0
for _i, (_name, _n) in enumerate(NORMS):
    NIDX[_name], SQ0[_name], ADD0[_name] = _i, _q, _a
    _q += _n
    _a += _n - 1

PROJ = {
    "mem": [(k, 2 * l + j) for l in range(2) for k in ("mk", "mv") for j in range(2)],
    "proj1": ([("kc", 0), ("vc", 0)] + [("dv", j) for j in range(4)] + [("vs", 0), ("vw", 0), ("gl", 0)]
              + [x for j in range(4) for x in (("dk", j), ("w1k", j))]
              + [("ks", 0), ("kw", 0), ("dq", 0), ("dq", 1), ("w1v", 0), ("dq", 2), ("w1v", 1),
                 ("dq", 3), ("w1v", 2), ("nq", 0), ("w1v", 3), ("nq", 1), ("nq", 2), ("nq", 3)]),
    "projA": [x for c in range(6) for x in (("cg", c), ("cu", c), ("cb", c))] + [("qa", 0), ("qa", 1)],
    "kv": [("sk", j) for j in range(6)] + [("sv", j) for j in range(6)],
    "projB": [("qb", j) for j in range(8)],
}
TURNED = ("mv", "dv", "vs", "vw", "gl", "sv")
ROTARY = ("dk", "ks", "kw", "dq", "nq")
JOBS = {}
_t = _f = _tf = _rf = 0
for _part, _units in PROJ.items():
    JOBS[_part] = []
    _n = 0
    for _u, (_kind, _j) in enumerate(_units):
        _x = dict(kind=_kind, j=_j, u=U0[_part] + _u)
        if not _kind.startswith("w1"):
            _x.update(n=_n, t=_t)
            _n += 1
            _t += 1
        if _kind in TURNED:
            _tf += 1
            _x.update(f=_f, c=_tf)
            _f += 1
        elif _kind in ROTARY:
            _rf += 1
            _x.update(f=_f, c=_rf)
            _f += 1
        JOBS[_part].append(_x)
TAKEN = {p: max(x["t"] for x in v if "t" in x) + 1 for p, v in JOBS.items()}
FLIPS = {x["f"]: x for v in JOBS.values() for x in v if "f" in x}

XN = {n: i for i, n in enumerate(
    ["mem", "ff1", "proj1", "out1", "ff2", "projA", "outA", "ffnA", "kv", "projB", "outB", "ffnB"])}
XU = {n: i for i, n in enumerate(["ff1", "mix1", "ff2", "mixA", "ffnA", "mixB", "ffnB"])}


BRANCH = {"cmp": 0, "sel": 1, "win": 2}
TILE_ORDER = (3, 0, 2, 1)
SHIFT = 1


def attention_quads(part):
    out = []
    if part == "mix1":
        for c in range(4):
            out.append(dict(kind="diff", half=0, blocks=NT, first=True, last=True, end=True,
                            members=[dict(chunk=c, tile=i, blocks=i + 1) for i in range(NT - 1, -1, -1)]))
        for i in TILE_ORDER:
            for g in range(NG):
                for b, kind in enumerate(("sel", "cmp", "win")):
                    nb = 1 if kind == "cmp" else i + 1
                    out.append(dict(kind=kind, half=g, blocks=nb, first=b == 0, last=b == 2,
                                    end=b == 2 and g == NG - 1,
                                    members=[dict(chunk=4 + r, tile=i, blocks=nb,
                                                  gate=3 * (r + 4 * g) + BRANCH[kind])
                                             for r in range(4)]))
    else:
        for c in range(6, 8):
            for h in range(2):
                out.append(dict(kind="mem", half=h, blocks=M // P, first=True, last=True, end=h == 1,
                                members=[dict(chunk=c, tile=i, blocks=M // P) for i in range(NT)]))
    return out


def items_after(qs, t, m):
    return [(x, b) for i, x in enumerate(qs) for b in range(x["blocks"])
            if 4 * (i + 1) + 4 * (b + 1) // x["blocks"] - 1 + SHIFT == 4 * t + m]


def number_quads():
    plans, s, q, e, o = {}, 0, 0, 0, 0
    for part in ("mix1", "mixA", "mixB"):
        plans[part] = attention_quads(part)
        for x in plans[part]:
            x["q"], x["e"], x["o"] = q, e, o
            for m, y in enumerate(x["members"]):
                y.update(kind=x["kind"], half=x["half"], p=4 * q + m, s=s, m=m,
                         n=NCMP if x["kind"] == "cmp" else y["blocks"] * P)
                s += 2 if x["kind"] == "diff" else 1
            q += 1
            e += x["blocks"]
            o += x["end"]
    return plans, s


ATT, NSTEP = number_quads()
QUADS = [x for part in ("mix1", "mixA", "mixB") for x in ATT[part]]
SUB_AT = 6
TILE_END = {t: n for n, t in enumerate(t for t, x in enumerate(ATT["mix1"]) if x["end"] and t >= 4)}
LAG_P = 1

LAG_C = 2
HID_TURN = [("kw", 0), ("nq", 2)]
POOL_X_AT = 2
EARLY = 6
SIDE = {"mem": 1, "ff1": 1, "proj1": 2, "ff2": 2, "projA": 2, "ffnA": 2, "kv": 2, "ffnB": 2}
SSQ_AT = {"mem": 2, "ff1": 2, "proj1": 3, "ff2": 3, "projA": 3, "ffnA": 3, "kv": 3, "ffnB": 3}
LAG_T = 4
LAG_V = 6
SBANKS = 6


def program(nc, xT, memT, wstream, small, consts, constsb, out):
    F, R, BF = mybir.dt.float32, mybir.dt.float32r, mybir.dt.bfloat16
    ALU, ACT, AX = mybir.AluOpType, mybir.ActivationFunctionType, mybir.AxisListType

    ctx = ExitStack()
    with ctx:
        def sb(name, shape, dt=F):
            return ctx.enter_context(nc.sbuf_tensor(name, shape, dt))

        def sem(name):
            return ctx.enter_context(nc.semaphore(name))

        X = sb("X", [P, KC, S])
        XH = sb("XH", [P, KC, S], R)
        XL = sb("XL", [P, KC, S], R)
        W = sb("WORK", [P, FC, S])
        RAW = sb("RAW", [P, RING, D])
        WH = sb("WH", [P, RING, KC, P], R)
        WL = sb("WL", [P, RING, KC, P], R)
        HH = sb("HH", [P, 2, S], R)
        HL = sb("HL", [P, 2, S], R)
        RSTD = sb("RSTD", [P, S])
        LNV = sb("LNV", [P, S])
        SQ = sb("SQ", [P, 2, S])
        TMP = sb("TMP", [P, 2, S])
        Y0 = sb("Y0", [P, S])
        SUMS = sb("SUMS", [P, 2, P], R)
        ACC = sb("ACC", [P, S])
        PB = sb("PB", [P, 4, S])
        PT = sb("PT", [P, 2, S])
        CST = sb("CST", [P, NCONST])
        CSB = sb("CSB", [P, NCONSTB], BF)
        SM = sb("SM", [P, NSMALL])
        MK = sb("MK", [P, 2, 2, M])
        MV = sb("MV", [P, 2, 2, M])
        NMAX = sb("NMAX", [P, NSTEP])
        RSUM = sb("RSUM", [P, NSTEP])
        REC = sb("REC", [P, NSTEP])
        GATE = sb("GATE", [P, NT, 24])
        LAM = sb("LAM", [P, 8])
        HID = sb("HID", [P, 2, 2, 2 * NCMP])
        KCT = sb("KCT", [P, 32])
        VC = sb("VC", [32, P])
        EPSB = sb("EPSB", [P, 1])
        PS = ctx.enter_context(nc.psum_tensor("PS", [P, 8, S], F))

        Q = W
        V_DIFF = W[:, 14:18, :]
        V_SEL = W[:, 18, :].rearrange("p (t c) -> p t c", t=NT)
        V_WIN = W[:, 19, :].rearrange("p (t c) -> p t c", t=NT)
        V_SB = W[:, 14:20, :].rearrange("p a b -> p (a b)").rearrange("p (t c) -> p t c", t=NT)
        ASLOT = [PB[:, 2, :], PB[:, 3, :], W[:, 20, :], W[:, 21, :]]
        ESLOT = [PT[:, 0, :], PT[:, 1, :], TMP[:, 0, :], TMP[:, 1, :]]
        PSLOT = [PB[:, m, :] for m in range(4)] + [W[:, 20, :], W[:, 21, :], Y0[:, :], ACC[:, :]]
        Z = W[:, 16:20, :].rearrange("p a b -> p (a b)").rearrange("p (t c) -> p t c", t=2)[:, :, 0:S + 2]
        BH = HH[:, :, :].rearrange("p a b -> p (a b)")[:, 0:16 * 2 * NCMP].rearrange("p (l n) -> p l n", l=16)
        BL = HL[:, :, :].rearrange("p a b -> p (a b)")[:, 0:16 * 2 * NCMP].rearrange("p (l n) -> p l n", l=16)
        BT = PT[:, :, :].rearrange("p a b -> p (a b)")[:, 0:16 * 2 * NCMP]
        ONES, NEGS, TRI = CST[:, K_ONE:K_ONE + P], CST[:, K_NEG:K_NEG + P], CST[:, K_TRI:K_TRI + P]
        IDF, PERM = CST[:, K_ID:K_ID + P], CST[:, K_PERM:K_PERM + P]
        COS, SIN = CST[:, K_COS:K_COS + S], CST[:, K_SIN:K_SIN + S]
        CSB_IN = W[:, 8:10, :].rearrange("p a b -> p (a b)")[:, 0:NCONSTB]
        IDB = CSB[:, B_ID:B_ID + P]

        def split_x(stage, k, cols=S):
            if stage == "mem":
                c, r = 4 + k // 2, slice((k % 2) * M, (k % 2 + 1) * M)
                return XH[:, c, r], XL[:, c, r]
            return XH[:, k, 0:cols], XL[:, k, 0:cols]

        def gain(name, k):
            return SM[:, GCOL[name] + k:GCOL[name] + k + 1]

        consts_in, small_in = sem("consts_in"), sem("small_in")
        masks_ready = sem("masks_ready")
        xh_used = sem("xh_used")
        x_in = sem("x_in")
        mem_in = sem("mem_in")
        first_in = sem("first_in")
        loaded = [sem(f"loaded{i}") for i in range(LOADS)]
        hi_done = sem("hi_done")
        split_ready = sem("split_ready")
        unit_done = sem("unit_done")
        sq_ready = sem("sq_ready")
        sq_added = sem("sq_added")
        ssq_done = sem("ssq_done")
        ln_done = sem("ln_done")
        rstd_ready = sem("rstd_ready")
        sub_ready = sem("sub_ready")
        xh_ready = sem("xh_ready")
        xn_ready = sem("xn_ready")
        x_ready = sem("x_ready")
        g_scaled = sem("g_scaled")
        silu_done = sem("silu_done")
        gu_free = sem("gu_free")
        h_ready = sem("h_ready")
        hk_hi = sem("hk_hi")
        hk_ready = sem("hk_ready")
        y_done = sem("y_done")
        y0_done = sem("y0_done")
        y_scaled = sem("y_scaled")
        taken = sem("taken")
        flipped = sem("flipped")
        turned = sem("turned")
        roped = sem("roped")
        qk_done = sem("qk_done")
        nmax_ready = sem("nmax_ready")
        exp_done = sem("exp_done")
        p_ready = sem("p_ready")
        tr_done = sem("tr_done")
        pt_ready = sem("pt_ready")
        pv_done = sem("pv_done")
        o_taken = sem("o_taken")
        dve_chain = sem("dve_chain")
        lam_prod, lam_sum, lam_exp = sem("lam_prod"), sem("lam_sum"), sem("lam_exp")
        eps_set = sem("eps_set")
        stacked = sem("stacked")
        b_tmp, b_hi, b_ready = sem("b_tmp"), sem("b_hi"), sem("b_ready")
        hid_raw = sem("hid_raw")
        hid_turned = sem("hid_turned")
        hid_ready = sem("hid_ready")
        cmp_done = sem("cmp_done")
        cmp_taken = sem("cmp_taken")
        conv_done = sem("conv_done")
        sb_qk, sb_clip, sb_exp, sb_ln = sem("sb_qk"), sem("sb_clip"), sem("sb_exp"), sem("sb_ln")
        sb_l, sb_hi, sb_lo = sem("sb_l"), sem("sb_hi"), sem("sb_lo")
        sb_tri, sb_a, sb_pv, sb_o = sem("sb_tri"), sem("sb_a"), sem("sb_pv"), sem("sb_o")
        sums_ready = sem("sums_ready")
        out_ready, stored = sem("out_ready"), sem("stored")

        SBSTEPS = [(h, j) for h in range(12) for j in range(NT - 1, -1, -1)]

        def y_wait(eng, part, k):
            if part.startswith("out"):
                eng.wait_ge(unit_done, U0[part] + k + 1)
            elif k < KC - 1:
                eng.wait_ge(y_done, (KC - 1) * int(part[-1]) + k + 1)
            else:
                eng.wait_ge(unit_done, U0[part] + FC)

        def flip_wait(eng, f):
            eng.wait_ge(turned if FLIPS[f]["kind"] in TURNED else roped, FLIPS[f]["c"])

        block = ctx.enter_context(nc.Block())

        @block.sync
        def _(sp):
            sp.dma_start(SM[:, :], small).then_inc(small_in, 16)
            sp.dma_start(RAW[:, 0, :], wstream[0][:, 0:D]).then_inc(first_in, 16)
            sp.dma_start(W[:, 0:4, :].rearrange("p a b -> p (a b)"), memT).then_inc(mem_in, 16)
            sp.dma_start(RAW[:, 1, :], wstream[0][:, D:2 * D]).then_inc(loaded[0], 16)
            for s in range(1, LOADS):
                sp.dma_start(RAW[:, 2 * s:2 * s + 2, :].rearrange("p a b -> p (a b)"),
                             wstream[s]).then_inc(loaded[s], 16)
            sp.dma_start(CST[:, :], consts).then_inc(consts_in, 16)
            sp.dma_start(CSB_IN, constsb).then_inc(consts_in, 16)
            sp.dma_start(X[:, :, :].rearrange("p a b -> p (a b)"), xT).then_inc(x_in, 16)
            with sp.Fori(1, NLOAD // RING) as i:
                for s in range(LOADS):
                    sp.wait_ge(split_ready, i * RING + (2 * s + 2 - RING))
                    sp.dma_start(RAW[:, 2 * s:2 * s + 2, :].rearrange("p a b -> p (a b)"),
                                 wstream[bass.ds(i * LOADS + s, 1)].rearrange("o p n -> (o p) n")
                                 ).then_inc(loaded[s], 16)
            for k in range(KC):
                sp.wait_ge(out_ready, k + 1)
                sp.dma_start(out[:, k, :], W[:, k, :]).then_inc(stored, 16)
            sp.wait_ge(stored, 16 * KC)

        @block.gpsimd
        def _(pool):
            def split_unit(v, i=None):
                s = v % RING
                pool.wait_ge(hi_done, v + 1 if i is None else i * RING + (v + 1))
                pool.tensor_tensor(WL[:, s, :, :].rearrange("p a b -> p (a b)"), RAW[:, s, :],
                                   WH[:, s, :, :].rearrange("p a b -> p (a b)").bitcast(F),
                                   ALU.subtract).then_inc(split_ready, 1)

            def split_units(a, b):
                v = a
                while v < b and v % RING:
                    split_unit(v)
                    v += 1
                turns = (b - v) // RING
                if turns:
                    with pool.Fori(0, turns) as i:
                        for s in range(RING):
                            split_unit(v + s, i)
                for v in range(v + turns * RING, b):
                    split_unit(v)

            def update_x(part):
                for k in range(KC):
                    pool.wait_ge(y_scaled, KC * POSTS.index(part) + k + 1)
                    pool.tensor_tensor(X[:, k, :], X[:, k, :], TMP[:, k % 2, :],
                                       ALU.add).then_inc(x_ready, 1)

            def low_softplus():
                for t, (h, j) in enumerate(SBSTEPS):
                    w = S - j * P
                    pool.wait_ge(sb_hi, t + 1)
                    pool.tensor_tensor(XL[:, t % 8, 0:w], PB[:, t % 2, 0:w], XH[:, t % 8, 0:w].bitcast(F),
                                       ALU.subtract).then_inc(sb_lo, 1)

            first = 0
            for part, after in (("down0", "proj1"), ("out1", "gu1"), ("down1", "projA")):
                split_units(first, U0[after] + POOL_X_AT)
                first = U0[after] + POOL_X_AT
                update_x(part)
            split_units(first, U0["outB"] + RING)
            low_softplus()
            split_units(U0["outB"] + RING, NLOAD)

        @block.scalar
        def _(act):
            def round_unit(v, i=None):
                if v >= NLOAD:
                    return
                n = 16 * (v // RING + 1)
                if v == 0:
                    act.wait_ge(first_in, 16)
                else:
                    act.wait_ge(loaded[(v // 2) % LOADS], n if i is None else i * 16 + n)
                act.activation(WH[:, v % RING, :, :].rearrange("p a b -> p (a b)"), RAW[:, v % RING, :],
                               ACT.Copy).then_inc(hi_done, 1)

            def unit(u, i=None):
                act.wait_ge(unit_done, u + 1 if i is None else i * RING + (u + 1))

            def tables():
                act.preload_act_table_set("natural_log_exp_and_others")

            def round_x(src, gain_name, ready, chunks=range(KC)):
                for k in chunks:
                    ready(k)
                    act.activation(split_x(gain_name, k)[0], src(k), ACT.Copy, scale=gain(gain_name, k)
                                   ).then_inc(xh_ready, 1)

            def squares(name, src, n, ready=None, cols=S):
                for k in range(n):
                    if ready:
                        ready(k)
                    if k >= 2:
                        act.wait_ge(sq_added, ADD0[name] + max(k - 2, 1))
                    act.activation(SQ[:, k % 2, 0:cols], src(k), ACT.Square).then_inc(sq_ready, 1)

            def rstd(name, n, bank, cols=S):
                act.wait_ge(ssq_done, NIDX[name] + 1)
                act.activation(LNV[:, 0:cols], PS[:, bank, 0:cols], ACT.Ln, bias=EPSB[:, 0:1],
                               scale=1.0 / (n * P)).then_inc(ln_done, 1)
                act.wait_ge(ln_done, NIDX[name] + 1)
                act.activation(RSTD[:, 0:cols], LNV[:, 0:cols], ACT.Exp, scale=-0.5).then_inc(rstd_ready, 1)

            def pre_norm(name, ready, before_last=None, chunks=range(KC)):
                def x(k):
                    return X[:, k, :]

                def wait(k):
                    if k == KC - 1 and before_last:
                        before_last()
                    ready(k)

                round_x(x, name, wait, chunks)
                squares(name, x, KC)
                rstd(name, KC, 7)

            def post_norm(name, part):
                def ready(k):
                    if part.startswith("out"):
                        refill(part, 1, k)
                    if k == 0:
                        act.wait_ge(y0_done, POSTS.index(part) + 1)
                    elif part.startswith("down"):
                        y_wait(act, part, k)

                squares(name, lambda k: PS[:, k, :] if k else Y0[:, :], KC, ready)
                rstd(name, KC, 0)
                if part.startswith("down"):
                    refill(part, 2, FC - 2)

            def round_o(chunks, ready):
                for k in chunks:
                    ready(k)
                    act.activation(XH[:, k, :], W[:, k, :], ACT.Copy).then_inc(xh_ready, 1)

            def x_updated(stage):
                return lambda k: act.wait_ge(x_ready, KC * XU[stage] + k + 1)

            def xh_left(part, stage):
                def ready(k):
                    if k < KC - 1:
                        act.wait_ge(xh_used, (KC - 1) * ("outA", "outB").index(part) + k + 1)
                    else:
                        refill(part, 1, KC - 1)
                    act.wait_ge(x_ready, KC * XU[stage] + k + 1)
                return ready

            def gate_up(l):
                u0 = U0[f"gu{l}"]

                def step(f, slot, i=None):
                    u = u0 + 2 * f
                    unit(u, i)
                    round_unit(u + RING, i)
                    n = FC * l + f + 1
                    act.wait_ge(g_scaled, n if i is None else i * 2 + n)
                    if f >= 2:
                        act.wait_ge(h_ready, n - 2 if i is None else i * 2 + (n - 2))
                    act.activation(SQ[:, slot, :], TMP[:, slot, :], ACT.Silu).then_inc(silu_done, 1)
                    unit(u + 1, i)
                    round_unit(u + 1 + RING, i)

                step(0, 0)
                step(1, 1)
                with act.Fori(0, FC // 2 - 2) as i:
                    step(2, 0, i)
                    step(3, 1, i)
                for k in range(2):
                    act.wait_ge(h_ready, FC * l + k + 1)
                    act.activation(HH[:, k, :], W[:, k, :], ACT.Copy).then_inc(hk_hi, 1)
                step(FC - 2, 0)
                step(FC - 1, 1)

            def down(l):
                u0 = U0[f"down{l}"]
                act.wait_ge(h_ready, FC * (l + 1))
                turns = (FC - 2) // RING - 1
                with act.Fori(0, turns) as i:
                    for s in range(RING):
                        unit(u0 + s, i)
                        round_unit(u0 + s + RING, i)
                        act.activation(HH[:, s % 2, :],
                                       W[:, bass.ds(i * RING + (s + 2), 1), :].rearrange("p a b -> p (a b)"),
                                       ACT.Copy).then_inc(hk_hi, 1)
                for k in range(turns * RING, FC - 2):
                    unit(u0 + k)
                    round_unit(u0 + k + RING)
                    if k + 2 < FC:
                        act.activation(HH[:, k % 2, :], W[:, k + 2, :], ACT.Copy).then_inc(hk_hi, 1)

            def refill(part, n, off=0):
                for u in range(U0[part] + off, U0[part] + off + n):
                    unit(u)
                    round_unit(u + RING)

            def attention(part):
                qs = ATT[part]

                def exps(y):
                    for j in range(2 if y["kind"] == "diff" else 1):
                        s, n, q = y["s"] + j, y["n"], y["p"] // 4
                        act.wait_ge(nmax_ready, s + 1)
                        if j:
                            dst = TMP[:, y["m"] % 2, 0:n]
                            if y["p"] >= 2:
                                act.wait_ge(p_ready, y["p"] - 1)
                        else:
                            dst = PSLOT[4 * (q % 2) + y["m"]][:, 0:n]
                            if q >= 2:
                                act.wait_ge(tr_done, QUADS[q - 2]["e"] + QUADS[q - 2]["blocks"])
                        act.activation(dst, PS[:, s % 4, 0:n], ACT.Exp, bias=NMAX[:, s:s + 1],
                                       accum_out=RSUM[:, s:s + 1]).then_inc(exp_done, 1)

                def store(x, b):
                    e = x["e"] + b
                    act.wait_ge(tr_done, e + 1)
                    if e >= 2:
                        act.wait_ge(pv_done, e - 1)
                    kp = NCMP if x["kind"] == "cmp" else P
                    c = b * P if x["kind"] == "diff" else 0
                    act.activation(PT[0:kp, e % 2, c:S], PS[0:kp, 4 + e % 2, c:S],
                                   ACT.Copy).then_inc(pt_ready, 1)

                for t in range(len(qs) + 2):
                    for m in range(4):
                        for x, b in items_after(qs, t, m):
                            store(x, b)
                        if t < len(qs):
                            exps(qs[t]["members"][m])
                    if part == "mix1" and t <= len(qs):
                        finish_heads(t)

            def split_tile(n):
                i = TILE_ORDER[n]
                act.wait_ge(o_taken, 4 + n + 1)
                act.activation(XH[:, 4:8, i * P:(i + 1) * P], W[:, 4:8, i * P:(i + 1) * P],
                               ACT.Copy).then_inc(xh_ready, 1)

            def finish_heads(t):
                h = t - SUB_AT
                if 0 <= h < 4:
                    act.wait_ge(o_taken, h + 1)
                    squares(f"sub{h}", lambda k: W[:, h, :], 1)
                if 0 <= h - 2 < 4:
                    act.wait_ge(sub_ready, h - 1)
                    act.activation(XH[:, h - 2, :], W[:, h - 2, :], ACT.Copy).then_inc(xh_ready, 1)
                if 0 <= h - 1 < 4:
                    rstd(f"sub{h - 1}", 1, 7)
                if t - 3 in TILE_END:
                    split_tile(TILE_END[t - 3])

            def turn(x):
                act.wait_ge(flipped, x["f"] + 1)
                src = PS[:, 4 + x["f"] % 2, :].rearrange("p (t c) -> p t c", t=NT)
                j = x["j"]
                func = ACT.Copy
                if x["kind"] == "mv":
                    dst, src = MV[:, j // 2, :, (j % 2) * P:(j % 2 + 1) * P], src[:, 0:2, :]
                elif x["kind"] == "dv":
                    dst = V_DIFF[:, :, j * P:(j + 1) * P]
                elif x["kind"] == "vs":
                    dst = V_SEL
                elif x["kind"] == "vw":
                    dst = V_WIN
                elif x["kind"] == "sv":
                    dst = V_SB[:, :, j * P:(j + 1) * P]
                else:
                    dst, src, func = GATE[:, :, :], src[:, :, 0:24], ACT.Sigmoid
                act.activation(dst, src, func).then_inc(turned, 1)

            def round_b(kv):
                act.wait_ge(b_tmp, 16 * (kv + 1))
                act.activation(HH[:, :, :].rearrange("p a b -> p (a b)")[:, 0:32 * NCMP], BT,
                               ACT.Copy).then_inc(b_hi, 1)

            def gelu(kv):
                act.wait_ge(hid_turned, kv + 1)
                src = PS[:, 7, 0:P].rearrange("p (h n) -> p h n", h=2)[:, :, 0:2 * NCMP]
                act.activation(HID[:, kv, :, :], src, ACT.Gelu_apprx_tanh).then_inc(hid_ready, 1)

            def raw_hidden():
                act.activation(Y0[0:2 * NCMP, 0:256], PS[0:2 * NCMP, 6, 0:256], ACT.Copy).then_inc(hid_raw, 1)

            def project(part):
                jobs = JOBS[part]
                for n, x in enumerate(jobs):
                    if part == "mem" and n == EARLY:
                        act.wait_ge(x_in, 16)
                        round_x(lambda k: X[:, k, :], "ff1_pre", lambda k: None, range(4))
                    unit(x["u"])
                    round_unit(x["u"] + RING)
                    if n >= 2 and jobs[n - 2]["kind"] in TURNED:
                        turn(jobs[n - 2])
                    if x["kind"] == "vc":
                        act.wait_ge(taken, x["t"] + 1)
                        for kv in range(2):
                            for g in range(NG):
                                for par in range(2):
                                    act.dma_start(PB[par * DH:(par + 1) * DH, 2 * kv + g, 0:S - 1],
                                                  W[g * DH:(g + 1) * DH, 20 + kv, par:par + S - 1]
                                                  ).then_inc(stacked, 16)
                    if x["kind"] == "vs":
                        round_b(0)
                    if x["kind"] == "ks" or (x["kind"], x["j"]) == ("nq", 1):
                        raw_hidden()
                    if x["kind"] == "kw":
                        round_b(1)
                    if (x["kind"], x["j"]) in HID_TURN:
                        gelu(HID_TURN.index((x["kind"], x["j"])))
                for x in jobs[-2:]:
                    if x["kind"] in TURNED:
                        turn(x)

            act.wait_ge(eps_set, 1)
            tables()

            def mem(k):
                return W[:, k // 2, (k % 2) * M:(k % 2 + 1) * M]

            round_unit(0)
            act.wait_ge(small_in, 16)
            act.wait_ge(mem_in, 16)
            round_x(mem, "mem", lambda k: None)
            for v in range(1, RING):
                round_unit(v)
            squares("mem", mem, KC, cols=M)
            rstd("mem", KC, 7, M)
            act.wait_ge(lam_sum, 1)
            act.activation(LAM[:, 2:4], PS[:, 6, 0:2], ACT.Exp).then_inc(lam_exp, 1)
            project("mem")
            act.wait_ge(consts_in, 32)
            act.activation(SUMS[:, :, :].rearrange("p a b -> p (a b)"), CST[:, K_NEG:K_NEG + 2 * P],
                           ACT.Copy).then_inc(sums_ready, 1)
            pre_norm("ff1_pre", lambda k: None, chunks=range(4, KC))
            gate_up(0)
            down(0)
            tables()
            post_norm("ff1_post", "down0")
            pre_norm("mix_pre", x_updated("ff1"))
            project("proj1")
            tables()
            act.wait_ge(cmp_done, 1)
            act.activation(KCT[:, 0:NCMP], PS[:, 6, 0:NCMP], ACT.Copy).then_inc(cmp_taken, 1)
            act.activation(VC[0:NCMP, :], PS[0:NCMP, 7, 0:P], ACT.Copy).then_inc(cmp_taken, 1)
            attention("mix1")
            split_tile(NT - 1)
            post_norm("mix_post", "out1")
            pre_norm("ff2_pre", x_updated("mix1"))
            gate_up(1)
            down(1)
            tables()
            post_norm("ff2_post", "down1")
            pre_norm("mixA", x_updated("ff2"))
            project("projA")
            round_o(range(6), lambda k: act.wait_ge(conv_done, k + 1))
            attention("mixA")
            round_o((6, 7), lambda k: act.wait_ge(o_taken, 8 + k - 5))
            refill("outA", KC - 1)
            pre_norm("ffnA", xh_left("outA", "mixA"))
            gate_up(2)
            down(2)
            tables()
            pre_norm("kv", x_updated("ffnA"), lambda: refill("down2", 2, FC - 2))
            project("kv")
            round_x(lambda k: X[:, k, :], "mixB", lambda k: None)
            project("projB")
            n = len(SBSTEPS)
            def sb_exp_ln(t):
                e = ESLOT[t % 4][:, 0:S - SBSTEPS[t][1] * P]
                act.wait_ge(sb_clip, t + 1)
                act.activation(e, e, ACT.Exp).then_inc(sb_exp, 1)
                act.wait_ge(sb_exp, t + 1)
                act.activation(e, e, ACT.Ln, bias=1.0).then_inc(sb_ln, 1)

            def sb_round(t):
                w = S - SBSTEPS[t][1] * P
                act.wait_ge(sb_l, t + 1)
                if t >= 8:
                    act.wait_ge(sb_tri, t - 4)
                act.activation(XH[:, t % 8, 0:w], PB[:, t % 2, 0:w], ACT.Copy).then_inc(sb_hi, 1)

            def sb_weights(t):
                w = S - SBSTEPS[t][1] * P
                act.wait_ge(sb_tri, t + 1)
                if t >= 4:
                    act.wait_ge(sb_pv, t - 3)
                act.activation(ASLOT[t % 4][:, 0:w], PS[:, t % SBANKS, 0:w], ACT.Exp).then_inc(sb_a, 1)

            for t in range(n + LAG_T):
                if t >= LAG_T:
                    sb_weights(t - LAG_T)
                if t < n:
                    sb_exp_ln(t)
                if 1 <= t <= n:
                    sb_round(t - 1)
            round_o(range(5), lambda k: act.wait_ge(sb_o, k + 1))
            attention("mixB")
            round_o((5, 6, 7), lambda k: act.wait_ge(sb_o, k + 1) if k < 6 else
                    act.wait_ge(o_taken, 10 + k - 5))
            refill("outB", KC - 1)
            pre_norm("ffnB", xh_left("outB", "mixB"))
            gate_up(3)
            down(3)
            tables()
            squares("final", lambda k: X[:, k, :], KC, x_updated("ffnB"))
            refill("down3", 2, FC - 2)
            rstd("final", KC, 0)

        @block.tensor
        def _(pe):
            def three(o, wh, wl, xh, xl, start, stop):
                pe.matmul(o, wh, xh, start=start, stop=False)
                pe.matmul(o, wh, xl, start=False, stop=False)
                return pe.matmul(o, wl, xh, start=False, stop=stop)

            def have(u, i=None):
                pe.wait_ge(split_ready, u + 1 if i is None else i * RING + (u + 1))

            def features(u, bank, stage, cols=S, first=False, i=None):
                have(u, i)
                for k in range(KC):
                    if first:
                        pe.wait_ge(xn_ready, KC * XN[stage] + k + 1)
                    mm = three(PS[:, bank, 0:cols], WH[:, u % RING, k, :], WL[:, u % RING, k, :],
                               *split_x(stage, k, cols), k == 0, k == KC - 1)
                mm.then_inc(unit_done, 1)

            def side_by_side(units, stage, cols=S):
                for u, bank in units:
                    have(u)
                for k in range(KC):
                    pe.wait_ge(xn_ready, KC * XN[stage] + k + 1)
                    for u, bank in units:
                        mm = three(PS[:, bank, 0:cols], WH[:, u % RING, k, :], WL[:, u % RING, k, :],
                                   *split_x(stage, k, cols), k == 0, k == KC - 1)
                        if k == KC - 1:
                            mm.then_inc(unit_done, 1)

            def ssq(name, bank, cols=S):
                if name.startswith("sub"):
                    pe.wait_ge(sq_ready, SQ0[name] + 1)
                    src = SQ[:, 0, 0:cols]
                else:
                    pe.wait_ge(sq_added, ADD0[name] + KC - 1)
                    src = ACC[:, 0:cols]
                pe.matmul(PS[:, bank, 0:cols], ONES, src, start=True, stop=True).then_inc(ssq_done, 1)

            def gate_up(l, stage):
                u0 = U0[f"gu{l}"]
                n = SIDE[stage]
                side_by_side([(u0 + j, j) for j in range(n)], stage)
                for j in range(n, 4):
                    if j == SSQ_AT[stage]:
                        ssq(PRE[l], 7)
                    features(u0 + j, j, stage)
                if SSQ_AT[stage] == 4:
                    ssq(PRE[l], 7)
                with pe.Fori(0, FC // 2 - 1) as i:
                    for f in range(2):
                        pe.wait_ge(gu_free, i * 2 + (FC * l + f + 1))
                        for j in range(2):
                            features(u0 + 4 + 2 * f + j, 2 * f + j, stage, i=i)

            def down(l):
                u0 = U0[f"down{l}"]

                def step(k, order=range(KC), i=None):
                    u = u0 + k
                    have(u, i)
                    n = FC * l + k + 1
                    pe.wait_ge(hk_ready, n if i is None else i * RING + n)
                    for c in order:
                        if k == 0 and c == 0:
                            pe.wait_ge(gu_free, FC * (l + 1))
                        mm = three(PS[:, c, :], WH[:, u % RING, c, :], WL[:, u % RING, c, :],
                                   HH[:, k % 2, :], HL[:, k % 2, :], k == 0, False)
                    mm.then_inc(unit_done, 1)

                step(0, (4, 5, 6, 7, 0, 1, 2, 3))
                step(1)
                with pe.Fori(0, (FC - 2) // RING - 1) as i:
                    for s in range(RING):
                        step(2 + s, i=i)
                for k in range(FC - RING, FC - 2):
                    step(k)
                for k in (FC - 2, FC - 1):
                    have(u0 + k)
                for c in range(KC + LAG_C):
                    for k, bank in ((FC - 2, c), (FC - 1, c - LAG_C)):
                        if not 0 <= bank < KC:
                            continue
                        if bank == 0:
                            pe.wait_ge(hk_ready, FC * l + k + 1)
                        mm = three(PS[:, bank, :], WH[:, (u0 + k) % RING, bank, :],
                                   WL[:, (u0 + k) % RING, bank, :], HH[:, k % 2, :], HL[:, k % 2, :],
                                   False, k == FC - 1)
                        if bank == KC - 1:
                            mm.then_inc(unit_done, 1)
                        elif k == FC - 1:
                            mm.then_inc(y_done, 1)

            def flip(x):
                f = x["f"]
                pe.wait_ge(taken, x["t"] + 1)
                if f >= 2:
                    flip_wait(pe, f - 2)
                if x["kind"] in ROTARY:
                    mm = pe.matmul(PS[:, 4 + f % 2, :], PERM, SQ[:, f % 2, :], start=True, stop=True)
                else:
                    for t in range(2 if x["kind"] == "mv" else NT):
                        mm = pe.transpose(PS[:, 4 + f % 2, t * P:(t + 1) * P], SQ[:, f % 2, t * P:(t + 1) * P], IDF)
                mm.then_inc(flipped, 1)

            def compress(x):
                kv, t, u = int(x["kind"] == "w1v"), x["j"], x["u"]
                have(u)
                if t == 0:
                    pe.wait_ge(b_ready, kv + 1)
                    if kv:
                        pe.wait_ge(hid_raw, 1)
                    else:
                        pe.wait_ge(rstd_ready, NIDX["mix_pre"] + 1)
                for n in range(4):
                    l = 4 * t + n
                    o = PS[0:2 * NCMP, 6, 0:256]
                    wh, wl = (w[:, u % RING, 2 * n:2 * n + 2, :].rearrange("p a b -> p (a b)")
                              for w in (WH, WL))
                    pe.matmul(o, BH[:, l, :], wh, start=l == 0, stop=False)
                    pe.matmul(o, BL[:, l, :], wh, start=False, stop=False)
                    mm = pe.matmul(o, BH[:, l, :], wl, start=False, stop=l == 15)
                mm.then_inc(unit_done, 1)

            def hidden_turned(kv):
                pe.wait_ge(hid_raw, kv + 1)
                for hc in range(2):
                    mm = pe.transpose(PS[:, 7, hc * DH:hc * DH + 2 * NCMP],
                                      Y0[0:2 * NCMP, hc * P:(hc + 1) * P], IDF[0:2 * NCMP, 0:2 * NCMP])
                mm.then_inc(hid_turned, 1)

            def project(part, stage, norm=None, cols=S):
                jobs = JOBS[part]
                side = SIDE.get(stage, 1) if norm else 1
                if side > 1:
                    side_by_side([(x["u"], x["n"]) for x in jobs[:side]], stage, cols)
                for i, x in enumerate(jobs):
                    if side > 1 and i < side:
                        pass
                    elif "n" not in x:
                        compress(x)
                    else:
                        if x["n"] >= 4 or part == "projB":
                            pe.wait_ge(taken, x["t"] - 3)
                        features(x["u"], x["t"] % 4 if part == "projB" else x["n"] % 4, stage, cols=cols,
                                 first=x["n"] == 0)
                    if i == SSQ_AT.get(stage, 1) - 1 and norm:
                        if part == "mem":
                            pe.wait_ge(consts_in, 32)
                        ssq(norm, 7, cols)
                        if part == "mem":
                            pe.wait_ge(lam_prod, 1)
                            pe.matmul(PS[:, 6, 0:2], ONES, LAM[:, 0:2], start=True, stop=True).then_inc(lam_sum, 1)
                    if i >= 1 and "f" in jobs[i - 1]:
                        flip(jobs[i - 1])
                    if (x["kind"], x["j"]) in HID_TURN:
                        hidden_turned(HID_TURN.index((x["kind"], x["j"])))
                if "f" in jobs[-1]:
                    flip(jobs[-1])

            def scores(part, y):
                c, h, i = y["chunk"], y["half"], y["tile"]
                if part == "mix1" and y["s"] == 0:
                    pe.wait_ge(roped, 10)
                if y["p"] == 4 * 4:
                    pe.wait_ge(roped, 14)
                    pe.wait_ge(cmp_taken, 2)
                for m in range(2 if y["kind"] == "diff" else 1):
                    s, n = y["s"] + m, y["n"]
                    if s >= 4:
                        pe.wait_ge(exp_done, s - 3)
                    half = m if y["kind"] == "diff" else h
                    r = slice(DH * half, DH * half + DH)
                    q = Q[r, c, i * P:(i + 1) * P]
                    if y["kind"] == "diff":
                        k = W[r, 8 + c, 0:n]
                    elif y["kind"] == "sel":
                        k = W[r, 12, 0:n]
                    elif y["kind"] == "win":
                        k = W[r, 13, 0:n]
                    elif y["kind"] == "cmp":
                        k = KCT[r, 0:n]
                    else:
                        k = MK[r, 0 if part == "mixA" else 1, c - 6, :]
                    masked = y["kind"] != "mem"
                    mm = pe.matmul(PS[:, s % 4, 0:n], q, k, start=True, stop=not masked)
                    if y["kind"] == "cmp":
                        mm = pe.matmul(PS[:, s % 4, 0:n], IDB, CSB[:, B_CMP + 32 * i:B_CMP + 32 * i + n],
                                       start=False, stop=True)
                    elif masked:
                        mm = pe.matmul(PS[:, s % 4, n - P:n], IDB, CSB[:, B_CAUSAL:B_CAUSAL + P],
                                       start=False, stop=True)
                    mm.then_inc(qk_done, 1)

            def transposes(x, b):
                e = x["e"] + b
                if e >= 2:
                    pe.wait_ge(pt_ready, e - 1)
                for y in x["members"]:
                    if b >= y["blocks"]:
                        continue
                    n = y["tile"] if x["kind"] == "diff" else y["m"]
                    if b == 0:
                        pe.wait_ge(p_ready, y["p"] + 1)
                    kp = NCMP if x["kind"] == "cmp" else P
                    src = PSLOT[4 * (x["q"] % 2) + y["m"]]
                    mm = pe.transpose(PS[0:kp, 4 + e % 2, n * P:(n + 1) * P], src[:, b * P:b * P + kp], IDF)
                mm.then_inc(tr_done, 1)

            def values(part, x, b):
                e, h = x["e"] + b, x["half"]
                c = x["members"][0]["chunk"]
                pe.wait_ge(pt_ready, e + 1)
                if x["first"] and h == 0 and b == 0 and x["o"] >= 2:
                    pe.wait_ge(o_taken, x["o"] - 1)
                if x["o"] == 5:
                    pe.wait_ge(ln_done, NIDX["sub3"] + 1)
                if x["o"] == 0:
                    pe.wait_ge(cmp_taken, 2)
                bank = 6 + x["o"] % 2
                kp = NCMP if x["kind"] == "cmp" else P
                f = slice(h * DH, (h + 1) * DH)
                o, n = PS[f, bank, :], 0
                if x["kind"] == "diff":
                    v, o, n = V_DIFF[:, b, c * P:(c + 1) * P], PS[:, bank, b * P:S], b * P
                elif x["kind"] == "cmp":
                    v = VC[0:NCMP, f]
                elif x["kind"] == "sel":
                    v = V_SEL[:, b, f]
                elif x["kind"] == "win":
                    v = V_WIN[:, b, f]
                else:
                    f = slice((c - 6) * P + h * DH, (c - 6) * P + (h + 1) * DH)
                    v = MV[:, 0 if part == "mixA" else 1, b, f]
                pe.matmul(o, v, PT[0:kp, e % 2, n:S], start=x["first"] and b == 0,
                          stop=x["last"] and b == x["blocks"] - 1, skip_group_check=True).then_inc(pv_done, 1)

            def attention(part):
                qs = ATT[part]
                late = []
                for t in range(len(qs) + 2):
                    for m in range(4):
                        if t < len(qs):
                            scores(part, qs[t]["members"][m])
                        items = items_after(qs, t, m)
                        if late and (len(late) == 2 or not items):
                            values(part, *late.pop(0))
                        for item in items:
                            if len(late) == 2:
                                values(part, *late.pop(0))
                            transposes(*item)
                            late.append(item)
                        if part == "mix1" and m == 2 and 1 <= t - SUB_AT <= 4:
                            h = t - SUB_AT - 1
                            pe.wait_ge(o_taken, 4)
                            if h:
                                pe.wait_ge(ln_done, NIDX["sub0"] + h)
                            ssq(f"sub{h}", 7)

            def output(part, stage, order=range(KC)):
                for j in range(KC):
                    u = U0[part] + j
                    have(u)
                    for n, k in enumerate(order):
                        if j == 0:
                            all8 = part == "out1" and k >= 4
                            pe.wait_ge(xn_ready, KC * XN[stage] + (KC if all8 else n + 1))
                        mm = three(PS[:, j, :], WH[:, u % RING, k, :], WL[:, u % RING, k, :],
                                   XH[:, k, :], XL[:, k, :], n == 0, n == KC - 1)
                        if part != "out1" and j == KC - 1 and k < KC - 1:
                            mm.then_inc(xh_used, 1)
                    mm.then_inc(unit_done, 1)

            project("mem", "mem", "mem", M)
            pe.wait_ge(taken, TAKEN["mem"])
            gate_up(0, "ff1")
            down(0)
            ssq("ff1_post", 0)
            project("proj1", "proj1", "mix_pre")
            w2 = SM[:, C_W2:C_W2 + 256].rearrange("p (v h d) -> p v h d", v=2, h=2)
            pe.wait_ge(hid_ready, 2)
            for g in range(NG):
                n = slice(g * NCMP, (g + 1) * NCMP)
                for hc in range(2):
                    pe.matmul(PS[g * DH:(g + 1) * DH, 6, 0:NCMP], w2[:, 0, hc, :], HID[:, 0, hc, n],
                              start=hc == 0, stop=hc == 1)
            for g in range(NG):
                n = slice(g * NCMP, (g + 1) * NCMP)
                for hc in range(2):
                    mm = pe.matmul(PS[0:NCMP, 7, g * DH:(g + 1) * DH], HID[:, 1, hc, n], w2[:, 1, hc, :],
                                   start=hc == 0, stop=hc == 1)
            mm.then_inc(cmp_done, 1)
            pe.wait_ge(turned, FLIPS[JOBS["proj1"][8]["f"]]["c"])
            pe.wait_ge(masks_ready, 1)
            attention("mix1")
            output("out1", "out1")
            ssq("mix_post", 0)
            gate_up(1, "ff2")
            down(1)
            ssq("ff2_post", 0)
            project("projA", "projA", "mixA")
            pe.wait_ge(taken, TAKEN["projA"])
            attention("mixA")
            output("outA", "outA")
            gate_up(2, "ffnA")
            down(2)
            project("kv", "kv", "kv")
            project("projB", "projB")
            pe.wait_ge(taken, TAKEN["projB"])
            pe.wait_ge(turned, FLIPS[max(FLIPS)]["c"])
            n = len(SBSTEPS)

            def sb_scores(t):
                h, j = SBSTEPS[t]
                if t >= SBANKS:
                    pe.wait_ge(sb_a, t - SBANKS + 1)
                r = slice(DH * (h % 2), DH * (h % 2) + DH)
                pe.matmul(PS[:, t % SBANKS, 0:S - j * P], W[r, 8 + h // 2, j * P:(j + 1) * P],
                          Q[r, h // 2, j * P:S], start=True, stop=True).then_inc(sb_qk, 1)

            def sb_tail(t):
                h, j = SBSTEPS[t]
                w = S - j * P
                pe.wait_ge(sb_lo, t + 1)
                bank = PS[:, t % SBANKS, :]
                for n in range(NT - j):
                    col, width, m = n * P, w - n * P, SUMS[:, 1 if n == 0 else 0, :]
                    for part in (XH, XL):
                        pe.matmul(bank[:, col:w], m, part[:, (t - n) % 8, 0:width], start=False,
                                  stop=False, skip_group_check=True)
                pe.matmul(bank[:, 0:P], IDB, CSB[:, B_STRICT:B_STRICT + P], start=False, stop=True,
                          skip_group_check=True).then_inc(sb_tri, 1)

            def sb_values(t):
                h, j = SBSTEPS[t]
                c = h // 2
                w = S - j * P
                pe.wait_ge(sb_a, t + 1)
                if h % 2 == 0 and j == NT - 1 and c >= 2:
                    pe.wait_ge(sb_o, c - 1)
                r = slice(DH * (h % 2), DH * (h % 2) + DH)
                pe.matmul(PS[r, 6 + c % 2, j * P:S], V_SB[:, j, h * DH:(h + 1) * DH], ASLOT[t % 4][:, 0:w],
                          start=j == NT - 1, stop=j == 0, skip_group_check=True).then_inc(sb_pv, 1)

            pe.wait_ge(sums_ready, 1)
            for t in range(n + LAG_V):
                if t < n:
                    sb_scores(t)
                if 0 <= t - LAG_T < n:
                    sb_tail(t - LAG_T)
                if t >= LAG_V:
                    sb_values(t - LAG_V)
            pe.wait_ge(sb_o, 6)
            attention("mixB")
            output("outB", "outB")
            gate_up(3, "ffnB")
            down(3)
            ssq("final", 0)

        @block.vector
        def _(dve):
            chained = [0]

            def chain(ins):
                chained[0] += 1
                ins.then_inc(dve_chain, 1)
                dve.wait_ge(dve_chain, chained[0])

            def low(stage, name, k, src):
                dve.wait_ge(xh_ready, KC * XN[stage] + k + 1)
                hi, lo = split_x(stage, k)
                dve.scalar_tensor_tensor(lo, src, gain(name, k), hi.bitcast(F),
                                         ALU.mult, ALU.subtract).then_inc(xn_ready, 1)

            def add_squares(name, cols=S, chunks=range(1, KC)):
                for k in chunks:
                    dve.wait_ge(sq_ready, SQ0[name] + k + 1)
                    if k >= 2:
                        dve.wait_ge(sq_added, ADD0[name] + k - 1)
                    dve.tensor_tensor(ACC[:, 0:cols], SQ[:, 0, 0:cols] if k == 1 else ACC[:, 0:cols],
                                      SQ[:, k % 2, 0:cols], ALU.add).then_inc(sq_added, 1)

            def low_o(stage, chunks):
                for k in chunks:
                    dve.wait_ge(xh_ready, KC * XN[stage] + k + 1)
                    dve.tensor_tensor(XL[:, k, :], W[:, k, :], XH[:, k, :].bitcast(F),
                                      ALU.subtract).then_inc(xn_ready, 1)

            def gate_up(l):
                u0 = U0[f"gu{l}"]
                dve.wait_ge(rstd_ready, NIDX[PRE[l]] + 1)

                def step(f, i=None):
                    n, u = FC * l + f + 1, u0 + 2 * f + 1
                    n, u = (n, u) if i is None else (i * 2 + n, i * RING + u)
                    s = f % 2
                    h = W[:, f, :] if i is None else W[:, bass.ds(i * 2 + f, 1), :].rearrange("p a b -> p (a b)")
                    dve.wait_ge(unit_done, u)
                    dve.tensor_tensor(TMP[:, s, :], RSTD[:, :], PS[:, 2 * s, :], ALU.mult).then_inc(g_scaled, 1)
                    dve.wait_ge(unit_done, u + 1)
                    dve.tensor_tensor(Y0[:, :], RSTD[:, :], PS[:, 2 * s + 1, :], ALU.mult).then_inc(gu_free, 1)
                    dve.wait_ge(gu_free, n)
                    dve.wait_ge(silu_done, n)
                    dve.tensor_tensor(h, SQ[:, s, :], Y0[:, :], ALU.mult).then_inc(h_ready, 1)
                    dve.wait_ge(h_ready, n)

                with dve.Fori(0, FC // 2 - 1) as i:
                    step(0, i)
                    step(1, i)
                for k in range(2):
                    dve.wait_ge(hk_hi, FC * l + k + 1)
                    dve.tensor_tensor(HL[:, k, :], W[:, k, :], HH[:, k, :].bitcast(F),
                                      ALU.subtract).then_inc(hk_ready, 1)
                step(FC - 2)
                step(FC - 1)

            def down(l):
                with dve.Fori(0, FC // 2 - 1) as i:
                    for s in range(2):
                        dve.wait_ge(hk_hi, i * 2 + (FC * l + s + 3))
                        dve.tensor_tensor(HL[:, s, :],
                                          W[:, bass.ds(i * 2 + (s + 2), 1), :].rearrange("p a b -> p (a b)"),
                                          HH[:, s, :].bitcast(F), ALU.subtract).then_inc(hk_ready, 1)

            def post(name, part, update, stage, nxt):
                y_wait(dve, part, 0)
                dve.tensor_copy(Y0[:, :], PS[:, 0, :]).then_inc(y0_done, 1)
                add_squares(name)
                dve.wait_ge(rstd_ready, NIDX[name] + 1)
                x0 = KC * XU[update]
                for k in range(KC + 2):
                    if k < KC:
                        if k >= 2:
                            dve.wait_ge(x_ready, x0 + k - 1)
                        dve.scalar_tensor_tensor(TMP[:, k % 2, :], PS[:, k, :] if k else Y0[:, :], gain(name, k),
                                                 RSTD[:, :], ALU.mult, ALU.mult).then_inc(y_scaled, 1)
                    if k >= 2:
                        low(stage, nxt, k - 2, X[:, k - 2, :])
                add_squares(nxt)

            def add_y(part, stage, nxt):
                for k in range(KC + 1):
                    if k < KC:
                        y_wait(dve, part, k)
                        dve.tensor_tensor(X[:, k, :], X[:, k, :], PS[:, k, :], ALU.add).then_inc(x_ready, 1)
                    if k >= 1 and stage:
                        low(stage, nxt, k - 1, X[:, k - 1, :])
                    elif k >= 2:
                        add_squares(nxt, chunks=(k - 1,))
                if stage:
                    add_squares(nxt)

            def rope(x):
                f = x["f"]
                dst = W[:, {"dq": 0, "nq": 4, "dk": 8, "ks": 12, "kw": 13}[x["kind"]] + x["j"], :]
                if x["c"] >= 2:
                    dve.wait_ge(roped, x["c"] - 1)
                dve.tensor_tensor(TMP[:, 0, :], SQ[:, f % 2, :], COS, ALU.mult).then_inc(dve_chain, 1)
                chained[0] += 1
                dve.wait_ge(flipped, f + 1)
                chain(dve.tensor_tensor(TMP[:, 1, :], SIN, PS[:, 4 + f % 2, :], ALU.mult))
                dve.tensor_tensor(dst, TMP[:, 0, :], TMP[:, 1, :], ALU.add).then_inc(roped, 1)

            def build_b(kv):
                dve.wait_ge(stacked, 16 * 8)
                if kv:
                    dve.wait_ge(b_ready, 1)
                for l in range(16):
                    src = PB[:, 2 * kv:2 * kv + 2, 2 * l:2 * l + 16 * (NCMP - 1) + 1:16]
                    dve.tensor_scalar(BT[:, 2 * NCMP * l:2 * NCMP * (l + 1)].rearrange("p (g c) -> p g c", g=NG), src,
                                      SM[:, C_PE + 16 * kv + l:C_PE + 16 * kv + l + 1], None,
                                      ALU.add).then_inc(b_tmp, 1)

            def low_b(kv):
                dve.wait_ge(b_hi, kv + 1)
                dve.tensor_tensor(HL[:, :, :].rearrange("p a b -> p (a b)")[:, 0:32 * NCMP], BT,
                                  HH[:, :, :].rearrange("p a b -> p (a b)")[:, 0:32 * NCMP].bitcast(F),
                                  ALU.subtract).then_inc(b_ready, 1)

            def conv(x, bank):
                c, rs = x["j"], RSTD[:, :]
                z = Z[:, c % 2, :]
                w = [SM[:, C_CONV + 3 * c + n:C_CONV + 3 * c + n + 1] for n in range(3)]
                if x["kind"] == "cg":
                    dve.tensor_tensor(W[:, 12 + c % 2, :], rs, bank, ALU.mult).then_inc(taken, 1)
                elif x["kind"] == "cu":
                    dve.tensor_tensor(TMP[:, 0, :], rs, bank, ALU.mult).then_inc(taken, 1)
                    dve.wait_ge(taken, x["t"] + 1)
                    chain(dve.tensor_tensor(z[:, 2:S + 2], W[:, 12 + c % 2, :], TMP[:, 0, :], ALU.mult))
                    chain(dve.tensor_scalar(TMP[:, 0, :], z[:, 0:S], w[0], None, ALU.mult))
                    chain(dve.scalar_tensor_tensor(TMP[:, 1, :], z[:, 1:S + 1], w[1], TMP[:, 0, :],
                                                   ALU.mult, ALU.add))
                    chain(dve.scalar_tensor_tensor(TMP[:, 0, :], z[:, 2:S + 2], w[2], TMP[:, 1, :],
                                                   ALU.mult, ALU.add))
                else:
                    dve.tensor_tensor(TMP[:, 1, :], rs, bank, ALU.mult).then_inc(taken, 1)
                    dve.wait_ge(taken, x["t"] + 1)
                    dve.tensor_tensor(W[:, c, :], TMP[:, 0, :], TMP[:, 1, :], ALU.mult).then_inc(conv_done, 1)
                    dve.wait_ge(conv_done, c + 1)

            def project(part, norm, cols=S):
                dve.wait_ge(rstd_ready, NIDX[norm] + 1)
                jobs = JOBS[part]
                rs = RSTD[:, 0:cols]
                for i, x in enumerate(jobs + [dict(kind="end")]):
                    kind, j = x["kind"], x.get("j")
                    if part == "mem" and i == EARLY:
                        for k in range(4):
                            low("ff1", "ff1_pre", k, X[:, k, :])
                    if "t" in x:
                        dve.wait_ge(unit_done, x["u"] + 1)
                        bank = PS[:, x["t"] % 4 if part == "projB" else x["n"] % 4, 0:cols]
                        if "f" in x and x["f"] >= 2:
                            if FLIPS[x["f"] - 2]["kind"] in ROTARY:
                                dve.wait_ge(roped, FLIPS[x["f"] - 2]["c"])
                            dve.wait_ge(flipped, x["f"] - 1)
                        if kind in ("cg", "cu", "cb"):
                            conv(x, bank)
                        elif kind in ("dq", "nq"):
                            dve.scalar_tensor_tensor(SQ[:, x["f"] % 2, :], bank, QSCALE, rs,
                                                     ALU.mult, ALU.mult).then_inc(taken, 1)
                        elif "f" in x:
                            dve.tensor_tensor(SQ[:, x["f"] % 2, 0:cols], rs, bank, ALU.mult).then_inc(taken, 1)
                        elif kind in ("qa", "qb"):
                            dve.scalar_tensor_tensor(W[:, j + (6 if kind == "qa" else 0), :], bank, QSCALE, rs,
                                                     ALU.mult, ALU.mult).then_inc(taken, 1)
                        else:
                            dst = {"mk": lambda: MK[:, j // 2, j % 2, :], "kc": lambda: W[:, 20, :],
                                   "vc": lambda: W[:, 21, :], "sk": lambda: W[:, 8 + j, :]}[kind]()
                            dve.tensor_tensor(dst, rs, bank, ALU.mult).then_inc(taken, 1)
                    prev = jobs[i - 1] if i else x
                    if prev["kind"] in ROTARY:
                        dve.wait_ge(taken, prev["t"] + 1)
                        rope(prev)
                    if kind == "dv" and j == 3:
                        build_b(0)
                    if kind == "vw":
                        low_b(0)
                    if kind == "kw":
                        build_b(1)
                    if kind == "dq" and j == 0:
                        low_b(1)

            def attention(part):
                qs = ATT[part]
                members = [y for x in qs for y in x["members"]]

                def maximum(y):
                    for j in range(2 if y["kind"] == "diff" else 1):
                        s = y["s"] + j
                        dve.wait_ge(qk_done, s + 1)
                        dve.tensor_reduce(NMAX[:, s:s + 1], PS[:, s % 4, 0:y["n"]], AX.X, ALU.max,
                                          negate=True).then_inc(nmax_ready, 1)

                def scale(y):
                    s, n = y["s"], y["n"]
                    p = PSLOT[4 * (y["p"] // 4 % 2) + y["m"]][:, 0:n]
                    if y["kind"] == "diff":
                        dve.wait_ge(exp_done, s + 2)
                        chain(dve.reciprocal(REC[:, s:s + 2], RSUM[:, s:s + 2]))
                        p1 = TMP[:, y["m"] % 2, 0:n]
                        chain(dve.tensor_scalar(p1, p1, REC[:, s + 1:s + 2], LAM[:, 6:7], ALU.mult, ALU.mult))
                        dve.scalar_tensor_tensor(p, p, REC[:, s:s + 1], p1, ALU.mult,
                                                 ALU.add).then_inc(p_ready, 1)
                        return
                    dve.wait_ge(exp_done, s + 1)
                    chain(dve.reciprocal(REC[:, s:s + 1], RSUM[:, s:s + 1]))
                    if y["kind"] == "mem":
                        dve.tensor_scalar(p, p, REC[:, s:s + 1], None, ALU.mult).then_inc(p_ready, 1)
                    else:
                        dve.tensor_scalar(p, p, REC[:, s:s + 1], GATE[:, y["tile"], y["gate"]:y["gate"] + 1],
                                          ALU.mult, ALU.mult).then_inc(p_ready, 1)

                def take(x):
                    dve.wait_ge(pv_done, x["e"] + x["blocks"])
                    bank = PS[:, 6 + x["o"] % 2, :]
                    y = x["members"][0]
                    if x["kind"] in ("diff", "mem"):
                        dst = W[:, y["chunk"], :]
                    else:
                        dst = W[:, 4:8, y["tile"] * P:(y["tile"] + 1) * P]
                        bank = bank.rearrange("p (c s) -> p c s", c=4)
                    dve.tensor_copy(dst, bank).then_inc(o_taken, 1)

                for i in range(len(members) + 8):
                    if i < len(members):
                        maximum(members[i])
                    if 0 <= i - LAG_P < len(members):
                        scale(members[i - LAG_P])
                    t = i // 4
                    if i % 4 == 1 and part == "mix1":
                        finish_heads(t)
                    if i % 4 == 3 and t >= 2 and qs[t - 2]["end"]:
                        take(qs[t - 2])

            def low_tile(n):
                i = TILE_ORDER[n]
                dve.wait_ge(xh_ready, KC * XN["out1"] + 4 + n + 1)
                dve.tensor_tensor(XL[:, 4:8, i * P:(i + 1) * P], W[:, 4:8, i * P:(i + 1) * P],
                                  XH[:, 4:8, i * P:(i + 1) * P].bitcast(F), ALU.subtract).then_inc(xn_ready, 1)

            def finish_heads(t):
                h = t - SUB_AT - 3
                if 0 <= h < 4:
                    low_o("out1", (h,))
                h = t - SUB_AT - 2
                if 0 <= h < 4:
                    dve.wait_ge(rstd_ready, NIDX[f"sub{h}"] + 1)
                    chain(dve.scalar_tensor_tensor(W[:, h, :], W[:, h, :], SM[:, C_SUB:C_SUB + 1], RSTD[:, :],
                                                   ALU.mult, ALU.mult))
                    dve.tensor_scalar(W[:, h, :], W[:, h, :], 1.0 - LAMBDA_INIT, None,
                                      ALU.mult).then_inc(sub_ready, 1)
                if t - 4 in TILE_END:
                    low_tile(TILE_END[t - 4])

            dve.memset(EPSB[:, :], EPS).then_inc(eps_set, 1)
            dve.wait_ge(small_in, 16)
            dve.tensor_tensor(LAM[:, 0:2], SM[:, C_LAM:C_LAM + 2], SM[:, C_LAM + 2:C_LAM + 4],
                              ALU.mult).then_inc(lam_prod, 1)
            for name in ("ff1_post", "ff2_post"):
                g = SM[:, GCOL[name]:GCOL[name] + KC]
                chain(dve.tensor_scalar(g, g, 0.5, None, ALU.mult))
            def mem(k):
                return W[:, k // 2, (k % 2) * M:(k % 2 + 1) * M]

            for k in range(KC):
                low("mem", "mem", k, mem(k))
            add_squares("mem", M)
            dve.wait_ge(consts_in, 32)
            dve.tensor_copy(CSB[:, :], CSB_IN).then_inc(masks_ready, 1)
            dve.wait_ge(masks_ready, 1)
            dve.wait_ge(lam_exp, 1)
            chain(dve.tensor_tensor(LAM[:, 4:5], LAM[:, 3:4], LAM[:, 2:3], ALU.subtract))
            chain(dve.tensor_scalar(LAM[:, 6:7], LAM[:, 4:5], LAMBDA_INIT, None, ALU.subtract))
            project("mem", "mem", M)
            for k in range(4, KC):
                low("ff1", "ff1_pre", k, X[:, k, :])
            add_squares("ff1_pre")
            gate_up(0)
            down(0)
            post("ff1_post", "down0", "ff1", "proj1", "mix_pre")
            project("proj1", "mix_pre")
            dve.wait_ge(turned, FLIPS[JOBS["proj1"][8]["f"]]["c"])
            g0 = GATE[:, :, :].rearrange("p t (h b) -> p t h b", b=3)[:, :, :, 0]
            chain(dve.tensor_tensor(g0, g0, CST[:, K_ROW:K_ROW + 32].rearrange("p (t h) -> p t h", t=NT),
                                    ALU.mult))
            attention("mix1")
            low_tile(NT - 1)
            post("mix_post", "out1", "mix1", "ff2", "ff2_pre")
            gate_up(1)
            down(1)
            post("ff2_post", "down1", "ff2", "projA", "mixA")
            for s in range(2):
                chain(dve.memset(Z[:, s, 0:2], 0.0))
            project("projA", "mixA")
            low_o("outA", range(6))
            attention("mixA")
            low_o("outA", (6, 7))
            add_y("outA", "ffnA", "ffnA")
            gate_up(2)
            down(2)
            add_y("down2", "kv", "kv")
            project("kv", "kv")
            for k in range(KC):
                low("projB", "mixB", k, X[:, k, :])
            project("projB", "kv")
            n = len(SBSTEPS)

            def sb_take(c):
                dve.wait_ge(sb_pv, 8 * (c + 1))
                dve.tensor_copy(W[:, c, :], PS[:, 6 + c % 2, :]).then_inc(sb_o, 1)

            def sb_clip_(t):
                w = S - SBSTEPS[t][1] * P
                dve.wait_ge(sb_qk, t + 1)
                if t >= 4:
                    dve.wait_ge(sb_l, t - 3)
                dve.tensor_scalar(ESLOT[t % 4][:, 0:w], PS[:, t % SBANKS, 0:w], SPW, None,
                                  ALU.min).then_inc(sb_clip, 1)

            def sb_soft(t):
                w = S - SBSTEPS[t][1] * P
                dve.wait_ge(sb_ln, t + 1)
                if t >= 2:
                    dve.wait_ge(sb_lo, t - 1)
                lt = PB[:, t % 2, :]
                chain(dve.tensor_tensor(lt[:, 0:w], ESLOT[t % 4][:, 0:w], PS[:, t % SBANKS, 0:w], ALU.max))
                dve.tensor_tensor(lt[:, 0:P], lt[:, 0:P], CST[:, K_MASK:K_MASK + P], ALU.mult).then_inc(sb_l, 1)

            for t in range(n + LAG_V + 3):
                if t < n:
                    sb_clip_(t)
                if 1 <= t <= n:
                    sb_soft(t - 1)
                d = t - LAG_V - 1
                if 0 <= d < n and d % 8 == 7:
                    sb_take(d // 8)
            low_o("outB", range(5))
            attention("mixB")
            low_o("outB", (5, 6, 7))
            add_y("outB", "ffnB", "ffnB")
            gate_up(3)
            down(3)
            add_y("down3", None, "final")
            dve.wait_ge(rstd_ready, NIDX["final"] + 1)
            for k in range(KC):
                dve.scalar_tensor_tensor(W[:, k, :], X[:, k, :], gain("final", k), RSTD[:, :],
                                         ALU.mult, ALU.mult).then_inc(out_ready, 1)


PRE = ["ff1_pre", "ff2_pre", "ffnA", "ffnB"]
POSTS = ["down0", "out1", "down1"]

def column_units(w):
    n = w.shape[1] // P
    return w.reshape(KC, P, n, P).transpose(2, 1, 0, 3)


def row_units(w):
    return w.reshape(w.shape[0] // P, P, KC, P)


def gate_up_units(g, u):
    return np.stack([column_units(g), column_units(u)], axis=1).reshape(2 * FC, P, KC, P)


def compress_units(w):
    return w.reshape(4, 4, P, 2, P).transpose(0, 2, 1, 3, 4).reshape(4, P, 8, P)


def per_feature(g):
    return g.reshape(-1, P).T


def make_constants():
    c = np.zeros((P, NCONST), np.float32)
    r = np.arange(P)
    c[:, K_ONE:K_ONE + P] = 1.0
    c[:, K_NEG:K_NEG + P] = -1.0
    c[:, K_TRI:K_TRI + P] = -(r[:, None] >= r[None, :]).astype(np.float32)
    c[:, K_ID:K_ID + P] = np.eye(P, dtype=np.float32)
    for b in (0, DH):
        for n in range(8):
            c[b + n + 8, K_PERM + b + n] = -1.0
            c[b + n, K_PERM + b + n + 8] = 1.0
    c[:, K_MASK:K_MASK + P] = (r[:, None] < r[None, :])
    pos = np.arange(S, dtype=np.float32)
    inv = np.float32(500000.0) ** (-np.arange(0, 16, 2, dtype=np.float32) / np.float32(16))
    ang = (pos[None, :] * inv[:, None]).astype(np.float32)
    c[:, K_COS:K_COS + S] = 1.0
    for b in (0, 8, DH, DH + 8):
        c[b:b + 8, K_COS:K_COS + S] = np.cos(ang)
        c[b:b + 8, K_SIN:K_SIN + S] = np.sin(ang)
    tok = r[:, None] + P * np.arange(NT)[None, :]
    c[:, K_ROW:K_ROW + 32] = np.repeat((tok >= 31), 8, axis=1)
    b = np.zeros((P, NCONSTB), np.float32)
    b[:, B_ID:B_ID + P] = np.eye(P)
    b[:, B_CAUSAL:B_CAUSAL + P] = np.where(r[None, :] <= r[:, None], 0.0, NEG)
    b[:, B_STRICT:B_STRICT + P] = np.where(r[:, None] < r[None, :], 0.0, NEG)
    end = 16 * np.arange(32) + 31
    for t in range(NT):
        b[:, B_CMP + 32 * t:B_CMP + 32 * t + 32] = np.where(end[None, :] <= (P * t + r)[:, None], 0.0, NEG)
    return c, b


def kernel(**inputs):
    import concourse.bacc as bacc
    from concourse.bass_utils import run_bass_kernel_spmd

    a = {k: np.asarray(v) for k, v in inputs.items()}
    w_in = a["w_in"][0]
    pair = np.concatenate([np.r_[DH * c:DH * (c + 1), DH * (c + 4):DH * (c + 5)] for c in range(4)])
    dq, dk, dv, nq = w_in[:, 0:512], w_in[:, 512:1024], w_in[:, 1024:1536], w_in[:, 1536:2048][:, pair]
    kc, vc, ks, vs, kw, vw = (w_in[:, 2048 + P * i:2048 + P * (i + 1)] for i in range(6))
    gl = np.concatenate([w_in[:, 2816:2840], np.zeros((D, P - 24), np.float32)], axis=1)
    blocks = {"kc": kc, "vc": vc, "dv": dv, "vs": vs, "vw": vw, "gl": gl, "dk": dk, "ks": ks, "kw": kw,
              "dq": dq, "nq": nq}
    blocks = {k: column_units(v) for k, v in blocks.items()}
    blocks["w1k"], blocks["w1v"] = compress_units(a["cmp_k_w1"][0]), compress_units(a["cmp_v_w1"][0])
    proj1 = np.stack([blocks[k][j] for k, j in PROJ["proj1"]])
    w_out = a["w_out"][0]
    w_out = np.concatenate([w_out[0:512], w_out[512:1024][pair]], axis=0)
    ain = a["a_in_2"][0]
    gate_b, gate_c, conv_u, qm = (ain[:, 0:768], ain[:, 768:1536], ain[:, 1536:2304], ain[:, 2304:2560])
    proj_a = np.stack([gate_c.reshape(D, 6, P), conv_u.reshape(D, 6, P), gate_b.reshape(D, 6, P)],
                      axis=2).reshape(D, 18 * P)
    proj_a = np.concatenate([proj_a, qm], axis=1)
    parts = [column_units(a["w_mem_kv_2"][0]), column_units(a["w_mem_kv_2"][1]),
             gate_up_units(a["ff1_w_gate"][0], a["ff1_w_up"][0]), row_units(a["ff1_w_down"][0]),
             proj1, column_units(w_out),
             gate_up_units(a["ff2_w_gate"][0], a["ff2_w_up"][0]), row_units(a["ff2_w_down"][0]),
             column_units(proj_a), column_units(a["w_o_2"][0]),
             gate_up_units(a["w_gate_2"][0], a["w_up_2"][0]), row_units(a["w_down_2"][0]),
             column_units(a["w_kv_shared_2"]), column_units(a["b_in_2"][0]), column_units(a["w_o_2"][1]),
             gate_up_units(a["w_gate_2"][1], a["w_up_2"][1]), row_units(a["w_down_2"][1]),
             np.zeros((NLOAD - NUNITS, P, KC, P), np.float32)]
    stream = np.concatenate([p.reshape(-1, P, D) for p in parts], axis=0)
    stream = stream.reshape(NLOAD // 2, 2, P, D).transpose(0, 2, 1, 3).reshape(NLOAD // 2, P, 2 * D)

    def col(v):
        return np.concatenate([v, np.zeros(P - v.shape[0], np.float32)])[:, None]

    gains = {"mem": a["mem_norm_2"], "ff1_pre": a["ff1_norm_pre"][0], "ff1_post": a["ff1_norm_post"][0],
             "mix_pre": a["mix_norm_pre"][0], "mix_post": a["mix_norm_post"][0],
             "ff2_pre": a["ff2_norm_pre"][0], "ff2_post": a["ff2_norm_post"][0],
             "mixA": a["mix_norm_2"][0], "ffnA": a["ffn_norm_2"][0], "kv": a["kv_norm_2"],
             "mixB": a["mix_norm_2"][1], "ffnB": a["ffn_norm_2"][1], "final": a["final_norm_2"]}
    small = [per_feature(gains[g]) for g in GAINS] + [a["diff_subln"][0][:, None]]
    small += [col(a[n][0]) for n in ("lambda_q1", "lambda_q2", "lambda_k1", "lambda_k2")]
    small += [a[n][0].reshape(16, P).T for n in ("cmp_pe_k", "cmp_pe_v")]
    small += [a[n][0].reshape(2, P, DH).transpose(1, 0, 2).reshape(P, P) for n in ("cmp_k_w2", "cmp_v_w2")]
    small += [a["conv_w_2"][0].reshape(3, 6, P).transpose(2, 1, 0).reshape(P, 18)]
    small = np.concatenate(small, axis=1)
    consts, constsb = make_constants()
    arrays = {
        "xT": a["x"][0].T.reshape(KC, P, S).transpose(1, 0, 2).reshape(P, KC * S),
        "memT": a["mem_2"][0].T.reshape(KC, P, M).transpose(1, 0, 2).reshape(P, KC * M),
        "wstream": stream, "small": small, "consts": consts, "constsb": constsb,
    }
    arrays = {k: np.ascontiguousarray(v) for k, v in arrays.items()}
    nc = bacc.Bacc("TRN2", target_bir_lowering=False, num_devices=1)
    args = [nc.dram_tensor(k, v.shape, mybir.dt.from_np(v.dtype), kind="ExternalInput").ap()
            for k, v in arrays.items()]
    args.append(nc.dram_tensor("outT", (P, KC, S), mybir.dt.float32, kind="ExternalOutput").ap())
    program(nc, *args)
    r = run_bass_kernel_spmd(nc, [arrays], core_ids=[0])
    y = np.asarray(r.results[0]["outT"])
    return np.ascontiguousarray(y.transpose(2, 1, 0).reshape(1, S, D))
```
